# Optimizing a Trainium2 kernel written in Bass

```python
import math
import jax, jax.numpy as jnp
from jax import lax
import numpy as np

D_MODEL = 1024
BATCH = 1
SEQ = 512
DEPTH = 2
DEC_BATCH = 1
DEC_SEQ = 32
PAST_LEN = 256

CHUNK = 64
Q_BLOCK = 128
HEAD_DIM = 64
N_DIFF_HEADS = D_MODEL // 256
N_SB_HEADS = D_MODEL // 128
N_FOX_HEADS = D_MODEL // HEAD_DIM
DIFF_W = N_DIFF_HEADS * 2 * HEAD_DIM
SB_W = N_SB_HEADS * HEAD_DIM
FOX_W = N_FOX_HEADS * HEAD_DIM
ROPE_DIM = HEAD_DIM // 4
ROPE_THETA = 500000.0
N_EXPERTS = 16
N_GROUPS = 4
EXPERTS_PER_GROUP = N_EXPERTS // N_GROUPS
TOP_K = 2
D_EXPERT = D_MODEL // 2
N_EVEN = (DEPTH + 1) // 2
N_ODD = DEPTH // 2
FORGET_BIAS_INIT = 3.0
EPS = 1e-6

kernel_name = 'hybrid_stream_diff_sb_fox_moe_step'

def _rmsnorm(x, g):
    xf = x.astype(jnp.float32)
    y = xf * lax.rsqrt(jnp.mean(xf * xf, axis=-1, keepdims=True) + EPS)
    return y.astype(x.dtype) * g

def _rope(x, pos):
    half = ROPE_DIM // 2
    inv = ROPE_THETA ** (-jnp.arange(half, dtype=jnp.float32) / half)
    ang = pos.astype(jnp.float32)[:, None] * inv[None, :]
    cos = jnp.cos(ang)[:, None, None, :]
    sin = jnp.sin(ang)[:, None, None, :]
    xr = x[..., :ROPE_DIM].astype(jnp.float32)
    x1, x2 = xr[..., :half], xr[..., half:]
    rot = jnp.concatenate([x1 * cos - x2 * sin, x2 * cos + x1 * sin], axis=-1)
    return jnp.concatenate([rot.astype(x.dtype), x[..., ROPE_DIM:]], axis=-1)

def _sweep(fn, q_arrays, q_pos):
    T = q_pos.shape[0]
    if T <= Q_BLOCK:
        return fn(*q_arrays, q_pos)
    nb = T // Q_BLOCK

    def split(a):
        return jnp.moveaxis(a.reshape(a.shape[0], nb, Q_BLOCK, *a.shape[2:]), 1, 0)

    xs = (*[split(a) for a in q_arrays], q_pos.reshape(nb, Q_BLOCK))
    out = lax.map(lambda args: fn(*args), xs)
    out = jnp.moveaxis(out, 0, 1)
    return out.reshape(out.shape[0], T, *out.shape[3:])

def _diff_block(q, qpos, k, v, kpos, lam):
    s = jnp.einsum('bqhcd,bkhcd->bchqk', q, k).astype(jnp.float32) * (HEAD_DIM ** -0.5)
    vis = (kpos[None, :] // CHUNK) <= (qpos[:, None] // CHUNK)
    p = jax.nn.softmax(jnp.where(vis, s, -jnp.inf), axis=-1)
    w = p[:, 0] - lam * p[:, 1]
    return jnp.einsum('bhqk,bkhe->bqhe', w.astype(v.dtype), v)

def _sb_block(q, qpos, k, v, kpos):
    z = jnp.einsum('bqhd,bkhd->bhqk', q, k).astype(jnp.float32) * (HEAD_DIM ** -0.5)
    vis = kpos[None, :] < qpos[:, None]
    log_keep = jnp.where(vis, jax.nn.log_sigmoid(-z), 0.0)
    later = lax.cumsum(log_keep, axis=3, reverse=True) - log_keep
    w = jnp.where(vis, jnp.exp(jax.nn.log_sigmoid(z) + later), 0.0)
    return jnp.einsum('bhqk,bkhd->bqhd', w.astype(v.dtype), v)

def _fox_block(q, dq, qpos, k, v, dk, kpos):
    s = jnp.einsum('bqhd,bkhd->bhqk', q, k).astype(jnp.float32) * (HEAD_DIM ** -0.5)
    bias = jnp.moveaxis(dq, 1, 2)[..., :, None] - jnp.moveaxis(dk, 1, 2)[..., None, :]
    vis = kpos[None, :] <= qpos[:, None]
    p = jax.nn.softmax(jnp.where(vis, s + bias, -jnp.inf), axis=-1)
    return jnp.einsum('bhqk,bkhd->bqhd', p.astype(v.dtype), v)

def _even_mixer(h, past, w_in, w_out, lq1, lk1, lq2, lk2, subln_g, layer):
    B, T, _ = h.shape
    P = 0 if past is None else past[0].shape[1]
    qpos = P + jnp.arange(T)
    kpos = jnp.arange(P + T)
    proj = h @ w_in
    aq, ak, av, bq, bk, bv = jnp.split(
        proj, [DIFF_W, 2 * DIFF_W, 3 * DIFF_W, 3 * DIFF_W + SB_W, 3 * DIFF_W + 2 * SB_W], axis=-1)
    aq = _rope(aq.reshape(B, T, N_DIFF_HEADS, 2, HEAD_DIM), qpos)
    ak = _rope(ak.reshape(B, T, N_DIFF_HEADS, 2, HEAD_DIM), qpos).reshape(B, T, N_DIFF_HEADS, 2 * HEAD_DIM)
    av = av.reshape(B, T, N_DIFF_HEADS, 2 * HEAD_DIM)
    bq = bq.reshape(B, T, N_SB_HEADS, HEAD_DIM)
    bk = bk.reshape(B, T, N_SB_HEADS, HEAD_DIM)
    bv = bv.reshape(B, T, N_SB_HEADS, HEAD_DIM)
    rows = (ak, av, bk, bv)
    if past is None:
        ak_all, av_all, bk_all, bv_all = ak, av, bk, bv
    else:
        ak_all = jnp.concatenate([past[0], ak], axis=1)
        av_all = jnp.concatenate([past[1], av], axis=1)
        bk_all = jnp.concatenate([past[2], bk], axis=1)
        bv_all = jnp.concatenate([past[3], bv], axis=1)
    lam_init = 0.8 - 0.6 * math.exp(-0.3 * layer)
    f32 = jnp.float32
    lam = (jnp.exp(jnp.sum(lq1.astype(f32) * lk1.astype(f32)))
           - jnp.exp(jnp.sum(lq2.astype(f32) * lk2.astype(f32))) + lam_init)
    kd = ak_all.reshape(B, P + T, N_DIFF_HEADS, 2, HEAD_DIM)
    a_out = _sweep(lambda qb, pb: _diff_block(qb, pb, kd, av_all, kpos, lam), (aq,), qpos)
    a_out = _rmsnorm(a_out, subln_g) * (1.0 - lam_init)
    b_out = _sweep(lambda qb, pb: _sb_block(qb, pb, bk_all, bv_all, kpos), (bq,), qpos)
    mixed = jnp.concatenate([a_out.reshape(B, T, DIFF_W), b_out.reshape(B, T, SB_W)], axis=-1)
    return mixed @ w_out, rows

def _odd_mixer(h, past, w_in, b_f, w_out):
    B, T, _ = h.shape
    P = 0 if past is None else past[0].shape[1]
    qpos = P + jnp.arange(T)
    kpos = jnp.arange(P + T)
    proj = h @ w_in
    q, k, v, fl = jnp.split(proj, [FOX_W, 2 * FOX_W, 3 * FOX_W], axis=-1)
    q = q.reshape(B, T, N_FOX_HEADS, HEAD_DIM)
    k = k.reshape(B, T, N_FOX_HEADS, HEAD_DIM)
    v = v.reshape(B, T, N_FOX_HEADS, HEAD_DIM)
    logf = jax.nn.log_sigmoid((fl + b_f).astype(jnp.float32))
    rows = (k, v, logf)
    if past is None:
        k_all, v_all, logf_all = k, v, logf
    else:
        k_all = jnp.concatenate([past[0], k], axis=1)
        v_all = jnp.concatenate([past[1], v], axis=1)
        logf_all = jnp.concatenate([past[2].astype(jnp.float32), logf], axis=1)
    dcum = jnp.cumsum(logf_all, axis=1)
    dq = dcum[:, P:]
    o = _sweep(lambda qb, db, pb: _fox_block(qb, db, pb, k_all, v_all, dcum, kpos), (q, dq), qpos)
    return o.reshape(B, T, FOX_W) @ w_out, rows

def _moe(h, w_router, b_router, w_gate, w_up, w_down):
    B, T, D = h.shape
    t = h.reshape(B * T, D)
    s = jax.nn.sigmoid((t @ w_router).astype(jnp.float32))
    sel = s + b_router.astype(jnp.float32)
    grp_score = lax.top_k(sel.reshape(-1, N_GROUPS, EXPERTS_PER_GROUP), TOP_K)[0].sum(-1)
    grp = jnp.argmax(grp_score, axis=-1)
    in_grp = (jnp.arange(N_EXPERTS) // EXPERTS_PER_GROUP)[None, :] == grp[:, None]
    _, idx = lax.top_k(jnp.where(in_grp, sel, -jnp.inf), TOP_K)
    w = jnp.take_along_axis(s, idx, axis=-1)
    w = w / jnp.sum(w, axis=-1, keepdims=True)
    gates = jnp.sum(jax.nn.one_hot(idx, N_EXPERTS, dtype=jnp.float32) * w[..., None], axis=1)
    a = jax.nn.silu(jnp.einsum('nd,edf->nef', t, w_gate)) * jnp.einsum('nd,edf->nef', t, w_up)
    a = a * gates[:, :, None].astype(a.dtype)
    return jnp.einsum('nef,efd->nd', a, w_down).reshape(B, T, D)

def _trunk(x, c, past, wts):
    new_even, new_odd = [], []
    for l in range(DEPTH):
        mod = jax.nn.silu(c) @ wts['w_ada'][l] + wts['b_ada'][l]
        sh1, sc1, g1, sh2, sc2, g2 = [m[:, None, :] for m in jnp.split(mod, 6, axis=-1)]
        h = _rmsnorm(x, wts['norm_mix'][l]) * (1.0 + sc1) + sh1
        i = l // 2
        if l % 2 == 0:
            p = None if past is None else (past['diff_k'][i], past['diff_v'][i], past['sb_k'][i], past['sb_v'][i])
            out, rows = _even_mixer(h, p, wts['w_in_even'][i], wts['w_out_even'][i], wts['diff_lq1'][i],
                                    wts['diff_lk1'][i], wts['diff_lq2'][i], wts['diff_lk2'][i],
                                    wts['diff_subln'][i], l)
            new_even.append(rows)
        else:
            p = None if past is None else (past['fox_k'][i], past['fox_v'][i], past['fox_logf'][i])
            out, rows = _odd_mixer(h, p, wts['w_in_odd'][i], wts['b_forget'][i], wts['w_out_odd'][i])
            new_odd.append(rows)
        x = x + g1 * out
        h = _rmsnorm(x, wts['norm_ffn'][l]) * (1.0 + sc2) + sh2
        x = x + g2 * _moe(h, wts['w_router'], wts['b_router'], wts['w_gate'][l], wts['w_up'][l], wts['w_down'][l])
    y = _rmsnorm(x, wts['norm_final'])
    even = [jnp.stack(r, axis=0) for r in zip(*new_even)]
    odd = [jnp.stack(r, axis=0) for r in zip(*new_odd)]
    return y, even, odd

def setup_inputs(seed: int = 0) -> dict:
    key = jax.random.key(seed)
    ks = iter(jax.random.split(key, 40))

    def nrm(shape, scale=1.0):
        return jax.random.normal(next(ks), shape, jnp.float32) * scale

    D = D_MODEL
    return {
        'x_prompt': nrm((BATCH, SEQ, D)),
        'x_sample': nrm((DEC_BATCH, DEC_SEQ, D)),
        'c_prompt': nrm((BATCH, D)),
        'c_sample': nrm((DEC_BATCH, D)),
        'cache_diff_k': nrm((N_EVEN, DEC_BATCH, PAST_LEN, N_DIFF_HEADS, 2 * HEAD_DIM)),
        'cache_diff_v': nrm((N_EVEN, DEC_BATCH, PAST_LEN, N_DIFF_HEADS, 2 * HEAD_DIM)),
        'cache_sb_k': nrm((N_EVEN, DEC_BATCH, PAST_LEN, N_SB_HEADS, HEAD_DIM)),
        'cache_sb_v': nrm((N_EVEN, DEC_BATCH, PAST_LEN, N_SB_HEADS, HEAD_DIM)),
        'cache_fox_k': nrm((N_ODD, DEC_BATCH, PAST_LEN, N_FOX_HEADS, HEAD_DIM)),
        'cache_fox_v': nrm((N_ODD, DEC_BATCH, PAST_LEN, N_FOX_HEADS, HEAD_DIM)),
        'cache_fox_logf': jax.nn.log_sigmoid(FORGET_BIAS_INIT + nrm((N_ODD, DEC_BATCH, PAST_LEN, N_FOX_HEADS))),
        'w_ada': nrm((DEPTH, D, 6 * D), 0.5 * D ** -0.5),
        'b_ada': nrm((DEPTH, 6 * D), 0.02),
        'norm_mix': 1.0 + nrm((DEPTH, D), 0.02),
        'norm_ffn': 1.0 + nrm((DEPTH, D), 0.02),
        'w_in_even': nrm((N_EVEN, D, 3 * DIFF_W + 3 * SB_W), D ** -0.5),
        'w_out_even': nrm((N_EVEN, DIFF_W + SB_W, D), (DIFF_W + SB_W) ** -0.5),
        'diff_lq1': nrm((N_EVEN, HEAD_DIM), 0.1),
        'diff_lk1': nrm((N_EVEN, HEAD_DIM), 0.1),
        'diff_lq2': nrm((N_EVEN, HEAD_DIM), 0.1),
        'diff_lk2': nrm((N_EVEN, HEAD_DIM), 0.1),
        'diff_subln': 1.0 + nrm((N_EVEN, 2 * HEAD_DIM), 0.02),
        'w_in_odd': nrm((N_ODD, D, 3 * FOX_W + N_FOX_HEADS), D ** -0.5),
        'b_forget': FORGET_BIAS_INIT + nrm((N_ODD, N_FOX_HEADS), 0.1),
        'w_out_odd': nrm((N_ODD, FOX_W, D), FOX_W ** -0.5),
        'w_router': nrm((D, N_EXPERTS), D ** -0.5),
        'b_router': nrm((N_EXPERTS,), 0.01),
        'w_gate': nrm((DEPTH, N_EXPERTS, D, D_EXPERT), D ** -0.5),
        'w_up': nrm((DEPTH, N_EXPERTS, D, D_EXPERT), D ** -0.5),
        'w_down': nrm((DEPTH, N_EXPERTS, D_EXPERT, D), D_EXPERT ** -0.5),
        'norm_final': 1.0 + nrm((D,), 0.02),
    }

def reference(x_prompt, x_sample, c_prompt, c_sample, cache_diff_k, cache_diff_v, cache_sb_k, cache_sb_v,
              cache_fox_k, cache_fox_v, cache_fox_logf, w_ada, b_ada, norm_mix, norm_ffn, w_in_even,
              w_out_even, diff_lq1, diff_lk1, diff_lq2, diff_lk2, diff_subln, w_in_odd, b_forget, w_out_odd,
              w_router, b_router, w_gate, w_up, w_down, norm_final):
    wts = {'w_ada': w_ada, 'b_ada': b_ada, 'norm_mix': norm_mix, 'norm_ffn': norm_ffn,
           'w_in_even': w_in_even, 'w_out_even': w_out_even, 'diff_lq1': diff_lq1, 'diff_lk1': diff_lk1,
           'diff_lq2': diff_lq2, 'diff_lk2': diff_lk2, 'diff_subln': diff_subln, 'w_in_odd': w_in_odd,
           'b_forget': b_forget, 'w_out_odd': w_out_odd, 'w_router': w_router, 'b_router': b_router,
           'w_gate': w_gate, 'w_up': w_up, 'w_down': w_down, 'norm_final': norm_final}
    past = {'diff_k': cache_diff_k, 'diff_v': cache_diff_v, 'sb_k': cache_sb_k, 'sb_v': cache_sb_v,
            'fox_k': cache_fox_k, 'fox_v': cache_fox_v, 'fox_logf': cache_fox_logf}
    y_prompt, (dk_p, dv_p, sk_p, sv_p), (fk_p, fv_p, fl_p) = _trunk(x_prompt, c_prompt, None, wts)
    y_sample, (dk_s, dv_s, sk_s, sv_s), (fk_s, fv_s, fl_s) = _trunk(x_sample, c_sample, past, wts)
    return (y_prompt, y_sample, dk_p, dv_p, sk_p, sv_p, fk_p, fv_p, fl_p,
            dk_s, dv_s, sk_s, sv_s, fk_s, fv_s, fl_s)


_drawn_inputs = setup_inputs


def setup_inputs(seed=0):
    import zlib

    import numpy as np

    out = dict(_drawn_inputs(seed))
    spreads = {}
    factors = {}
    for name, (base, spread) in spreads.items():
        noise = np.random.default_rng([zlib.crc32(name.encode()), seed]).standard_normal(out[name].shape)
        drawn = base * np.exp(spread * noise) if base else spread * noise
        out[name] = __import__('jax').numpy.asarray(drawn.astype(out[name].dtype))
    for name, factor in factors.items():
        out[name] = (out[name] * factor).astype(out[name].dtype)
    return out
```

```python
from contextlib import ExitStack

import numpy as np

import concourse.bass as bass
from concourse import mybir

F32 = mybir.dt.float32
BF16 = mybir.dt.bfloat16
I32 = mybir.dt.int32
ALU = mybir.AluOpType
ACT = mybir.ActivationFunctionType
X = mybir.AxisListType.X

P = 128
D = 1024
KD = D // P
SEQ, DEC, PAST = 512, 32, 256
NT = SEQ // P
TILES = NT + 1
TOK = SEQ + DEC
HD = 64
N_DIFF, N_SB, N_FOX = D // 256, D // 128, D // HD
QKV = 3 * D
CB = 512
NE, NG, EPG = 16, 4, 4
DE = D // 2
KE = DE // P
EPS = 1e-6
NEG = -1e30
LAM_INIT = 0.8 - 0.6
MAX_ITEMS = (2 * TOK + NE * (P - 1)) // P + 1
SLOTS = MAX_ITEMS * P


def rows(t):
    return P if t < NT else DEC


def group(t):
    return 0 if t < NT else 1


def cols(t):
    return slice(P * t, P * t + rows(t))


class Link:

    def __init__(self, eng, sem, base=0):
        self.eng, self.sem, self.base, self.n = eng, sem, base, 0

    def step(self, ins):
        ins.then_inc(self.sem, 1)
        self.n += 1

    def wait(self):
        self.eng.wait_ge(self.sem, self.base + self.n)

    def do(self, ins):
        self.step(ins)
        self.wait()


def encoder_step(nc, a, out, rope_dram):
    ctx = ExitStack()
    with ctx:
        def sb(name, shape, dt=F32):
            return ctx.enter_context(nc.sbuf_tensor(name, shape, dt))

        def sems(prefix, *names):
            return {n: ctx.enter_context(nc.semaphore(f"{prefix}_{n}")) for n in names}

        slot_rows = nc.dram_tensor("slot_rows", (SLOTS, D), F32, kind="Internal").ap()

        x = sb("x", [P, TILES, D])
        hT = sb("hT", [P, KD, TOK])
        arena = sb("arena", [P, TILES * QKV])
        ring = sb("ring", [P, 3, KD * CB])
        bc = sb("bc", [P, 4, 2, D])
        work = sb("work", [P, 4608])
        G1, A2, B2, G2 = range(4)

        ident = sb("ident", [P, P])
        ident_b = sb("ident_b", [P, P], BF16)
        causal_b = sb("causal_b", [P, P], BF16)
        chunk_b = sb("chunk_b", [P, P], BF16)
        strict_b = sb("strict_b", [P, P], BF16)
        ones = sb("ones", [P, P])
        neg_ones = sb("neg_ones", [P, P])
        upto = sb("upto", [P, P])
        before = sb("before", [P, P])
        neg_from = sb("neg_from", [P, P])
        pick = sb("pick", [P, 2, P])
        eps = sb("eps", [P, 1])
        silu_c = sb("silu_c", [P, KD, 32])
        c_in = sb("c_in", [P, 2, KD])
        ss = sb("ss", [P, 8])
        rstd = sb("rstd", [P, 8])
        rope = sb("rope", [P, TILES, 2, 8])
        lamv = sb("lamv", [P, 4, HD])
        lam = sb("lam", [P, 8])
        subg = sb("subg", [P, 1])
        wr = sb("wr", [P, KD, NE])
        br = sb("br", [P, NE])
        wf = sb("wf", [P, KD, N_FOX])
        bfb = sb("bfb", [P, N_FOX])
        logf = sb("logf", [P, 7, N_FOX])
        dcum = sb("dcum", [P, 7, N_FOX])
        ndcum = sb("ndcum", [P, 7, N_FOX])
        small = sb("small", [P, 64])
        ids = sb("ids", [P, 2, TILES], I32)
        item_expert = sb("item_expert", [1, MAX_ITEMS], I32)
        n_items = sb("n_items", [1, 2], I32)
        gates = sb("gates", [P, 2, TILES])
        bank = [ctx.enter_context(nc.psum_tensor(f"bank{i}", [P, 512], F32)) for i in range(8)]

        qkv = arena[:, :].rearrange("p (t c) -> p t c", c=QKV)
        w1 = ring[:, 2, :]

        g = sems("g", "settled", "phase", "const", "load_x", "load_small", "load_rope", "zero_rows", "setup")
        out_sems = sems("out", "kv0", "kv1", "y")

        phase_no = {"pe": 0, "act": 0, "dve": 0, "pool": 0}

        def phase_end(name, eng):
            phase_no[name] += 1
            eng.drain()
            eng.sem_inc(g["phase"], 1)
            eng.wait_ge(g["phase"], 4 * phase_no[name])

        def settle(eng):
            eng.sem_inc(g["settled"], 1)

        block = ctx.enter_context(nc.Block())

        PH = {}
        order = ["setup"]
        for l in range(2):
            order += [f"ada{l}", f"norm_mix{l}", f"proj{l}"]
            order += ["rope", "diff", "sb"] if l == 0 else ["forget", "fox"]
            order += [f"out{l}", f"norm_ffn{l}", f"route{l}", f"moe{l}", f"combine{l}"]
        order += ["final"]
        for i, n in enumerate(order):
            PH[n] = 4 * (i + 1)

        def setup_pool(pool):
            pool.memset(ident[:, :], 0.0)
            pool.memset(ident_b[:, :], 0.0)
            pool.memset(causal_b[:, :], 0.0)
            pool.memset(chunk_b[:, :], 0.0)
            pool.memset(strict_b[:, :], 0.0)
            pool.memset(ones[:, :], 1.0)
            pool.memset(neg_ones[:, :], -1.0)
            pool.memset(upto[:, :], 1.0)
            pool.memset(before[:, :], 1.0)
            pool.memset(neg_from[:, :], -1.0)
            pool.memset(pick[:, :, :], 0.0)
            pool.memset(eps[:, :], EPS)
            pool.memset(silu_c[:, :, :], 0.0).then_inc(g["const"], 1)
            pool.wait_ge(g["const"], 1)
            pool.memset(chunk_b[0:64, 64:128], NEG)
            for m in (ident, ident_b):
                pool.affine_select(out=m[:, :], in_=m[:, :], compare_op=ALU.not_equal, fill=1.0, base=0,
                                   pattern=[[-1, P]], channel_multiplier=1)
            pool.affine_select(out=causal_b[:, :], in_=causal_b[:, :], compare_op=ALU.is_ge, fill=NEG, base=0,
                               pattern=[[-1, P]], channel_multiplier=1)
            pool.affine_select(out=strict_b[:, :], in_=strict_b[:, :], compare_op=ALU.is_ge, fill=NEG, base=-1,
                               pattern=[[1, P]], channel_multiplier=-1)
            pool.affine_select(out=upto[:, :], in_=upto[:, :], compare_op=ALU.is_ge, fill=0.0, base=0,
                               pattern=[[1, P]], channel_multiplier=-1)
            pool.affine_select(out=before[:, :], in_=before[:, :], compare_op=ALU.is_ge, fill=0.0, base=-1,
                               pattern=[[1, P]], channel_multiplier=-1)
            pool.affine_select(out=neg_from[:, :], in_=neg_from[:, :], compare_op=ALU.is_ge, fill=0.0, base=0,
                               pattern=[[-1, P]], channel_multiplier=1)
            for grp in range(2):
                for q in range(4):
                    pool.drain()
                    pool.affine_select(out=pick[:, grp, :], in_=pick[:, grp, :], compare_op=ALU.not_equal,
                                       fill=1.0, base=-(32 * q + grp), pattern=[[0, P]], channel_multiplier=1)
            phase_end("pool", pool)

        def setup_act(act):
            act.wait_ge(g["load_small"], 16 * 11)
            act.wait_ge(g["const"], 1)
            act.activation(silu_c[:, :, 0:2], c_in[:, :, :].rearrange("p g k -> p k g"), ACT.Silu)
            phase_end("act", act)

        def setup_dve(dve):
            dve.memset(arena[:, 0:D], 0.0).then_inc(g["zero_rows"], 1)
            dve.memset(ss[:, :], 1.0)
            dve.wait_ge(g["load_small"], 16 * 11)
            lk = Link(dve, g["setup"])
            for i in range(2):
                lk.do(dve.tensor_tensor(lamv[:, 2 * i, :], lamv[:, 2 * i, :], lamv[:, 2 * i + 1, :], ALU.mult))
                lk.do(dve.reduce_sum(lam[:, i:i + 1], lamv[:, 2 * i, :], X))
            dve.tensor_scalar(subg[:, :], subg[:, :], 1.0 - LAM_INIT, None, ALU.mult)
            phase_end("dve", dve)

        def setup_sync(sp):
            small_loads = [
                (c_in[:, 0, :], a["c_prompt"].rearrange("a (p k) -> (a p) k", p=P)),
                (c_in[:, 1, :], a["c_sample"].rearrange("a (p k) -> (a p) k", p=P)),
                (lamv[:, 0, :], a["diff_lq1"][0, :].partition_broadcast(P)),
                (lamv[:, 1, :], a["diff_lk1"][0, :].partition_broadcast(P)),
                (lamv[:, 2, :], a["diff_lq2"][0, :].partition_broadcast(P)),
                (lamv[:, 3, :], a["diff_lk2"][0, :].partition_broadcast(P)),
                (subg[:, :], a["diff_subln"].rearrange("a (p k) -> (a p) k", p=P)),
                (wr[:, :, :], a["w_router"].rearrange("(k p) e -> p k e", p=P)),
                (br[:, :], a["b_router"].partition_broadcast(P)),
                (wf[:, :, :], a["w_in_odd"][0, :, QKV:QKV + N_FOX].rearrange("(k p) e -> p k e", p=P)),
                (bfb[:, :], a["b_forget"][0, :].partition_broadcast(P)),
            ]
            for dst, src in small_loads:
                sp.dma_start(dst, src).then_inc(g["load_small"], 16)
            sp.dma_start(x[:, 0:NT, :], a["x_prompt"][0].rearrange("(t p) d -> p t d", p=P)).then_inc(g["load_x"], 16)
            sp.dma_start(x[0:DEC, NT, :], a["x_sample"][0]).then_inc(g["load_x"], 16)
            sp.dma_start(rope[:, 0:NT, :, :].rearrange("p t a b -> p t (a b)"),
                         rope_dram[0:SEQ, :].rearrange("(t p) c -> p t c", p=P)).then_inc(g["load_rope"], 16)
            sp.dma_start(rope[0:DEC, NT, :, :].rearrange("p a b -> p (a b)"),
                         rope_dram[SEQ:TOK, :]).then_inc(g["load_rope"], 16)
            sp.dma_start(logf[:, 4:6, :], a["cache_fox_logf"][0, 0].rearrange("(t p) h -> p t h", p=P)).then_inc(g["load_rope"], 16)
            sp.wait_ge(g["zero_rows"], 1)
            sp.dma_start(slot_rows.rearrange("(n p) d -> p n d", p=P),
                         arena[:, 0:D].unsqueeze(1).to_broadcast([P, MAX_ITEMS, D])).then_inc(g["load_rope"], 16)
            sp.wait_ge(g["load_rope"], 64)
            sp.sem_inc(g["zero_rows"], 1)

        part = arena[:, 9216:10240].rearrange("p (b c) -> p b c", b=2)
        normg = arena[:, 10240:12288].rearrange("p (b c) -> p b c", b=2)
        bias2 = arena[0:2, 12288:13312].rearrange("p (b c) -> p b c", b=2)
        mod1 = arena[:, 5120:9216].rearrange("p (v g c) -> p v g c", v=2, g=2)
        ADA = sems("ada", "w0", "w1", "w2", "bias0", "bias1", "norm", "mv", "part", "biased", "rows", "placed")

        def mod_place(b):
            v, h = b // 2, slice(CB * (b % 2), CB * (b % 2) + CB)
            if v < 2:
                return lambda grp: mod1[0:(P, DEC)[grp], v, grp, h]
            slot = {2: G1, 3: B2, 4: A2, 5: G2}[v]
            return lambda grp: bc[0:(P, DEC)[grp], slot, grp, h]

        def ada_sync(sp, l):
            s = ADA
            before_this = "setup" if l == 0 else "combine0"
            if l == 0:
                sp.wait_ge(g["zero_rows"], 2)
            for b in range(12):
                if b == 0 and l == 1:
                    sp.wait_ge(g["phase"], PH[before_this])
                if b >= 3:
                    sp.wait_ge(s["mv"], 12 * l + b - 2)
                sp.dma_start(ring[:, b % 3, :].rearrange("p (k c) -> p k c", k=KD),
                             a["w_ada"][l, :, CB * b:CB * b + CB].rearrange("(p k) c -> p k c", k=KD)
                             ).then_inc(s[f"w{b % 3}"], 16)
                if b == 0:
                    sp.wait_ge(g["phase"], PH[before_this])
                    for i, n in enumerate(("norm_mix", "norm_ffn")):
                        sp.dma_start(normg[:, i, :], a[n][l, :].partition_broadcast(P)).then_inc(s["norm"], 16)
                if b >= 2:
                    sp.wait_ge(s["biased"], 12 * l + b - 1)
                sp.dma_start(bias2[:, b % 2, :], a["b_ada"][l, CB * b:CB * b + CB].partition_broadcast(2)
                             ).then_inc(s[f"bias{b % 2}"], 16)

        def ada_pe(pe, l):
            s = ADA

            def matvec(b):
                pe.wait_ge(s[f"w{b % 3}"], 64 * l + 16 * (b // 3 + 1))
                if b >= 2:
                    pe.wait_ge(s["part"], 12 * l + b - 1)
                w = ring[:, b % 3, :].rearrange("p (k c) -> p k c", k=KD)
                for k in range(KD):
                    q = k % 4
                    last = nc.tensor.matmul(bank[b % 2][32 * q:32 * q + 32, :], silu_c[:, k, :], w[:, k, :],
                                            start=k < 4, stop=k >= 4)
                last.then_inc(s["mv"], 1)

            def spread(b):
                pe.wait_ge(s["biased"], 12 * l + b + 1)
                if b >= 2:
                    pe.wait_ge(s["placed"], 24 * l + 2 * (b - 1))
                for grp in range(2):
                    n = (P, DEC)[grp]
                    nc.tensor.matmul(bank[2 + 2 * (b % 2) + grp][0:n, :], pick[:, grp, 0:n], part[:, b % 2, :],
                                     start=True, stop=True).then_inc(s["rows"], 1)

            matvec(0)
            for b in range(1, 12):
                matvec(b)
                spread(b - 1)
            spread(11)
            phase_end("pe", pe)

        def ada_act(act, l):
            s = ADA
            for b in range(12):
                act.wait_ge(s["mv"], 12 * l + b + 1)
                if b >= 2:
                    act.wait_ge(s["rows"], 24 * l + 2 * (b - 1))
                act.activation(part[:, b % 2, :], bank[b % 2][:, :], ACT.Copy).then_inc(s["part"], 1)
            phase_end("act", act)

        def ada_dve(dve, l):
            s = ADA

            def bias(b):
                dve.wait_ge(s["part"], 12 * l + b + 1)
                dve.wait_ge(s[f"bias{b % 2}"], 96 * l + 16 * (b // 2 + 1))
                dve.tensor_tensor(part[0:2, b % 2, :], part[0:2, b % 2, :], bias2[:, b % 2, :],
                                  ALU.add).then_inc(s["biased"], 1)

            def place(b):
                to, h = mod_place(b), slice(CB * (b % 2), CB * (b % 2) + CB)
                for grp in range(2):
                    n = (P, DEC)[grp]
                    dve.wait_ge(s["rows"], 24 * l + 2 * b + grp + 1)
                    src = bank[2 + 2 * (b % 2) + grp][0:n, :]
                    if b // 2 in (1, 4):
                        dve.scalar_tensor_tensor(out=to(grp), in0=src, scalar=1.0,
                                                 in1=normg[0:n, 0 if b // 2 == 1 else 1, h],
                                                 op0=ALU.add, op1=ALU.mult).then_inc(s["placed"], 1)
                    else:
                        dve.tensor_copy(to(grp), src).then_inc(s["placed"], 1)

            dve.wait_ge(s["norm"], 32 * l + 32)
            bias(0)
            for b in range(1, 12):
                bias(b)
                place(b - 1)
            place(11)
            phase_end("dve", dve)

        h_rows = arena[:, 0:TILES * D].rearrange("p (t d) -> p t d", d=D)
        junk = arena[:, 13312:14336]
        NORM = sems("norm", "square", "rstd", "scaled", "shifted", "tr", "ev_a", "ev_v", "self")
        NORM_NO = {"norm_mix0": 0, "norm_ffn0": 1, "norm_mix1": 2, "norm_ffn1": 3}

        def scale_shift(name, t):
            r, grp = rows(t), group(t)
            if name.startswith("norm_mix"):
                return mod1[0:r, 1, grp, :], mod1[0:r, 0, grp, :]
            return bc[0:r, A2, grp, :], bc[0:r, B2, grp, :]

        def norm_act(act, name):
            s, o = NORM, NORM_NO[name]
            if name == "norm_mix0":
                act.wait_ge(g["load_x"], 32)
            for t in range(TILES):
                if t >= 1:
                    act.wait_ge(s["square"], TILES * o + t)
                act.activation(junk[0:rows(t), :], x[0:rows(t), t, :], ACT.Square,
                               accum_out=ss[0:rows(t), t:t + 1]).then_inc(s["square"], 1)
            act.wait_ge(s["square"], TILES * (o + 1))
            act.activation(rstd[:, 0:TILES], ss[:, 0:TILES], ACT.Ln, scale=1.0 / D, bias=eps[:, :]).then_inc(s["self"], 1)
            act.wait_ge(s["self"], o + 1)
            act.activation(rstd[:, 0:TILES], rstd[:, 0:TILES], ACT.Exp, scale=-0.5).then_inc(s["rstd"], 1)
            for t in range(TILES):
                act.wait_ge(s["tr"], 10 * o + 2 * t + 1)
                act.activation(hT[:, 0:4, cols(t)], bank[(2 * t) % 8][:, :].rearrange("p (k c) -> p k c", k=4)[:, :, 0:rows(t)],
                               ACT.Copy).then_inc(s["ev_a"], 1)
            phase_end("act", act)

        def norm_dve(dve, name):
            s, o = NORM, NORM_NO[name]
            dve.wait_ge(s["rstd"], o + 1)
            for t in range(TILES):
                r = rows(t)
                dve.scalar_tensor_tensor(out=h_rows[0:r, t, :], in0=x[0:r, t, :], scalar=rstd[0:r, t:t + 1],
                                         in1=scale_shift(name, t)[0], op0=ALU.mult, op1=ALU.mult).then_inc(s["scaled"], 1)
                if t >= 1:
                    evac(dve, s, o, t - 1)
            evac(dve, s, o, TILES - 1)
            phase_end("dve", dve)

        def evac(dve, s, o, t):
            dve.wait_ge(s["tr"], 10 * o + 2 * t + 2)
            dve.tensor_copy(hT[:, 4:8, cols(t)],
                            bank[(2 * t + 1) % 8][:, :].rearrange("p (k c) -> p k c", k=4)[:, :, 0:rows(t)]).then_inc(s["ev_v"], 1)

        def norm_pool(pool, name):
            s, o = NORM, NORM_NO[name]
            for t in range(TILES):
                r = rows(t)
                pool.wait_ge(s["scaled"], 5 * o + t + 1)
                pool.tensor_tensor(h_rows[0:r, t, :], h_rows[0:r, t, :], scale_shift(name, t)[1],
                                   ALU.add).then_inc(s["shifted"], 1)
            phase_end("pool", pool)

        def norm_pe(pe, name):
            s, o = NORM, NORM_NO[name]
            for t in range(TILES):
                r = rows(t)
                pe.wait_ge(s["shifted"], 5 * o + t + 1)
                if t == 4:
                    pe.wait_ge(s["ev_a"], 5 * o + 1)
                    pe.wait_ge(s["ev_v"], 5 * o + 1)
                for half in range(2):
                    for k in range(4):
                        d0 = P * (4 * half + k)
                        last = nc.tensor.transpose(bank[(2 * t + half) % 8][:, P * k:P * k + r],
                                                   h_rows[0:r, t, d0:d0 + P], ident[0:r, 0:r])
                    last.then_inc(s["tr"], 1)
            phase_end("pe", pe)

        PROJ = sems("proj", "w0", "w1", "mm", "done", "ev_a", "ev_v")

        def proj_weights(sp, s, w, b, slot):
            sp.dma_start(ring[:, slot, :].rearrange("p (k c) -> p k c", k=KD),
                         w[:, bass.ds(b * CB, CB)].rearrange("(k p) c -> p k c", p=P)).then_inc(s[f"w{slot}"], 16)

        def proj_sync(sp, l):
            s, w = PROJ, a["w_in_even" if l == 0 else "w_in_odd"][0]
            sp.wait_ge(ADA["mv"], 12 * l + 12)
            proj_weights(sp, s, w, 0, 0)
            proj_weights(sp, s, w, 1, 1)
            with sp.Fori(1, 3) as j:
                for h in range(2):
                    sp.wait_ge(s["done"], 2 * j + h - 1 + 6 * l)
                    proj_weights(sp, s, w, 2 * j + h, h)

        def proj_pe(pe, l):
            s = PROJ
            with pe.Fori(0, 3) as j:
                for h in range(2):
                    pe.wait_ge(s[f"w{h}"], 16 * j + 16 + 48 * l)
                    w = ring[:, h, :].rearrange("p (k c) -> p k c", k=KD)
                    for t in range(TILES):
                        if t % 2 == 0:
                            pe.wait_ge(s["ev_a"], 3 * (2 * j + h) + t // 2 + 1 + 21 * l)
                        else:
                            pe.wait_ge(s["ev_v"], 2 * (2 * j + h) + t // 2 + 1 + 14 * l)
                        for k in range(KD):
                            last = nc.tensor.matmul(bank[t][0:rows(t), :], hT[:, k, cols(t)], w[:, k, :],
                                                    start=k == 0, stop=k == KD - 1)
                        last.then_inc(s["mm"], 1)
                    nc.tensor.drain().then_inc(s["done"], 1)
            if l == 1:
                for t in range(TILES):
                    for k in range(KD):
                        nc.tensor.matmul(bank[5][0:rows(t), N_FOX * t:N_FOX * t + N_FOX], hT[:, k, cols(t)],
                                         wf[:, k, :], start=k == 0, stop=k == KD - 1)
            phase_end("pe", pe)

        def proj_act(act, l):
            s = PROJ
            act.sem_inc(s["ev_a"], 3)
            with act.Fori(0, 3) as j:
                for h in range(2):
                    for t in (0, 2, 4):
                        act.wait_ge(s["mm"], 5 * (2 * j + h) + t + 1 + 30 * l)
                        act.activation(qkv[0:rows(t), t, bass.ds((2 * j + h) * CB, CB)], bank[t][0:rows(t), :],
                                       ACT.Copy).then_inc(s["ev_a"], 1)
            phase_end("act", act)

        def proj_dve(dve, l):
            s = PROJ
            dve.sem_inc(s["ev_v"], 2)
            with dve.Fori(0, 3) as j:
                for h in range(2):
                    for t in (1, 3):
                        dve.wait_ge(s["mm"], 5 * (2 * j + h) + t + 1 + 30 * l)
                        dve.tensor_copy(qkv[0:rows(t), t, bass.ds((2 * j + h) * CB, CB)],
                                        bank[t][0:rows(t), :]).then_inc(s["ev_v"], 1)
            phase_end("dve", dve)

        ROPE = sems("rope", "self", "lam")

        def rope_dve(dve):
            dve.wait_ge(g["load_rope"], 64)
            lk = Link(dve, ROPE["self"])
            t1, t2, t3, t4 = (work[:, 512 * i:512 * i + 512] for i in range(4))
            for t0, nt, r in ((0, NT, P), (NT, 1, DEC)):
                n = nt * 64
                for blk in range(2):
                    v = qkv[0:r, t0:t0 + nt, CB * blk:CB * blk + CB].rearrange("p t (h d) -> p t h d", d=HD)
                    x1, x2 = v[:, :, :, 0:8], v[:, :, :, 8:16]
                    cos = rope[0:r, t0:t0 + nt, 0, :].unsqueeze(2).to_broadcast([r, nt, 8, 8])
                    sin = rope[0:r, t0:t0 + nt, 1, :].unsqueeze(2).to_broadcast([r, nt, 8, 8])

                    def tmp(b):
                        return b[0:r, 0:n].rearrange("p (t h d) -> p t h d", t=nt, d=8)
                    lk.step(dve.tensor_tensor(tmp(t1), x1, cos, ALU.mult))
                    lk.step(dve.tensor_tensor(tmp(t2), x2, sin, ALU.mult))
                    lk.step(dve.tensor_tensor(tmp(t3), x2, cos, ALU.mult))
                    lk.do(dve.tensor_tensor(tmp(t4), x1, sin, ALU.mult))
                    lk.step(dve.tensor_tensor(x1, tmp(t1), tmp(t2), ALU.subtract))
                    lk.do(dve.tensor_tensor(x2, tmp(t3), tmp(t4), ALU.add))
            dve.wait_ge(ROPE["lam"], 1)
            dve.tensor_scalar(lam[:, 2:3], lam[:, 1:2], lam[:, 0:1], -LAM_INIT, ALU.subtract, ALU.add)
            phase_end("dve", dve)

        def store_kv(sp, l):
            sp.wait_ge(g["phase"], PH["rope" if l == 0 else "forget"])
            s = out_sems[f"kv{l}"]
            if l == 0:
                parts = [("diff_k", 1 * CB, CB), ("diff_v", 2 * CB, CB), ("sb_k", 4 * CB, CB), ("sb_v", 5 * CB, CB)]
            else:
                parts = [("fox_k", D, D), ("fox_v", 2 * D, D)]
            for n, c0, w in parts:
                sp.dma_start(out[n + "_p"].rearrange("a b (t p) h d -> p (a b t) (h d)", p=P),
                             qkv[:, 0:NT, c0:c0 + w]).then_inc(s, 16)
                sp.dma_start(out[n + "_s"].rearrange("a b p h d -> (a b p) (h d)"),
                             qkv[0:DEC, NT, c0:c0 + w]).then_inc(s, 16)
            if l == 1:
                sp.dma_start(out["fox_logf_p"].rearrange("a b (t p) h -> p (a b t) h", p=P), logf[:, 0:NT, :]).then_inc(s, 16)
                sp.dma_start(out["fox_logf_s"].rearrange("a b p h -> (a b p) h"), logf[0:DEC, 6, :]).then_inc(s, 16)

        KP, KS, QS, QKT = 512, 1024, 1312, 1344
        DF = sems("df", "past_k", "past_v", "staged", "staged_v", "tr", "tr_ev", "s", "mx", "e", "sc", "w", "pt", "pt_ev",
                  "o", "sq", "on", "ot", "ot_ev", "self_v", "self_a", "v_free")
        df_q = work[:, 0:640].rearrange("p (t d) -> p t d", d=P)
        df_k = work[:, 640:1536].rearrange("p (t d) -> p t d", d=P)
        df_pv = work[:, 4096:4480].rearrange("p (t d) -> p t d", d=P)
        df_p = work[:, 1792:3840].rearrange("p (u c k) -> p u c k", u=2, c=2)
        df_on = work[:, 3840:4096].rearrange("p (u d) -> p u d", u=2)
        df_qk = w1[:, 0:QKT]
        df_pt = w1[:, QKT:QKT + 1024].rearrange("p (u k) -> p u k", u=2)

        def transpose_rows(out_bank, tiles, np_):
            c = 0
            for src, r in tiles:
                last = nc.tensor.transpose(out_bank[0:np_, c:c + r], src, ident[0:r, 0:r])
                c += r
            return last

        def nkeys(i):
            return P * (i + 1) if i < NT else PAST + DEC

        def key_tiles(i):
            return [(j, P, P * j) for j in range(i + 1)] if i < NT else [(4, P, 0), (5, P, P), (6, DEC, 2 * P)]

        def diff_sync(sp):
            sp.wait_ge(g["phase"], PH["rope"])
            ck = a["cache_diff_k"][0, 0].rearrange("(t p) h d -> p t (h d)", p=P)
            cv = a["cache_diff_v"][0, 0].rearrange("(t p) h d -> p t (h d)", p=P)
            with sp.Fori(0, N_DIFF) as h:
                sp.wait_ge(DF["tr"], 3 * h + 1)
                sp.dma_start(df_k[:, 4:6, :], ck[:, :, bass.ds(h * P, P)]).then_inc(DF["past_k"], 16)
                sp.wait_ge(DF["v_free"], h + 1)
                sp.dma_start(df_pv[:, 0:2, :], cv[:, :, bass.ds(h * P, P)]).then_inc(DF["past_v"], 16)

        def diff_pool(pool):
            with pool.Fori(0, N_DIFF) as h:
                pool.wait_ge(DF["tr"], 3 * h + 1)
                for dst, c0, t_new in ((df_q, 0, 4), (df_k, CB, 6)):
                    pool.tensor_copy(dst[:, 0:NT, :], qkv[:, 0:NT, bass.ds(h * P + c0, P)]).then_inc(DF["staged"], 1)
                    pool.tensor_copy(dst[0:DEC, t_new, :], qkv[0:DEC, NT, bass.ds(h * P + c0, P)]).then_inc(DF["staged"], 1)
                pool.wait_ge(DF["v_free"], h + 1)
                pool.tensor_copy(df_pv[0:DEC, 2, :], qkv[0:DEC, NT, bass.ds(h * P + 2 * CB, P)]).then_inc(DF["staged_v"], 1)
            phase_end("pool", pool)

        def diff_pe(pe):
            pe.sem_inc(DF["tr"], 1)
            pe.sem_inc(DF["v_free"], 1)
            with pe.Fori(0, N_DIFF) as h:
                pe.wait_ge(DF["staged"], 4 * h + 4)
                transpose_rows(bank[7], [(df_q[:, t, :], P) for t in range(NT)], P).then_inc(DF["tr"], 1)
                transpose_rows(bank[4], [(df_k[:, t, :], P) for t in range(NT)], P).then_inc(DF["tr"], 1)
                pe.wait_ge(DF["past_k"], 16 * h + 16)
                pe.wait_ge(DF["tr_ev"], 3 * h + 1)
                transpose_rows(bank[7], [(df_k[:, 4, :], P), (df_k[:, 5, :], P), (df_k[0:DEC, 6, :], DEC),
                                         (df_q[0:DEC, 4, :], DEC)], P).then_inc(DF["tr"], 1)
                pe.wait_ge(DF["tr_ev"], 3 * h + 3)

                def scores(i):
                    if i >= 2:
                        pe.wait_ge(DF["e"], 10 * h + 2 * (i - 2) + 2)
                    if i == NT:
                        settle(pe)
                    r = rows(i)
                    q0, k0 = (P * i, KP) if i < NT else (QS, KS)
                    for c in range(2):
                        b = bank[2 * (i % 2) + c]
                        half = slice(HD * c, HD * c + HD)
                        last = nc.tensor.matmul(b[0:r, 0:nkeys(i)], df_qk[half, q0:q0 + r],
                                                df_qk[half, k0:k0 + nkeys(i)], start=True, stop=i == NT)
                        if i < NT:
                            last = nc.tensor.matmul(b[:, P * i:P * i + P], ident_b[:, :], chunk_b[:, :],
                                                    start=False, stop=True)
                        last.then_inc(DF["s"], 1)

                def turn(i):
                    pe.wait_ge(DF["w"], 5 * h + i + 1)
                    if i >= 1:
                        pe.wait_ge(DF["pt_ev"], 5 * h + i)
                    if i == NT:
                        settle(pe)
                    r = rows(i)
                    for n, (j, kr, c) in enumerate(key_tiles(i)):
                        last = nc.tensor.transpose(bank[4][0:kr, r * n:r * n + r], df_p[0:r, i % 2, 0, c:c + kr],
                                                   ident[0:r, 0:r])
                    last.then_inc(DF["pt"], 1)

                def values(i):
                    pe.wait_ge(DF["pt_ev"], 5 * h + i + 1)
                    if i >= 1:
                        pe.wait_ge(DF["on"], 5 * h + i)
                    if i == NT:
                        pe.wait_ge(DF["past_v"], 16 * h + 16)
                        pe.wait_ge(DF["staged_v"], h + 1)
                        settle(pe)
                    r = rows(i)
                    tiles = key_tiles(i)
                    for n, (j, kr, c) in enumerate(tiles):
                        if j < NT:
                            v = qkv[:, j, bass.ds(h * P + 2 * CB, P)]
                        else:
                            v = df_pv[0:kr, j - 4, :]
                        last = nc.tensor.matmul(bank[5][0:r, 0:P], df_pt[0:kr, i % 2, r * n:r * n + r], v,
                                                start=n == 0, stop=n == len(tiles) - 1)
                    last.then_inc(DF["o"], 1)

                def back(i):
                    pe.wait_ge(DF["on"], 5 * h + i + 1)
                    if i >= 1:
                        pe.wait_ge(DF["ot_ev"], 5 * h + i)
                    if i == NT:
                        settle(pe)
                    r = rows(i)
                    nc.tensor.transpose(bank[6][:, 0:r], df_on[0:r, i % 2, :], ident[0:r, 0:r]).then_inc(DF["ot"], 1)

                scores(0)
                for i in range(TILES):
                    if i + 1 < TILES:
                        scores(i + 1)
                    turn(i)
                    if i >= 1:
                        back(i - 1)
                    values(i)
                back(TILES - 1)
                nc.tensor.drain().then_inc(DF["v_free"], 1)
            phase_end("pe", pe)

        def diff_act(act):
            act.preload_act_table_set("natural_log_exp_and_others")
            with act.Fori(0, N_DIFF) as h:
                for n, (b, c0, w) in enumerate(((7, 0, 512), (4, KP, 512), (7, KS, 320))):
                    act.wait_ge(DF["tr"], 3 * h + n + 2)
                    act.activation(df_qk[:, c0:c0 + w], bank[b][:, 0:w], ACT.Copy).then_inc(DF["tr_ev"], 1)

                def probs(i):
                    r = rows(i)
                    if i >= 2:
                        act.wait_ge(DF["pt"], 5 * h + i - 1)
                    act.wait_ge(DF["mx"], 5 * h + i + 1)
                    for c in range(2):
                        act.activation(df_p[0:r, i % 2, c, 0:nkeys(i)], bank[2 * (i % 2) + c][0:r, 0:nkeys(i)], ACT.Exp,
                                       scale=HD ** -0.5, bias=small[0:r, 8 * (i % 2) + c:8 * (i % 2) + c + 1],
                                       accum_out=small[0:r, 8 * (i % 2) + 2 + c:8 * (i % 2) + 3 + c]).then_inc(DF["e"], 1)

                def turned(i):
                    r, n = rows(i), len(key_tiles(i))
                    act.wait_ge(DF["pt"], 5 * h + i + 1)
                    if i < NT:
                        act.activation(df_pt[:, i % 2, 0:r * n], bank[4][:, 0:r * n], ACT.Copy).then_inc(DF["pt_ev"], 1)
                    else:
                        act.activation(df_pt[:, i % 2, 0:2 * r], bank[4][:, 0:2 * r], ACT.Copy)
                        act.activation(df_pt[0:DEC, i % 2, 2 * r:3 * r], bank[4][0:DEC, 2 * r:3 * r],
                                       ACT.Copy).then_inc(DF["pt_ev"], 1)

                def norm(i):
                    r = rows(i)
                    act.wait_ge(DF["o"], 5 * h + i + 1)
                    z = small[0:r, 32:33]
                    lk = Link(act, DF["self_a"], base=15 * h + 3 * i)
                    lk.do(act.activation(df_on[0:r, i % 2, :], bank[5][0:r, 0:P], ACT.Square, accum_out=z))
                    lk.do(act.activation(z, z, ACT.Ln, scale=1.0 / P, bias=eps[0:r, :]))
                    lk.do(act.activation(z, z, ACT.Exp, scale=-0.5))
                    act.activation(df_on[0:r, i % 2, :], bank[5][0:r, 0:P], ACT.Copy, scale=z).then_inc(DF["on"], 1)

                def placed(i):
                    r = rows(i)
                    act.wait_ge(DF["ot"], 5 * h + i + 1)
                    act.activation(hT[:, bass.ds(h, 1), cols(i)].rearrange("p a c -> p (a c)"), bank[6][:, 0:r],
                                   ACT.Copy, scale=subg[:, :]).then_inc(DF["ot_ev"], 1)

                probs(0)
                for i in range(TILES):
                    if i + 1 < TILES:
                        probs(i + 1)
                    turned(i)
                    if i >= 1:
                        placed(i - 1)
                    norm(i)
                placed(TILES - 1)
            phase_end("act", act)

        def diff_dve(dve):
            with dve.Fori(0, N_DIFF) as h:
                lk = Link(dve, DF["self_v"], base=15 * h)

                def maxima(i):
                    r, o = rows(i), 8 * (i % 2)
                    for c in range(2):
                        dve.wait_ge(DF["s"], 10 * h + 2 * i + c + 1)
                        ins = dve.reduce_max(small[0:r, o + 4 + c:o + 5 + c], bank[2 * (i % 2) + c][0:r, 0:nkeys(i)], X)
                    lk.do(ins)
                    dve.tensor_scalar(small[0:r, o:o + 2], small[0:r, o + 4:o + 6], -HD ** -0.5, None,
                                      ALU.mult).then_inc(DF["mx"], 1)

                def weights(i):
                    r, o, n = rows(i), 8 * (i % 2), nkeys(i)
                    dve.wait_ge(DF["e"], 10 * h + 2 * i + 2)
                    lk.do(dve.reciprocal(small[0:r, o + 6:o + 8], small[0:r, o + 2:o + 4]))
                    dve.tensor_scalar(small[0:r, o + 7:o + 8], small[0:r, o + 7:o + 8], lam[0:r, 2:3], None, ALU.mult)
                    lk.do(dve.tensor_scalar(df_p[0:r, i % 2, 0, 0:n], df_p[0:r, i % 2, 0, 0:n],
                                            small[0:r, o + 6:o + 7], None, ALU.mult))
                    dve.scalar_tensor_tensor(out=df_p[0:r, i % 2, 0, 0:n], in0=df_p[0:r, i % 2, 1, 0:n],
                                             scalar=small[0:r, o + 7:o + 8], in1=df_p[0:r, i % 2, 0, 0:n],
                                             op0=ALU.mult, op1=ALU.add).then_inc(DF["w"], 1)

                maxima(0)
                for i in range(TILES):
                    if i + 1 < TILES:
                        maxima(i + 1)
                    weights(i)
            phase_end("dve", dve)

        SB = sems("sb", "past_k", "past_v", "staged", "tr", "ev_a", "ev_v", "z", "abs", "self_a", "e", "sp", "tri", "r", "w",
                  "pv", "o", "v_free", "self_p")
        sb_q = work[:, 0:640].rearrange("p (t d) -> p t d", d=P)
        sb_k = work[:, 640:1536].rearrange("p (t d) -> p t d", d=P)
        sb_v = work[:, 1536:2432].rearrange("p (t d) -> p t d", d=P)
        sb_r = work[:, 2432:3520].rearrange("p (h c) -> p h c", h=2)
        sb_w = work[:, 3520:4608].rearrange("p (u c) -> p u c", u=2)
        sb_qT = w1[:, 0:TOK]
        sb_kT = w1[:, TOK:TOK + 7 * P]
        sb_e = w1[:, 1440:2528].rearrange("p (u c) -> p u c", u=2)
        sb_s = w1[:, 2528:3616].rearrange("p (u c) -> p u c", u=2)
        SB_UNITS = [(j, hd) for j in (3, 2, 1, 0) for hd in (0, 1)]
        SB_SAMPLE = {3: 6, 2: 5, 1: 4}

        def sb_cols(j):
            return (SEQ - P * j) + (DEC if j >= 1 else 0)

        def sb_sync(sp):
            sp.wait_ge(g["phase"], PH["diff"])
            ck = a["cache_sb_k"][0, 0].rearrange("(t p) h d -> p t (h d)", p=P)
            cv = a["cache_sb_v"][0, 0].rearrange("(t p) h d -> p t (h d)", p=P)
            with sp.Fori(0, N_SB // 2) as i:
                sp.wait_ge(SB["tr"], 3 * i + 1)
                sp.dma_start(sb_k[:, 4:6, :], ck[:, :, bass.ds(i * P, P)]).then_inc(SB["past_k"], 16)
                sp.wait_ge(SB["v_free"], i + 1)
                sp.dma_start(sb_v[:, 4:6, :], cv[:, :, bass.ds(i * P, P)]).then_inc(SB["past_v"], 16)

        def sb_pool(pool):
            pool.memset(sb_k[:, 6, :], 0.0)
            pool.memset(sb_v[:, 6, :], 0.0)
            pool.drain()
            with pool.Fori(0, N_SB // 2) as i:
                pool.wait_ge(SB["tr"], 3 * i + 1)
                for dst, c0, t_new in ((sb_q, 3 * CB, 4), (sb_k, 4 * CB, 6)):
                    pool.tensor_copy(dst[:, 0:NT, :], qkv[:, 0:NT, bass.ds(i * P + c0, P)]).then_inc(SB["staged"], 1)
                    pool.tensor_copy(dst[0:DEC, t_new, :], qkv[0:DEC, NT, bass.ds(i * P + c0, P)]).then_inc(SB["staged"], 1)
                pool.wait_ge(SB["v_free"], i + 1)
                pool.tensor_copy(sb_v[:, 0:NT, :], qkv[:, 0:NT, bass.ds(i * P + 5 * CB, P)]).then_inc(SB["staged"], 1)
                pool.tensor_copy(sb_v[0:DEC, 6, :], qkv[0:DEC, NT, bass.ds(i * P + 5 * CB, P)]).then_inc(SB["staged"], 1)
                for u, (j, hd) in enumerate(SB_UNITS):
                    if j == 0:
                        continue
                    n = sb_cols(j)
                    pool.wait_ge(SB["sp"], 8 * i + u + 1)
                    settle(pool)
                    pool.tensor_copy(sb_r[:, hd, P * j:P * j + (P if j < 3 else n)],
                                     sb_s[:, u % 2, 0:(P if j < 3 else n)]).then_inc(SB["r"], 1)
                    if j < 3:
                        pool.wait_ge(SB["tri"], 8 * i + u + 1)
                        pool.tensor_tensor(sb_r[:, hd, P * j + P:TOK], sb_r[:, hd, P * j + P:TOK],
                                           sb_s[:, u % 2, P:n], ALU.add).then_inc(SB["r"], 1)
            phase_end("pool", pool)

        SB_R = [1, 2, 4, 6, 8, 10, 10, 10]

        def sb_pe(pe):
            pe.sem_inc(SB["tr"], 1)
            pe.sem_inc(SB["v_free"], 1)
            with pe.Fori(0, N_SB // 2) as i:
                pe.wait_ge(SB["staged"], 6 * i + 4)
                transpose_rows(bank[0], [(sb_q[:, t, :], P) for t in range(NT)], P).then_inc(SB["tr"], 1)
                transpose_rows(bank[1], [(sb_k[:, t, :], P) for t in range(NT)], P).then_inc(SB["tr"], 1)
                pe.wait_ge(SB["past_k"], 16 * i + 16)
                pe.wait_ge(SB["ev_a"], 3 * i + 1)
                transpose_rows(bank[0], [(sb_k[:, 4, :], P), (sb_k[:, 5, :], P), (sb_k[:, 6, :], P),
                                         (sb_q[0:DEC, 4, :], DEC)], P).then_inc(SB["tr"], 1)
                pe.wait_ge(SB["ev_a"], 3 * i + 3)
                pe.wait_ge(SB["ev_v"], i + 1)
                pe.wait_ge(SB["staged"], 6 * i + 6)
                pe.wait_ge(SB["past_v"], 16 * i + 16)

                def logits(u):
                    j, hd = SB_UNITS[u]
                    b, half, n = bank[2 + u % 4], slice(HD * hd, HD * hd + HD), SEQ - P * j
                    if u >= 4:
                        pe.wait_ge(SB["w"], 8 * i + u - 3)
                    nc.tensor.matmul(b[:, 0:n], sb_kT[half, P * j:P * j + P], sb_qT[half, P * j:SEQ],
                                     start=True, stop=False, skip_group_check=True)
                    if j >= 1:
                        kt = SB_SAMPLE[j]
                        nc.tensor.matmul(b[:, n:n + DEC], sb_kT[half, P * kt:P * kt + P], sb_qT[half, SEQ:TOK],
                                         start=False, stop=False, skip_group_check=True)
                    if j == 3:
                        nc.tensor.matmul(b[:, n:n + DEC], ident_b[:, :], strict_b[:, 0:DEC],
                                         start=False, stop=False, skip_group_check=True)
                    nc.tensor.matmul(b[:, 0:P], ident_b[:, :], strict_b[:, :],
                                     start=False, stop=True, skip_group_check=True).then_inc(SB["z"], 1)

                def later(u):
                    j, hd = SB_UNITS[u]
                    b, n = bank[2 + u % 4], sb_cols(j)
                    pe.wait_ge(SB["sp"], 8 * i + u + 1)
                    last = nc.tensor.matmul(b[:, 0:n], neg_from[:, :], sb_s[:, u % 2, 0:n], start=False, stop=True,
                                            skip_group_check=True)
                    if j < 3:
                        pe.wait_ge(SB["r"], 10 * i + SB_R[u - 2])
                        last = nc.tensor.matmul(b[:, P:n], neg_ones[:, :], sb_r[:, hd, P * j + P:P * j + n],
                                                start=False, stop=True, skip_group_check=True)
                    last.then_inc(SB["tri"], 1)

                def values(u):
                    j, hd = SB_UNITS[u]
                    half, n = slice(HD * hd, HD * hd + HD), SEQ - P * j
                    pe.wait_ge(SB["w"], 8 * i + u + 1)
                    last = nc.tensor.matmul(bank[7][half, P * j:SEQ], sb_v[:, j, half], sb_w[:, u % 2, 0:n],
                                            start=j == 3, stop=j == 0, skip_group_check=True)
                    if j >= 1:
                        last = nc.tensor.matmul(bank[6][half, 0:DEC], sb_v[:, SB_SAMPLE[j], half],
                                                sb_w[:, u % 2, n:n + DEC], start=j == 3, stop=j == 1)
                    last.then_inc(SB["pv"], 1)

                logits(0)
                logits(1)
                for u in range(8):
                    if u + 2 < 8:
                        logits(u + 2)
                    later(u)
                    if u >= 1:
                        values(u - 1)
                values(7)
                nc.tensor.drain().then_inc(SB["v_free"], 1)
            phase_end("pe", pe)

        def sb_act(act):
            act.preload_act_table_set("natural_log_exp_and_others")
            with act.Fori(0, N_SB // 2) as i:
                act.wait_ge(SB["tr"], 3 * i + 2)
                act.activation(sb_qT[:, 0:SEQ], bank[0][:, :], ACT.Copy, scale=HD ** -0.5).then_inc(SB["ev_a"], 1)
                act.wait_ge(SB["tr"], 3 * i + 4)
                act.activation(sb_kT[:, 4 * P:7 * P], bank[0][:, 0:3 * P], ACT.Copy).then_inc(SB["ev_a"], 1)
                act.activation(sb_qT[:, SEQ:TOK], bank[0][:, 3 * P:3 * P + DEC], ACT.Copy, scale=HD ** -0.5).then_inc(SB["ev_a"], 1)

                def log_part(u):
                    j, _ = SB_UNITS[u]
                    n, e = sb_cols(j), sb_e[:, u % 2, 0:sb_cols(j)]
                    act.wait_ge(SB["z"], 8 * i + u + 1)
                    if u >= 2:
                        act.wait_ge(SB["sp"], 8 * i + u - 1)
                    lk = Link(act, SB["self_a"], base=16 * i + 2 * u)
                    lk.do(act.activation(e, bank[2 + u % 4][:, 0:n], ACT.Abs))
                    lk.do(act.activation(e, e, ACT.Exp, scale=-1.0))
                    act.activation(e, e, ACT.Ln, bias=1.0).then_inc(SB["e"], 1)

                def weight(u):
                    n = sb_cols(SB_UNITS[u][0])
                    act.wait_ge(SB["tri"], 8 * i + u + 1)
                    if u >= 2:
                        act.wait_ge(SB["pv"], 8 * i + u - 1)
                    act.activation(sb_w[:, u % 2, 0:n], bank[2 + u % 4][:, 0:n], ACT.Exp).then_inc(SB["w"], 1)

                log_part(0)
                log_part(1)
                for u in range(8):
                    if u + 2 < 8:
                        log_part(u + 2)
                    weight(u)
            phase_end("act", act)

        def sb_dve(dve):
            with dve.Fori(0, N_SB // 2) as i:
                dve.wait_ge(SB["tr"], 3 * i + 3)
                dve.tensor_copy(sb_kT[:, 0:SEQ], bank[1][:, :]).then_inc(SB["ev_v"], 1)
                for u, (j, hd) in enumerate(SB_UNITS):
                    n = sb_cols(j)
                    dve.wait_ge(SB["e"], 8 * i + u + 1)
                    if u >= 2:
                        dve.wait_ge(SB["tri"], 8 * i + u - 1)
                        dve.wait_ge(SB["r"], 10 * i + SB_R[u - 2])
                    dve.scalar_tensor_tensor(out=sb_s[:, u % 2, 0:n], in0=bank[2 + u % 4][:, 0:n], scalar=0.0,
                                             in1=sb_e[:, u % 2, 0:n], op0=ALU.max, op1=ALU.add).then_inc(SB["sp"], 1)
                for hd in range(2):
                    half = slice(HD * hd, HD * hd + HD)
                    dve.wait_ge(SB["pv"], 8 * i + 7 + hd)
                    dve.tensor_copy(hT[half, bass.ds(i + 4, 1), 0:SEQ].rearrange("p a c -> p (a c)"), bank[7][half, :])
                    dve.tensor_copy(hT[half, bass.ds(i + 4, 1), SEQ:TOK].rearrange("p a c -> p (a c)"),
                                    bank[6][half, 0:DEC]).then_inc(SB["o"], 1)
            phase_end("dve", dve)

        FG = sems("fg", "self", "biased", "l1", "logf", "cum")

        def forget_dve(dve):
            lk = Link(dve, FG["self"])
            y = work[:, 0:TILES * N_FOX].rearrange("p (t h) -> p t h", h=N_FOX)
            for t in range(TILES):
                r = rows(t)
                dve.tensor_tensor(y[0:r, t, :], bank[5][0:r, N_FOX * t:N_FOX * t + N_FOX], bfb[0:r, :],
                                  ALU.add).then_inc(FG["biased"], 1)
            dve.wait_ge(FG["l1"], 2)
            e = work[:, 128:128 + TILES * N_FOX].rearrange("p (t h) -> p t h", h=N_FOX)
            dve.scalar_tensor_tensor(out=logf[:, 0:NT, :], in0=y[:, 0:NT, :], scalar=0.0, in1=e[:, 0:NT, :],
                                     op0=ALU.min, op1=ALU.subtract).then_inc(FG["logf"], 1)
            dve.scalar_tensor_tensor(out=logf[0:DEC, 6, :], in0=y[0:DEC, NT, :], scalar=0.0, in1=e[0:DEC, NT, :],
                                     op0=ALU.min, op1=ALU.subtract).then_inc(FG["logf"], 1)
            dve.wait_ge(FG["cum"], 1)
            b6 = bank[6][:, 0:7 * N_FOX].rearrange("p (t h) -> p t h", h=N_FOX)
            for t0, t1, r in ((0, 6, P), (6, 7, DEC)):
                dve.tensor_copy(dcum[0:r, t0:t1, :], b6[0:r, t0:t1, :])
                dve.tensor_scalar(ndcum[0:r, t0:t1, :], b6[0:r, t0:t1, :], -1.0, None, ALU.mult)
            phase_end("dve", dve)

        def forget_act(act):
            act.preload_act_table_set("natural_log_exp_and_others")
            act.wait_ge(FG["biased"], TILES)
            for n, (c0, c1, r) in enumerate(((0, NT * N_FOX, P), (NT * N_FOX, TILES * N_FOX, DEC))):
                e = work[0:r, 128 + c0:128 + c1]
                lk = Link(act, FG["self"], base=2 * n)
                lk.do(act.activation(e, work[0:r, c0:c1], ACT.Abs))
                lk.do(act.activation(e, e, ACT.Exp, scale=-1.0))
                act.activation(e, e, ACT.Ln, bias=1.0).then_inc(FG["l1"], 1)
            phase_end("act", act)

        def forget_pool(pool):
            pool.tensor_scalar(qkv[:, 0:NT, 0:D], qkv[:, 0:NT, 0:D], HD ** -0.5, None, ALU.mult)
            pool.tensor_scalar(qkv[0:DEC, NT, 0:D], qkv[0:DEC, NT, 0:D], HD ** -0.5, None, ALU.mult)
            phase_end("pool", pool)

        def forget_pe(pe):
            pe.wait_ge(FG["logf"], 2)
            pe.wait_ge(g["load_rope"], 64)
            for tiles in ([(0, P), (1, P), (2, P), (3, P)], [(4, P), (5, P), (6, DEC)]):
                for n, (t, r) in enumerate(tiles):
                    dst = bank[6][0:r, N_FOX * t:N_FOX * t + N_FOX]
                    last = nc.tensor.matmul(dst, upto[0:r, 0:r], logf[0:r, t, :], start=True, stop=n == 0)
                    for m, (e, _) in enumerate(tiles[:n]):
                        last = nc.tensor.matmul(dst, ones[:, 0:r], logf[:, e, :], start=False, stop=m == n - 1)
            last.then_inc(FG["cum"], 1)
            phase_end("pe", pe)

        FX = sems("fx", "past_k", "past_v", "staged", "staged_v", "tr", "ev_a", "ev_v", "s", "m", "e", "p", "pt", "pt_ev", "pv",
                  "o", "v_free", "self_v")
        KQ = HD + 2
        fx_q = work[:, 0:660].rearrange("p (t h d) -> p t h d", h=2, d=KQ)
        fx_k = work[:, 660:1584].rearrange("p (t h d) -> p t h d", h=2, d=KQ)
        fx_v = work[:, 1584:2480].rearrange("p (t h d) -> p t h d", h=2, d=HD)
        fx_p = work[:, 2480:4016].rearrange("p (u k) -> p u k", u=3)
        fx_qk = w1[:, 0:2 * QKT].rearrange("p (h c) -> p h c", h=2)
        fx_pt = w1[:, 2 * QKT:2 * QKT + 1024].rearrange("p (u k) -> p u k", u=2)
        FX_UNITS = [(i, hd) for i in range(TILES) for hd in (0, 1)]

        def fox_sync(sp):
            sp.wait_ge(g["phase"], PH["forget"])
            ck = a["cache_fox_k"][0, 0].rearrange("(t p) h d -> p t h d", p=P)
            cv = a["cache_fox_v"][0, 0].rearrange("(t p) h d -> p t h d", p=P)
            with sp.Fori(0, N_FOX // 2) as i:
                sp.wait_ge(FX["tr"], 6 * i + 1)
                for hd in range(2):
                    sp.dma_start(fx_k[:, 4:6, hd, 0:HD], ck[:, :, bass.ds(2 * i + hd, 1), :].rearrange("p t a d -> p t (a d)")
                                 ).then_inc(FX["past_k"], 16)
                sp.wait_ge(FX["v_free"], i + 1)
                sp.dma_start(fx_v[:, 4:6, :, :].rearrange("p t h d -> p t (h d)"),
                             cv[:, :, bass.ds(2 * i, 2), :].rearrange("p t h d -> p t (h d)")).then_inc(FX["past_v"], 16)

        def fox_pool(pool):
            pool.memset(fx_q[:, :, :, HD:HD + 1], 1.0)
            pool.memset(fx_k[:, :, :, HD + 1:HD + 2], 1.0)
            pool.drain()
            with pool.Fori(0, N_FOX // 2) as i:
                pool.wait_ge(FX["tr"], 6 * i + 1)
                for t0, nt, r, tk in ((0, NT, P, 0), (NT, 1, DEC, 6)):
                    def heads(c0):
                        return qkv[0:r, t0:t0 + nt, bass.ds(i * P + c0, P)].rearrange("p t (h d) -> p t h d", d=HD)
                    pool.tensor_copy(fx_q[0:r, t0:t0 + nt, :, 0:HD], heads(0)).then_inc(FX["staged"], 1)
                    pool.tensor_copy(fx_q[0:r, t0:t0 + nt, :, HD + 1], dcum[0:r, tk:tk + nt, bass.ds(2 * i, 2)]
                                     ).then_inc(FX["staged"], 1)
                    pool.tensor_copy(fx_k[0:r, tk:tk + nt, :, 0:HD], heads(D)).then_inc(FX["staged"], 1)
                pool.tensor_copy(fx_k[:, 0:6, :, HD], ndcum[:, 0:6, bass.ds(2 * i, 2)]).then_inc(FX["staged"], 1)
                pool.tensor_copy(fx_k[0:DEC, 6, :, HD], ndcum[0:DEC, 6, bass.ds(2 * i, 2)]).then_inc(FX["staged"], 1)
                pool.wait_ge(FX["v_free"], i + 1)
                pool.tensor_copy(fx_v[:, 0:NT, :, :].rearrange("p t h d -> p t (h d)"),
                                 qkv[:, 0:NT, bass.ds(i * P + 2 * D, P)]).then_inc(FX["staged_v"], 1)
                pool.tensor_copy(fx_v[0:DEC, 6, :, :].rearrange("p h d -> p (h d)"),
                                 qkv[0:DEC, NT, bass.ds(i * P + 2 * D, P)]).then_inc(FX["staged_v"], 1)
            phase_end("pool", pool)

        def fox_pe(pe):
            pe.sem_inc(FX["tr"], 1)
            pe.sem_inc(FX["v_free"], 1)
            with pe.Fori(0, N_FOX // 2) as i:
                pe.wait_ge(FX["staged"], 8 * i + 8)
                for hd in range(2):
                    b0, b1 = (0, 1) if hd == 0 else (1, 0)
                    if hd == 1:
                        pe.wait_ge(FX["ev_a"], 3 * i + 2)
                    transpose_rows(bank[b0], [(fx_q[:, t, hd, :], P) for t in range(NT)], KQ).then_inc(FX["tr"], 1)
                    if hd == 1:
                        pe.wait_ge(FX["ev_a"], 3 * i + 3)
                    transpose_rows(bank[b1], [(fx_k[:, t, hd, :], P) for t in range(NT)], KQ).then_inc(FX["tr"], 1)
                    if hd == 0:
                        pe.wait_ge(FX["past_k"], 32 * i + 32)
                        pe.wait_ge(FX["ev_a"], 3 * i + 1)
                    else:
                        pe.wait_ge(FX["ev_v"], 3 * i + 1)
                    transpose_rows(bank[b0], [(fx_k[:, 4, hd, :], P), (fx_k[:, 5, hd, :], P), (fx_k[0:DEC, 6, hd, :], DEC),
                                              (fx_q[0:DEC, 4, hd, :], DEC)], KQ).then_inc(FX["tr"], 1)
                pe.wait_ge(FX["ev_a"], 3 * i + 3)

                def scores(u):
                    t, hd = FX_UNITS[u]
                    b, r, n = bank[2 + u % 3], rows(t), nkeys(t)
                    if hd == 1:
                        pe.wait_ge(FX["ev_v"], 3 * i + 3)
                    if u >= 3:
                        pe.wait_ge(FX["e"], 10 * i + u - 2)
                    q0, k0 = (P * t, KP) if t < NT else (QS, KS)
                    nc.tensor.matmul(b[0:r, 0:n], fx_qk[0:KQ, hd, q0:q0 + r], fx_qk[0:KQ, hd, k0:k0 + n],
                                     start=True, stop=False)
                    nc.tensor.matmul(b[0:r, n - r:n], ident_b[0:r, 0:r], causal_b[0:r, 0:r],
                                     start=False, stop=True).then_inc(FX["s"], 1)

                def turn(u):
                    t, hd = FX_UNITS[u]
                    r = rows(t)
                    pe.wait_ge(FX["p"], 10 * i + u + 1)
                    if u >= 2:
                        pe.wait_ge(FX["pt_ev"], 10 * i + u - 1)
                    if t == NT:
                        settle(pe)
                    for n, (j, kr, c) in enumerate(key_tiles(t)):
                        last = nc.tensor.transpose(bank[5 + u % 2][0:kr, r * n:r * n + r], fx_p[0:r, u % 3, c:c + kr],
                                                   ident[0:r, 0:r])
                    last.then_inc(FX["pt"], 1)

                def values(u):
                    t, hd = FX_UNITS[u]
                    r, half = rows(t), slice(HD * hd, HD * hd + HD)
                    pe.wait_ge(FX["pt_ev"], 10 * i + u + 1)
                    if u == 0:
                        pe.wait_ge(FX["staged_v"], 2 * i + 2)
                    if t == NT and hd == 0:
                        pe.wait_ge(FX["past_v"], 16 * i + 16)
                    dst = bank[7][half, P * t:P * t + P] if t < NT else bank[5 + u % 2][half, P:P + DEC]
                    tiles = key_tiles(t)
                    for n, (j, kr, c) in enumerate(tiles):
                        last = nc.tensor.matmul(dst, fx_v[0:kr, j, hd, :], fx_pt[0:kr, u % 2, r * n:r * n + r],
                                                start=n == 0, stop=n == len(tiles) - 1)
                    last.then_inc(FX["pv"], 1)

                scores(0)
                scores(1)
                for u in range(10):
                    if u + 2 < 10:
                        scores(u + 2)
                    turn(u)
                    if u >= 1:
                        values(u - 1)
                values(9)
                nc.tensor.drain().then_inc(FX["v_free"], 1)
            phase_end("pe", pe)

        def fox_act(act):
            act.preload_act_table_set("natural_log_exp_and_others")
            with act.Fori(0, N_FOX // 2) as i:
                for n, (b, c0, w) in enumerate(((0, 0, 512), (1, KP, 512), (0, KS, 320))):
                    act.wait_ge(FX["tr"], 6 * i + n + 2)
                    act.activation(fx_qk[0:KQ, 0, c0:c0 + w], bank[b][0:KQ, 0:w], ACT.Copy).then_inc(FX["ev_a"], 1)

                def probs(u):
                    t, hd = FX_UNITS[u]
                    r, n = rows(t), nkeys(t)
                    act.wait_ge(FX["m"], 10 * i + u + 1)
                    if u >= 3:
                        act.wait_ge(FX["pt"], 10 * i + u - 2)
                    act.activation(fx_p[0:r, u % 3, 0:n], bank[2 + u % 3][0:r, 0:n], ACT.Exp, scale=1.0,
                                   bias=small[0:r, u:u + 1], accum_out=small[0:r, 16 + u:17 + u]).then_inc(FX["e"], 1)

                def turned(u):
                    t, hd = FX_UNITS[u]
                    r, n = rows(t), len(key_tiles(t))
                    act.wait_ge(FX["pt"], 10 * i + u + 1)
                    if u >= 2:
                        act.wait_ge(FX["pv"], 10 * i + u - 1)
                    b = bank[5 + u % 2]
                    if t < NT:
                        act.activation(fx_pt[:, u % 2, 0:r * n], b[:, 0:r * n], ACT.Copy).then_inc(FX["pt_ev"], 1)
                    else:
                        act.activation(fx_pt[:, u % 2, 0:2 * r], b[:, 0:2 * r], ACT.Copy)
                        act.activation(fx_pt[0:DEC, u % 2, 2 * r:3 * r], b[0:DEC, 2 * r:3 * r],
                                       ACT.Copy).then_inc(FX["pt_ev"], 1)

                probs(0)
                probs(1)
                for u in range(10):
                    if u + 2 < 10:
                        probs(u + 2)
                    turned(u)
            phase_end("act", act)

        def fox_dve(dve):
            with dve.Fori(0, N_FOX // 2) as i:
                for n, (b, c0, w) in enumerate(((1, 0, 512), (0, KP, 512), (1, KS, 320))):
                    dve.wait_ge(FX["tr"], 6 * i + n + 5)
                    dve.tensor_copy(fx_qk[0:KQ, 1, c0:c0 + w], bank[b][0:KQ, 0:w]).then_inc(FX["ev_v"], 1)

                def maxima(u):
                    t, hd = FX_UNITS[u]
                    r, n = rows(t), nkeys(t)
                    dve.wait_ge(FX["s"], 10 * i + u + 1)
                    dve.reduce_max(small[0:r, u:u + 1], bank[2 + u % 3][0:r, 0:n], X, negate=True).then_inc(FX["m"], 1)

                def normed(u):
                    t, hd = FX_UNITS[u]
                    r, n = rows(t), nkeys(t)
                    dve.wait_ge(FX["e"], 10 * i + u + 1)
                    lk = Link(dve, FX["self_v"], base=10 * i + u)
                    lk.do(dve.reciprocal(small[0:r, 16 + u:17 + u], small[0:r, 16 + u:17 + u]))
                    dve.tensor_scalar(fx_p[0:r, u % 3, 0:n], fx_p[0:r, u % 3, 0:n], small[0:r, 16 + u:17 + u], None,
                                      ALU.mult).then_inc(FX["p"], 1)

                maxima(0)
                for u in range(10):
                    if u + 1 < 10:
                        maxima(u + 1)
                    normed(u)
                for hd in range(2):
                    half = slice(HD * hd, HD * hd + HD)
                    dve.wait_ge(FX["pv"], 10 * i + 9 + hd)
                    dve.tensor_copy(hT[half, bass.ds(i, 1), 0:SEQ].rearrange("p a c -> p (a c)"), bank[7][half, :])
                    dve.tensor_copy(hT[half, bass.ds(i, 1), SEQ:TOK].rearrange("p a c -> p (a c)"),
                                    bank[5 + hd][half, P:P + DEC]).then_inc(FX["o"], 1)
            phase_end("dve", dve)

        OUT = sems("outp", "w0", "w1", "mm", "ev", "add")
        o_tmp = arena[:, 0:1024].rearrange("p (u c) -> p u c", u=2)

        def out_sync(sp, l):
            s, w = OUT, a["w_out_even" if l == 0 else "w_out_odd"][0]
            sp.wait_ge(PROJ["done"], 6 * l + 6)
            for n in range(2):
                sp.dma_start(ring[:, n, :].rearrange("p (k c) -> p k c", k=KD),
                             w[:, CB * n:CB * n + CB].rearrange("(k p) c -> p k c", p=P)).then_inc(s[f"w{n}"], 16)

        def out_pe(pe, l):
            s = OUT
            for n in range(2):
                pe.wait_ge(s[f"w{n}"], 16 * l + 16)
                w = ring[:, n, :].rearrange("p (k c) -> p k c", k=KD)
                for t in range(TILES):
                    u = TILES * n + t
                    if u >= 8:
                        pe.wait_ge(s["ev"], 10 * l + u - 7)
                    for k in range(KD):
                        last = nc.tensor.matmul(bank[u % 8][0:rows(t), :], hT[:, k, cols(t)], w[:, k, :],
                                                start=k == 0, stop=k == KD - 1)
                    last.then_inc(s["mm"], 1)
            phase_end("pe", pe)

        def out_dve(dve, l):
            s = OUT
            dve.wait_ge(out_sems[f"kv{l}"], 16 * (8 if l == 0 else 6))
            for u in range(2 * TILES):
                n, t = u // TILES, u % TILES
                r = rows(t)
                dve.wait_ge(s["mm"], 10 * l + u + 1)
                if u >= 2:
                    dve.wait_ge(s["add"], 10 * l + u - 1)
                dve.tensor_tensor(o_tmp[0:r, u % 2, :], bank[u % 8][0:r, :], bc[0:r, G1, group(t), CB * n:CB * n + CB],
                                  ALU.mult).then_inc(s["ev"], 1)
            phase_end("dve", dve)

        def out_pool(pool, l):
            s = OUT
            for u in range(2 * TILES):
                n, t = u // TILES, u % TILES
                r = rows(t)
                pool.wait_ge(s["ev"], 10 * l + u + 1)
                pool.tensor_tensor(x[0:r, t, CB * n:CB * n + CB], x[0:r, t, CB * n:CB * n + CB],
                                   o_tmp[0:r, u % 2, :], ALU.add).then_inc(s["add"], 1)
            phase_end("pool", pool)

        RT = sems("rt", "logits", "e", "self", "mask", "pos", "cnt", "done", "scat")
        rt_self = [0]
        rt = arena[:, 5120:9216]

        def rv(i, n=TILES * NE):
            return rt[:, 96 * i:96 * i + n]

        def route_pe(pe, l):
            s = RT
            for t in range(TILES):
                for k in range(KD):
                    last = nc.tensor.matmul(bank[0][0:rows(t), NE * t:NE * t + NE], hT[:, k, cols(t)], wr[:, k, :],
                                            start=k == 0, stop=k == KD - 1)
            last.then_inc(s["logits"], 1)
            pe.wait_ge(s["mask"], l + 1)
            mask = rv(12).rearrange("p (t e) -> p t e", e=NE)
            for t in range(TILES):
                r = rows(t)
                dst = bank[1][0:r, NE * t:NE * t + NE]
                last = nc.tensor.matmul(dst, before[0:r, 0:r], mask[0:r, t, :], start=True, stop=t == 0)
                for e in range(t):
                    last = nc.tensor.matmul(dst, ones[:, 0:r], mask[:, e, :], start=False, stop=e == t - 1)
            for t in range(TILES):
                last = nc.tensor.matmul(bank[2][:, 0:NE], ones[0:rows(t), :], mask[0:rows(t), t, :],
                                        start=t == 0, stop=t == TILES - 1)
            last.then_inc(s["pos"], 1)
            phase_end("pe", pe)

        def route_act(act, l):
            s = RT
            act.preload_act_table_set("natural_log_exp_and_others")
            act.wait_ge(s["cnt"], l + 1)
            act.wait_ge(s["logits"], l + 1)
            act.activation(rv(0)[:, 0:NT * NE], bank[0][:, 0:NT * NE], ACT.Exp, scale=-1.0)
            act.activation(rv(0)[0:DEC, NT * NE:TILES * NE], bank[0][0:DEC, NT * NE:TILES * NE], ACT.Exp,
                           scale=-1.0).then_inc(s["e"], 1)
            phase_end("act", act)

        def route_pool(pool, l):
            s = RT
            pool.iota(rt[:, 2400:2416], pattern=[[-1, NE]], base=NE, channel_multiplier=0, allow_small_or_imprecise_dtypes=True)
            pool.iota(rt[:, 2416:2420], pattern=[[-1, NG]], base=NG, channel_multiplier=0, allow_small_or_imprecise_dtypes=True)
            pool.iota(rt[:, 2432:2432 + MAX_ITEMS], pattern=[[1, MAX_ITEMS]], base=0, channel_multiplier=0,
                      allow_small_or_imprecise_dtypes=True)
            pool.memset(rv(0), 1.0).then_inc(s["cnt"], 1)
            pool.wait_ge(s["done"], l + 1)
            for t in range(TILES):
                r = rows(t)
                for c in range(2):
                    pool.indirect_dma_start(slot_rows, bass.IndirectOffsetOnAxis(ids[0:r, c, t:t + 1], 0),
                                            h_rows[0:r, t, :], None).then_inc(s["scat"], 16)
            pool.wait_ge(s["scat"], 16 * 2 * TILES * (l + 1))
            phase_end("pool", pool)

        def route_dve(dve, l):
            s = RT
            lk = Link(dve, s["self"], base=rt_self[0])
            T3 = lambda v, e: v.rearrange("p (t e) -> p t e", e=e)
            sig, sel, pair, selm, tmp, oh1, oh2, key, mask, dst = rv(1), rv(2), rv(3, 120), rv(5), rv(6), rv(7), rv(8), rv(9), rv(12), rv(13)
            gs, gk, gsel = rt[:, 2080:2100], rt[:, 2100:2120], rt[:, 2120:2140]
            m1 = rt[:, 2140:2145]
            rank, grank, item = rt[:, 2400:2416], rt[:, 2416:2420], rt[:, 2432:2432 + MAX_ITEMS]

            def bt(v, n):
                return v.unsqueeze(1).to_broadcast([P, TILES, n])

            def be(v, n):
                return v.unsqueeze(2).to_broadcast([P, TILES, n])

            dve.wait_ge(s["cnt"], l + 1)
            dve.wait_ge(s["e"], l + 1)
            lk.do(dve.tensor_scalar(sig, rv(0), 1.0, None, ALU.add))
            lk.do(dve.reciprocal(sig, sig))
            lk.do(dve.tensor_tensor(T3(sel, NE), T3(sig, NE), bt(br[:, :], NE), ALU.add))
            s4 = sel.rearrange("p (n e) -> p n e", e=EPG)
            p6 = pair.rearrange("p (n e) -> p n e", e=6)
            lk.step(dve.tensor_tensor(p6[:, :, 0:3], s4[:, :, 0:3], s4[:, :, 1:4], ALU.add))
            lk.step(dve.tensor_tensor(p6[:, :, 3:5], s4[:, :, 0:2], s4[:, :, 2:4], ALU.add))
            lk.do(dve.tensor_tensor(p6[:, :, 5:6], s4[:, :, 0:1], s4[:, :, 3:4], ALU.add))
            lk.do(dve.tensor_reduce(gs, p6, X, ALU.max))

            def first_max(v, n, rank_row, best, onehot):
                v3, o3 = T3(v, n), T3(onehot, n)
                lk.do(dve.tensor_reduce(best, v3, X, ALU.max))
                lk.do(dve.tensor_tensor(o3, v3, be(best, n), ALU.is_ge))
                lk.do(dve.tensor_tensor(o3, o3, bt(rank_row, n), ALU.mult))
                lk.do(dve.tensor_reduce(best, o3, X, ALU.max))
                lk.do(dve.tensor_tensor(o3, o3, be(best, n), ALU.is_equal))

            first_max(gs, NG, grank, m1, gsel)
            lk.do(dve.tensor_scalar(gk, gsel, 1.0, -NEG, ALU.subtract, ALU.mult))
            lk.do(dve.tensor_tensor(selm.rearrange("p (n e) -> p n e", e=EPG), s4,
                                    gk.unsqueeze(2).to_broadcast([P, TILES * NG, EPG]), ALU.add))
            first_max(selm, NE, rank, m1, oh1)
            lk.do(dve.scalar_tensor_tensor(out=selm, in0=oh1, scalar=2.0 * NEG, in1=selm, op0=ALU.mult, op1=ALU.add))
            first_max(selm, NE, rank, m1, oh2)
            lk.do(dve.tensor_tensor(mask, oh1, oh2, ALU.add))
            dve.drain().then_inc(s["mask"], 1)
            for c, oh in enumerate((oh1, oh2)):
                lk.do(dve.tensor_tensor(tmp, sig, oh, ALU.mult))
                lk.do(dve.tensor_reduce(gates[:, c, :], T3(tmp, NE), X, ALU.add))
            lk.do(dve.tensor_tensor(m1, gates[:, 0, :], gates[:, 1, :], ALU.add))
            lk.do(dve.reciprocal(m1, m1))
            lk.do(dve.tensor_tensor(gates[:, :, :], gates[:, :, :], m1.unsqueeze(1).to_broadcast([P, 2, TILES]), ALU.mult))
            dve.wait_ge(s["pos"], l + 1)
            cnt, nt_, end, st = rt[:, 2144:2160], rt[:, 2160:2176], rt[:, 2176:2192], rt[:, 2192:2208]
            lk.do(dve.tensor_copy(cnt, bank[2][:, 0:NE]))
            lk.do(dve.tensor_scalar(nt_, cnt, 0.0, None, ALU.is_gt))
            lk.do(dve.memset(nt_[:, 0:1], 1.0))
            for j in range(1, TILES):
                lk.do(dve.scalar_tensor_tensor(out=nt_, in0=cnt, scalar=float(P * j), in1=nt_, op0=ALU.is_gt, op1=ALU.add))
            lk.do(dve.tensor_tensor_scan(end, ones[:, 0:NE], nt_, 0.0, ALU.mult, ALU.add))
            lk.do(dve.tensor_tensor(st, end, nt_, ALU.subtract))
            lk.do(dve.tensor_scalar(st, st, float(P), None, ALU.mult))
            lk.do(dve.tensor_copy(dst[:, 0:NT * NE], bank[1][:, 0:NT * NE]))
            lk.do(dve.memset(dst[:, NT * NE:TILES * NE], 0.0))
            lk.do(dve.tensor_copy(dst[0:DEC, NT * NE:TILES * NE], bank[1][0:DEC, NT * NE:TILES * NE]))
            lk.do(dve.tensor_tensor(T3(dst, NE), T3(dst, NE), bt(st, NE), ALU.add))
            for c, oh in enumerate((oh1, oh2)):
                lk.do(dve.tensor_tensor(tmp, dst, oh, ALU.mult))
                lk.do(dve.tensor_reduce(m1, T3(tmp, NE), X, ALU.add))
                lk.do(dve.tensor_copy(ids[:, c, :], m1))
            grid = rt[0:1, 2560:2560 + MAX_ITEMS * NE].rearrange("p (n e) -> p n e", e=NE)
            lk.do(dve.tensor_tensor(grid, item[0:1, :].unsqueeze(2).to_broadcast([1, MAX_ITEMS, NE]),
                                    end[0:1, :].unsqueeze(1).to_broadcast([1, MAX_ITEMS, NE]), ALU.is_ge))
            ie = rt[0:1, 2304:2304 + MAX_ITEMS]
            lk.do(dve.tensor_reduce(ie, grid, X, ALU.add))
            lk.do(dve.tensor_scalar(ie, ie, float(NE - 1), None, ALU.min))
            lk.do(dve.tensor_copy(item_expert[:, :], ie))
            lk.do(dve.tensor_copy(n_items[:, 0:1], end[0:1, NE - 1:NE]))
            lk.do(dve.tensor_scalar(n_items[:, 1:2], end[0:1, NE - 1:NE], 1.0, None, ALU.subtract))
            rt_self[0] += lk.n
            dve.drain().then_inc(s["done"], 1)
            phase_end("dve", dve)

        MO = [sems(f"mo{l}", "wg", "wu", "wd", "x", "tx", "tx_a", "tx_v", "g", "u", "sg", "a", "at", "at_ev", "d", "ev_a", "ev_v", "y")
              for l in range(2)]
        m_x = arena[:, 5120:6144]
        m_xT = arena[:, 6144:7168].rearrange("p (k c) -> p k c", k=KD)
        m_sg = arena[:, 7168:7680]
        m_a = arena[:, 7680:8192]
        m_aT = arena[:, 8192:8704].rearrange("p (k c) -> p k c", k=KE)
        m_y = arena[:, 8704:9728]

        def items(eng):
            return eng.value_load(n_items[0:1, 0:1], min_val=9, max_val=MAX_ITEMS)

        def last_item(eng):
            return eng.value_load(n_items[0:1, 1:2], min_val=8, max_val=MAX_ITEMS - 1)

        def moe_sync(sp, l):
            s = MO[l]
            slabs = {"wg": (0, a["w_gate"][l], KD), "wu": (1, a["w_up"][l], KD), "wd": (2, a["w_down"][l], KE)}

            def load(n, e):
                slot, w, k = slabs[n]
                sp.dma_start(ring[:, slot, :], w[bass.ds(e, 1), :, :].rearrange("a (p k) c -> p (a k c)", k=k)).then_inc(s[n], 16)

            sp.wait_ge(g["phase"], PH[f"out{l}"])
            for n in ("wg", "wu", "wd"):
                load(n, 0)
            sp.wait_ge(g["phase"], PH[f"route{l}"])
            sp.dma_start(m_x, slot_rows[0:P, :]).then_inc(s["x"], 16)
            sp.sem_inc(s["y"], 16)
            n_it = items(sp)

            def store(n):
                sp.wait_ge(s["ev_a"], n)
                sp.wait_ge(s["ev_v"], n)
                sp.dma_start(slot_rows[bass.ds((n - 1) * P, P), :], m_y).then_inc(s["y"], 16)

            with sp.Fori(1, n_it) as n:
                e = sp.value_load(item_expert[0:1, bass.ds(n, 1)], min_val=0, max_val=NE - 1)
                sp.wait_ge(s["tx"], 2 * n)
                sp.dma_start(m_x, slot_rows[bass.ds(n * P, P), :]).then_inc(s["x"], 16)
                sp.wait_ge(s["g"], n)
                load("wg", e)
                sp.wait_ge(s["u"], n)
                load("wu", e)
                sp.wait_ge(s["d"], 2 * n)
                load("wd", e)
                store(n)
            store(n_it)
            sp.wait_ge(s["y"], 16 * n_it + 16)
            sp.sem_inc(s["ev_a"], 1)

        def moe_pe(pe, l):
            s = MO[l]
            n_last = last_item(pe)

            def transposes(n):
                pe.wait_ge(s["x"], 16 * n + 16)
                xk = m_x.rearrange("p (j k) -> p k j", k=KD)
                for half in range(2):
                    for k in range(4):
                        last = nc.tensor.transpose(bank[half][:, P * k:P * k + P], xk[:, 4 * half + k, :], ident[:, :])
                    last.then_inc(s["tx"], 1)

            def gate_up(n):
                pe.wait_ge(s["tx_a"], n + 1)
                pe.wait_ge(s["tx_v"], n + 1)
                for w, b, slot in (("wg", 2, 0), ("wu", 3, 1)):
                    pe.wait_ge(s[w], 16 * n + 16)
                    wt = ring[:, slot, :].rearrange("p (k c) -> p k c", k=KD)
                    for k in range(KD):
                        last = nc.tensor.matmul(bank[b][:, :], m_xT[:, k, :], wt[:, k, :], start=k == 0, stop=k == KD - 1)
                    last.then_inc(s["g" if w == "wg" else "u"], 1)

            def down(n):
                pe.wait_ge(s["a"], n + 1)
                ak = m_a.rearrange("p (j k) -> p k j", k=KE)
                for k in range(KE):
                    last = nc.tensor.transpose(bank[6][:, P * k:P * k + P], ak[:, k, :], ident[:, :])
                last.then_inc(s["at"], 1)
                pe.wait_ge(s["at_ev"], n + 1)
                pe.wait_ge(s["wd"], 16 * n + 16)
                wt = ring[:, 2, :].rearrange("p (k c) -> p k c", k=KE)
                for h in range(2):
                    for k in range(KE):
                        last = nc.tensor.matmul(bank[4 + h][:, :], m_aT[:, k, :], wt[:, k, CB * h:CB * h + CB],
                                                start=k == 0, stop=k == KE - 1)
                    last.then_inc(s["d"], 1)

            transposes(0)
            with pe.Fori(0, n_last) as n:
                gate_up(n)
                transposes(n + 1)
                down(n)
            gate_up(n_last)
            down(n_last)
            phase_end("pe", pe)

        def moe_act(act, l):
            s = MO[l]
            act.preload_act_table(ACT.Silu)
            n_last = last_item(act)

            def x_half(n):
                act.wait_ge(s["tx"], 2 * n + 1)
                act.activation(m_xT[:, 0:4, :], bank[0][:, :].rearrange("p (k c) -> p k c", k=4), ACT.Copy).then_inc(s["tx_a"], 1)

            def silu(n):
                act.wait_ge(s["g"], n + 1)
                act.activation(m_sg, bank[2][:, :], ACT.Silu).then_inc(s["sg"], 1)

            def y_half(n):
                act.wait_ge(s["d"], 2 * n + 1)
                act.wait_ge(s["y"], 16 * n + 16)
                act.activation(m_y[:, 0:CB], bank[4][:, :], ACT.Copy).then_inc(s["ev_a"], 1)

            x_half(0)
            with act.Fori(0, n_last) as n:
                silu(n)
                act.wait_ge(s["u"], n + 1)
                x_half(n + 1)
                y_half(n)
            silu(n_last)
            y_half(n_last)
            phase_end("act", act)

        def moe_dve(dve, l):
            s = MO[l]
            n_last = last_item(dve)

            def x_half(n):
                dve.wait_ge(s["tx"], 2 * n + 2)
                dve.tensor_copy(m_xT[:, 4:8, :], bank[1][:, :].rearrange("p (k c) -> p k c", k=4)).then_inc(s["tx_v"], 1)

            def product(n):
                dve.wait_ge(s["u"], n + 1)
                dve.wait_ge(s["sg"], n + 1)
                dve.tensor_tensor(m_a, bank[3][:, :], m_sg, ALU.mult).then_inc(s["a"], 1)

            def turned(n):
                dve.wait_ge(s["at"], n + 1)
                dve.tensor_copy(m_aT[:, :, :], bank[6][:, :].rearrange("p (k c) -> p k c", k=KE)).then_inc(s["at_ev"], 1)

            def y_half(n):
                dve.wait_ge(s["d"], 2 * n + 2)
                dve.wait_ge(s["y"], 16 * n + 16)
                dve.tensor_copy(m_y[:, CB:D], bank[5][:, :]).then_inc(s["ev_v"], 1)

            x_half(0)
            with dve.Fori(0, n_last) as n:
                product(n)
                x_half(n + 1)
                turned(n)
                y_half(n)
            product(n_last)
            turned(n_last)
            y_half(n_last)
            phase_end("dve", dve)

        CO = sems("co", "y0", "y1", "self", "acc")
        c_y = arena[:, 0:8192].rearrange("p (u c d) -> p u c d", u=4, c=2)

        def combine_pool(pool, l):
            s = CO
            pool.wait_ge(MO[l]["ev_a"], items(pool) + 1)
            settle(pool)

            def gather(t):
                r = rows(t)
                for c in range(2):
                    pool.indirect_dma_start(c_y[0:r, t % 4, c, :], None, slot_rows,
                                            bass.IndirectOffsetOnAxis(ids[0:r, c, t:t + 1], 0)).then_inc(s[f"y{t % 2}"], 16)
            gather(0)
            gather(1)
            for t in range(TILES):
                r = rows(t)
                if t + 2 < TILES:
                    if t + 2 >= 4:
                        pool.wait_ge(s["acc"], 5 * l + t - 1)
                    pool.wait_ge(s[f"y{t % 2}"], (96, 64)[t % 2] * l + 32 * (t // 2 + 1))
                    gather(t + 2)
            phase_end("pool", pool)

        def combine_dve(dve, l):
            s = CO
            lk = Link(dve, s["self"], base=20 * l)
            for t in range(TILES):
                r = rows(t)
                y0, y1 = c_y[0:r, t % 4, 0, :], c_y[0:r, t % 4, 1, :]
                dve.wait_ge(s[f"y{t % 2}"], (96, 64)[t % 2] * l + 32 * (t // 2 + 1))
                lk.do(dve.tensor_scalar(y0, y0, gates[0:r, 0, t:t + 1], None, ALU.mult))
                lk.do(dve.scalar_tensor_tensor(out=y0, in0=y1, scalar=gates[0:r, 1, t:t + 1], in1=y0,
                                               op0=ALU.mult, op1=ALU.add))
                lk.do(dve.tensor_tensor(y0, y0, bc[0:r, G2, group(t), :], ALU.mult))
                lk.do(dve.tensor_tensor(x[0:r, t, :], x[0:r, t, :], y0, ALU.add))
                dve.drain().then_inc(s["acc"], 1)
            phase_end("dve", dve)

        FN = sems("fn", "norm", "square", "self", "rstd", "y")
        nf = arena[:, 10240:11264]

        def final_act(act):
            for t in range(TILES):
                if t >= 1:
                    act.wait_ge(FN["square"], t)
                act.activation(junk[0:rows(t), :], x[0:rows(t), t, :], ACT.Square,
                               accum_out=ss[0:rows(t), t:t + 1]).then_inc(FN["square"], 1)
            act.wait_ge(FN["square"], TILES)
            act.activation(rstd[:, 0:TILES], ss[:, 0:TILES], ACT.Ln, scale=1.0 / D, bias=eps[:, :]).then_inc(FN["self"], 1)
            act.wait_ge(FN["self"], 1)
            act.activation(rstd[:, 0:TILES], rstd[:, 0:TILES], ACT.Exp, scale=-0.5).then_inc(FN["rstd"], 1)
            phase_end("act", act)

        def final_dve(dve):
            dve.wait_ge(FN["rstd"], 1)
            dve.wait_ge(FN["norm"], 16)
            for t in range(TILES):
                r = rows(t)
                dve.scalar_tensor_tensor(out=h_rows[0:r, t, :], in0=x[0:r, t, :], scalar=rstd[0:r, t:t + 1],
                                         in1=nf[0:r, :], op0=ALU.mult, op1=ALU.mult).then_inc(FN["y"], 1)
            phase_end("dve", dve)

        def final_sync(sp):
            sp.wait_ge(g["phase"], PH["combine1"])
            sp.dma_start(nf, a["norm_final"].partition_broadcast(P)).then_inc(FN["norm"], 16)
            for t in range(TILES):
                sp.wait_ge(FN["y"], t + 1)
                dst = out["y_prompt"][0, P * t:P * t + P, :] if t < NT else out["y_sample"][0]
                sp.dma_start(dst, h_rows[0:rows(t), t, :]).then_inc(out_sems["y"], 16)
            sp.wait_ge(out_sems["y"], 16 * TILES)
            sp.wait_ge(out_sems["kv0"], 16 * 8)
            sp.wait_ge(out_sems["kv1"], 16 * 6)

        @block.sync
        def _(sp):
            setup_sync(sp)
            for l in range(2):
                ada_sync(sp, l)
                proj_sync(sp, l)
                out_sync(sp, l)
                store_kv(sp, l)
                if l == 0:
                    diff_sync(sp)
                    sb_sync(sp)
                else:
                    fox_sync(sp)
                moe_sync(sp, l)
            final_sync(sp)

        @block.tensor
        def _(pe):
            phase_end("pe", pe)
            for l in range(2):
                ada_pe(pe, l)
                norm_pe(pe, f"norm_mix{l}")
                proj_pe(pe, l)
                if l == 0:
                    phase_end("pe", pe)
                    diff_pe(pe)
                    sb_pe(pe)
                else:
                    forget_pe(pe)
                    fox_pe(pe)
                out_pe(pe, l)
                norm_pe(pe, f"norm_ffn{l}")
                route_pe(pe, l)
                moe_pe(pe, l)
                phase_end("pe", pe)
            phase_end("pe", pe)

        @block.scalar
        def _(act):
            setup_act(act)
            for l in range(2):
                ada_act(act, l)
                norm_act(act, f"norm_mix{l}")
                proj_act(act, l)
                if l == 0:
                    act.activation(lam[:, 0:2], lam[:, 0:2], ACT.Exp).then_inc(ROPE["lam"], 1)
                    phase_end("act", act)
                    diff_act(act)
                    sb_act(act)
                else:
                    forget_act(act)
                    fox_act(act)
                phase_end("act", act)
                norm_act(act, f"norm_ffn{l}")
                route_act(act, l)
                moe_act(act, l)
                phase_end("act", act)
            final_act(act)

        @block.vector
        def _(dve):
            setup_dve(dve)
            for l in range(2):
                ada_dve(dve, l)
                norm_dve(dve, f"norm_mix{l}")
                proj_dve(dve, l)
                if l == 0:
                    rope_dve(dve)
                    diff_dve(dve)
                    sb_dve(dve)
                else:
                    forget_dve(dve)
                    fox_dve(dve)
                out_dve(dve, l)
                norm_dve(dve, f"norm_ffn{l}")
                route_dve(dve, l)
                moe_dve(dve, l)
                combine_dve(dve, l)
            final_dve(dve)

        @block.gpsimd
        def _(pool):
            setup_pool(pool)
            for l in range(2):
                phase_end("pool", pool)
                norm_pool(pool, f"norm_mix{l}")
                phase_end("pool", pool)
                if l == 0:
                    phase_end("pool", pool)
                    diff_pool(pool)
                    sb_pool(pool)
                else:
                    forget_pool(pool)
                    fox_pool(pool)
                out_pool(pool, l)
                norm_pool(pool, f"norm_ffn{l}")
                route_pool(pool, l)
                phase_end("pool", pool)
                combine_pool(pool, l)
            phase_end("pool", pool)


_INS = ["x_prompt", "x_sample", "c_prompt", "c_sample", "cache_diff_k", "cache_diff_v", "cache_sb_k", "cache_sb_v",
        "cache_fox_k", "cache_fox_v", "cache_fox_logf", "w_ada", "b_ada", "norm_mix", "norm_ffn", "w_in_even",
        "w_out_even", "diff_lq1", "diff_lk1", "diff_lq2", "diff_lk2", "diff_subln", "w_in_odd", "b_forget",
        "w_out_odd", "w_router", "b_router", "w_gate", "w_up", "w_down", "norm_final"]


def _outs():
    o = [("y_prompt", (1, SEQ, D)), ("y_sample", (1, DEC, D))]
    for tag, n in (("_p", SEQ), ("_s", DEC)):
        o += [("diff_k" + tag, (1, 1, n, N_DIFF, 2 * HD)), ("diff_v" + tag, (1, 1, n, N_DIFF, 2 * HD)),
              ("sb_k" + tag, (1, 1, n, N_SB, HD)), ("sb_v" + tag, (1, 1, n, N_SB, HD)),
              ("fox_k" + tag, (1, 1, n, N_FOX, HD)), ("fox_v" + tag, (1, 1, n, N_FOX, HD)),
              ("fox_logf" + tag, (1, 1, n, N_FOX))]
    return o


def _rope_table():
    pos = np.concatenate([np.arange(SEQ), PAST + np.arange(DEC)]).astype(np.float32)
    half = HD // 4 // 2
    inv = np.float32(500000.0) ** (-np.arange(half, dtype=np.float32) / np.float32(half))
    ang = pos[:, None] * inv[None, :].astype(np.float32)
    return np.concatenate([np.cos(ang), np.sin(ang)], axis=1).astype(np.float32)


def kernel(**inputs):
    import concourse.bacc as _bacc
    from concourse.bass_utils import run_bass_kernel_spmd as _run

    nc = _bacc.Bacc("TRN2", target_bir_lowering=False, num_devices=1)
    arrays, args = {}, {}
    for name in _INS:
        v = np.ascontiguousarray(inputs[name])
        arrays[f"in_{name}"] = v
        args[name] = nc.dram_tensor(f"in_{name}", v.shape, mybir.dt.from_np(v.dtype), kind="ExternalInput").ap()
    table = _rope_table()
    arrays["rope_table"] = table
    rope_dram = nc.dram_tensor("rope_table", table.shape, F32, kind="ExternalInput").ap()
    outs = {}
    for name, shape in _outs():
        outs[name] = nc.dram_tensor(f"out_{name}", shape, F32, kind="ExternalOutput").ap()
    encoder_step(nc, args, outs, rope_dram)
    r = _run(nc, [arrays], core_ids=[0])
    return tuple(r.results[0][f"out_{name}"] for name, _ in _outs())
```

```python
from contextlib import ExitStack

import numpy as np

import concourse.bass as bass
from concourse import mybir

F32 = mybir.dt.float32
F32R = mybir.dt.float32r
BF16 = mybir.dt.bfloat16
I32 = mybir.dt.int32
ALU = mybir.AluOpType
ACT = mybir.ActivationFunctionType
X = mybir.AxisListType.X

P = 128
D = 1024
KD = D // P
SEQ, DEC, PAST = 512, 32, 256
NT = SEQ // P
TILES = NT + 1
TOK = SEQ + DEC
HD = 64
N_DIFF, N_SB, N_FOX = D // 256, D // 128, D // HD
QKV = 3 * D
CB = 512
NE, NG, EPG = 16, 4, 4
DE = D // 2
KE = DE // P
EPS = 1e-6
NEG = -1e30
LAM_INIT = 0.8 - 0.6
MAX_ITEMS = (2 * TOK + NE * (P - 1)) // P + 1
SLOTS = MAX_ITEMS * P
HT_LEN = KD * TOK + P - DEC


def rows(t):
    return P if t < NT else DEC


def group(t):
    return 0 if t < NT else 1


def cols(t):
    return slice(P * t, P * t + rows(t))


class Link:

    def __init__(self, eng, sem, base=0):
        self.eng, self.sem, self.base, self.n = eng, sem, base, 0

    def step(self, ins):
        ins.then_inc(self.sem, 1)
        self.n += 1

    def wait(self):
        self.eng.wait_ge(self.sem, self.base + self.n)

    def do(self, ins):
        self.step(ins)
        self.wait()


def encoder_step(nc, a, out, rope_dram):
    ctx = ExitStack()
    with ctx:
        def sb(name, shape, dt=F32):
            return ctx.enter_context(nc.sbuf_tensor(name, shape, dt))

        def sems(prefix, *names):
            return {n: ctx.enter_context(nc.semaphore(f"{prefix}_{n}")) for n in names}

        rounded = {}

        def sb_both(name, shape):
            at = -(-nc.sbuf_base // 32) * 32
            t = sb(name, shape)
            rounded[t.name] = nc.alloc_sbuf_tensor_at(name + "_r", shape, F32R, offset=at)
            return t

        def r32(ap):
            return bass.AP(tensor=rounded[ap.tensor.name], offset=ap.offset, ap=ap.ap)

        def f32(ap):
            return r32(ap).bitcast(F32)

        slot_rows = nc.dram_tensor("slot_rows", (SLOTS, D), F32, kind="Internal").ap()

        mod_rows = nc.dram_tensor("mod_rows", (2, 2, 6 * D), F32, kind="Internal").ap()

        x = sb("x", [P, TILES, D])
        hT_flat = sb_both("hT", [P, HT_LEN])
        arena = sb_both("arena", [P, TILES * QKV])
        ring = sb_both("ring", [P, 3, KD * CB])
        bc = sb("bc", [P, 4, 2, D])
        work = sb_both("work", [P, 4608])
        G1, A2, B2, G2 = range(4)

        ident = sb("ident", [P, P])
        ident_b = sb("ident_b", [P, P], BF16)
        causal_b = sb("causal_b", [P, P], BF16)
        chunk_b = sb("chunk_b", [P, P], BF16)
        strict_b = sb("strict_b", [P, P], BF16)
        ones = sb("ones", [P, P])
        neg_ones = sb("neg_ones", [P, P])
        upto = sb("upto", [P, P])
        before = sb("before", [P, P])
        neg_from = sb("neg_from", [P, P])
        pick = sb("pick", [P, 32])
        ada_row = sb("ada_row", [2, CB])
        eps = sb("eps", [P, 1])
        silu_c = sb("silu_c", [P, KD, 32])
        c_in = sb("c_in", [P, 2, KD])
        ss = sb("ss", [P, 8])
        rstd = sb("rstd", [P, 8])
        rope = sb("rope", [P, TILES, 2, 8])
        lamv = work[:, 0:4 * HD].rearrange("p (n d) -> p n d", d=HD)
        lam = sb("lam", [P, 8])
        subg = sb("subg", [P, 1])
        wr = sb("wr", [P, KD, NE])
        br = sb("br", [P, NE])
        wf = sb_both("wf", [P, 2, 256])
        bfb = sb("bfb", [P, N_FOX])
        logf = sb("logf", [P, 7, N_FOX])
        dcum = sb("dcum", [P, 7, N_FOX])
        ndcum = sb("ndcum", [P, 7, N_FOX])
        small = sb("small", [P, 64])
        ids = sb("ids", [P, 2, TILES], I32)
        item_expert = sb("item_expert", [1, MAX_ITEMS], I32)
        n_items = sb("n_items", [1, 4], I32)
        total = sb("total", [1, 1])
        gates = sb("gates", [P, 2, TILES])
        bank = [ctx.enter_context(nc.psum_tensor(f"bank{i}", [P, 512], F32)) for i in range(8)]

        hT = hT_flat[:, 0:KD * TOK].rearrange("p (k c) -> p k c", k=KD)
        hT2_flat = work[:, 0:HT_LEN]
        hT2 = hT2_flat[:, 0:KD * TOK].rearrange("p (k c) -> p k c", k=KD)
        qkv = arena[:, :].rearrange("p (t c) -> p t c", c=QKV)
        w1 = ring[:, 2, :]

        g = sems("g", "settled", "phase", "const", "load_x", "load_small", "load_rope", "zero_rows", "zeroed", "setup")
        out_sems = sems("out", "kv0", "kv1", "y")

        phase_no = {"pe": 0, "act": 0, "dve": 0, "pool": 0}

        def phase_end(name, eng):
            phase_no[name] += 1
            eng.drain()
            eng.sem_inc(g["phase"], 1)
            eng.wait_ge(g["phase"], 4 * phase_no[name])

        def settle(eng):
            eng.sem_inc(g["settled"], 1)

        block = ctx.enter_context(nc.Block())

        PH = {}
        order = ["setup"]
        for l in range(2):
            order += ([f"ada{l}"] if l == 0 else []) + [f"norm_mix{l}", f"proj{l}"]
            order += ["rope", "diff", "sb"] if l == 0 else ["forget", "fox"]
            order += [f"out{l}", f"norm_ffn{l}", f"route{l}", f"moe{l}", f"combine{l}"]
        order += ["final"]
        for i, n in enumerate(order):
            PH[n] = 4 * (i + 1)

        def setup_pool(pool):
            pool.memset(ident[:, :], 0.0)
            pool.memset(ident_b[:, :], 0.0)
            pool.memset(causal_b[:, :], 0.0)
            pool.memset(chunk_b[:, :], 0.0)
            pool.memset(strict_b[:, :], 0.0)
            pool.memset(ones[:, :], 1.0)
            pool.memset(neg_ones[:, :], -1.0)
            pool.memset(upto[:, :], 1.0)
            pool.memset(before[:, :], 1.0)
            pool.memset(neg_from[:, :], -1.0)
            pool.memset(pick[:, :], 0.0)
            pool.memset(eps[:, :], EPS)
            pool.memset(wf[:, 1, P:256], 0.0)
            pool.memset(silu_c[:, :, :], 0.0).then_inc(g["const"], 1)
            pool.wait_ge(g["const"], 1)
            pool.memset(chunk_b[0:64, 64:128], NEG)
            for m in (ident, ident_b):
                pool.affine_select(out=m[:, :], in_=m[:, :], compare_op=ALU.not_equal, fill=1.0, base=0,
                                   pattern=[[-1, P]], channel_multiplier=1)
            pool.affine_select(out=causal_b[:, :], in_=causal_b[:, :], compare_op=ALU.is_ge, fill=NEG, base=0,
                               pattern=[[-1, P]], channel_multiplier=1)
            pool.affine_select(out=strict_b[:, :], in_=strict_b[:, :], compare_op=ALU.is_ge, fill=NEG, base=-1,
                               pattern=[[1, P]], channel_multiplier=-1)
            pool.affine_select(out=upto[:, :], in_=upto[:, :], compare_op=ALU.is_ge, fill=0.0, base=0,
                               pattern=[[1, P]], channel_multiplier=-1)
            pool.affine_select(out=before[:, :], in_=before[:, :], compare_op=ALU.is_ge, fill=0.0, base=-1,
                               pattern=[[1, P]], channel_multiplier=-1)
            pool.affine_select(out=neg_from[:, :], in_=neg_from[:, :], compare_op=ALU.is_ge, fill=0.0, base=0,
                               pattern=[[-1, P]], channel_multiplier=1)
            for q in range(4):
                pool.drain()
                pool.affine_select(out=pick[:, 0:2], in_=pick[:, 0:2], compare_op=ALU.not_equal,
                                   fill=1.0, base=-32 * q, pattern=[[-1, 2]], channel_multiplier=1)
            phase_end("pool", pool)

        def setup_act(act):
            act.wait_ge(g["load_small"], 16 * 11)
            act.wait_ge(g["const"], 1)
            act.activation(silu_c[:, :, 0:2], c_in[:, :, :].rearrange("p g k -> p k g"), ACT.Silu)
            act.activation(r32(wf[:, 0, :]), wf[:, 1, :], ACT.Copy).then_inc(g["const"], 1)
            phase_end("act", act)

        def setup_dve(dve):
            dve.memset(ring[:, 2, 0:D], 0.0).then_inc(g["zero_rows"], 1)
            dve.memset(ss[:, :], 1.0)
            dve.memset(total[:, :], 0.0)
            dve.wait_ge(g["load_small"], 16 * 11)
            lk = Link(dve, g["setup"])
            for i in range(2):
                lk.do(dve.tensor_tensor(lamv[:, 2 * i, :], lamv[:, 2 * i, :], lamv[:, 2 * i + 1, :], ALU.mult))
                lk.do(dve.reduce_sum(lam[:, i:i + 1], lamv[:, 2 * i, :], X))
            dve.tensor_scalar(subg[:, :], subg[:, :], 1.0 - LAM_INIT, None, ALU.mult)
            dve.wait_ge(g["const"], 2)
            dve.tensor_tensor(r32(wf[:, 1, :]), wf[:, 1, :], f32(wf[:, 0, :]), ALU.subtract)
            phase_end("dve", dve)

        def setup_sync(sp):
            small_loads = [
                (c_in[:, 0, :], a["c_prompt"].rearrange("a (p k) -> (a p) k", p=P)),
                (c_in[:, 1, :], a["c_sample"].rearrange("a (p k) -> (a p) k", p=P)),
                (lamv[:, 0, :], a["diff_lq1"][0, :].partition_broadcast(P)),
                (lamv[:, 1, :], a["diff_lk1"][0, :].partition_broadcast(P)),
                (lamv[:, 2, :], a["diff_lq2"][0, :].partition_broadcast(P)),
                (lamv[:, 3, :], a["diff_lk2"][0, :].partition_broadcast(P)),
                (subg[:, :], a["diff_subln"].rearrange("a (p k) -> (a p) k", p=P)),
                (wr[:, :, :], a["w_router"].rearrange("(k p) e -> p k e", p=P)),
                (br[:, :], a["b_router"].partition_broadcast(P)),
                (wf[:, 1, 0:P].rearrange("p (k e) -> p k e", e=N_FOX), a["w_in_odd"][0, :, QKV:QKV + N_FOX].rearrange("(k p) e -> p k e", p=P)),
                (bfb[:, :], a["b_forget"][0, :].partition_broadcast(P)),
            ]
            for dst, src in small_loads:
                sp.dma_start(dst, src).then_inc(g["load_small"], 16)
            sp.dma_start(x[:, 0:NT, :], a["x_prompt"][0].rearrange("(t p) d -> p t d", p=P)).then_inc(g["load_x"], 16)
            sp.dma_start(x[0:DEC, NT, :], a["x_sample"][0]).then_inc(g["load_x"], 16)
            sp.dma_start(rope[:, 0:NT, :, :].rearrange("p t a b -> p t (a b)"),
                         rope_dram[0:SEQ, :].rearrange("(t p) c -> p t c", p=P)).then_inc(g["load_rope"], 16)
            sp.dma_start(rope[0:DEC, NT, :, :].rearrange("p a b -> p (a b)"),
                         rope_dram[SEQ:TOK, :]).then_inc(g["load_rope"], 16)
            sp.dma_start(logf[:, 4:6, :], a["cache_fox_logf"][0, 0].rearrange("(t p) h -> p t h", p=P)).then_inc(g["load_rope"], 16)

        AD = sems("ada", "w0", "w1", "bias", "mv", "part", "sum", "row", "stored", "mix", "ffn", "out")
        ada_w = [ring[:, 0, 4 * CB * h:4 * CB * (h + 1)].rearrange("p (k c) -> p k c", k=4) for h in range(2)]
        mod1 = arena[:, 10240:14336].rearrange("p (v g c) -> p v g c", v=2, g=2)
        normg = arena[:, 9216:10240]

        def ada_part(l):
            return ring[:, 2, 3584:4096] if l == 0 else work[:, 4096:4608]

        def ada_load(sp, l, c, b):
            for h in range(2):
                if not (isinstance(c, int) and c == 0):
                    sp.wait_ge(AD["mv"], 2 * c + h - 1)
                sp.dma_start(ada_w[h], a["w_ada"][l, :, bass.ds(b * CB, CB)].rearrange("(p k) c -> p k c", k=KD)[:, 4 * h:4 * h + 4, :]
                             ).then_inc(AD[f"w{h}"], 16)

        def ada_bias(sp, l, c, b):
            if not (isinstance(c, int) and c == 0):
                sp.wait_ge(AD["stored"], 16 * c)
            sp.dma_start(ada_row[:, :], a["b_ada"][l, bass.ds(b * CB, CB)].partition_broadcast(2)).then_inc(AD["bias"], 16)

        def ada_store_before(sp, l, c, b):
            sp.wait_ge(AD["row"], c)
            sp.dma_start(mod_rows[l, :, bass.ds((b - 1) * CB, CB)], ada_row[:, :]).then_inc(AD["stored"], 16)

        def ada_matvec(pe, c, acc):
            for h in range(2):
                pe.wait_ge(AD[f"w{h}"], 16 * c + 16)
                for q in range(4):
                    last = nc.tensor.matmul(acc[32 * q:32 * q + 32, :], silu_c[:, 4 * h + q, :], ada_w[h][:, q, :],
                                            start=h == 0, stop=h == 1)
                last.then_inc(AD["mv"], 1)

        def ada_sum(pe, c, acc, l=0):
            pe.wait_ge(AD["part"], c + 1)
            nc.tensor.matmul(acc[0:32, :], pick[:, :], ada_part(l), start=True, stop=True).then_inc(AD["sum"], 1)

        def ada_copy(act, c, acc, l=0):
            act.wait_ge(AD["mv"], 2 * c + 2)
            act.wait_ge(AD["sum"], c)
            act.activation(ada_part(l), acc[:, :], ACT.Copy).then_inc(AD["part"], 1)

        def ada_add(dve, c, acc):
            dve.wait_ge(AD["sum"], c + 1)
            dve.wait_ge(AD["bias"], 16 * c + 16)
            dve.tensor_tensor(ada_row[:, :], ada_row[:, :], acc[0:2, :], ALU.add).then_inc(AD["row"], 1)

        def mod_load(sp, l, v, dst, sem):
            for grp in range(2):
                n = (P, DEC)[grp]
                sp.dma_start(dst[0:n, grp, :], mod_rows[l, grp, D * v:D * v + D].partition_broadcast(n)).then_inc(AD[sem], 16)

        def ada_sync(sp):
            for c in range(4):
                ada_load(sp, 0, c, c)
                if c >= 1:
                    ada_store_before(sp, 0, c, c)
                ada_bias(sp, 0, c, c)
            ada_store_before(sp, 0, 4, 4)
            sp.wait_ge(AD["stored"], 64)
            mix_load(sp, 0)

        def mix_load(sp, l):
            mod_load(sp, l, 0, mod1[:, 0], "mix")
            mod_load(sp, l, 1, mod1[:, 1], "mix")
            sp.dma_start(normg, a["norm_mix"][l, :].partition_broadcast(P)).then_inc(AD["mix"], 16)

        def out_load(sp, l):
            mod_load(sp, l, 2, bc[:, G1], "out")
            mod_load(sp, l, 3, bc[:, B2], "ffn")
            mod_load(sp, l, 4, bc[:, A2], "ffn")
            sp.dma_start(normg, a["norm_ffn"][l, :].partition_broadcast(P)).then_inc(AD["ffn"], 16)
            mod_load(sp, l, 5, bc[:, G2], "ffn")

        def ada_pe(pe):
            ada_matvec(pe, 0, bank[0])
            for c in range(1, 4):
                ada_matvec(pe, c, bank[c % 2])
                ada_sum(pe, c - 1, bank[(c - 1) % 2])
                pe.wait_ge(AD["row"], c)
            ada_sum(pe, 3, bank[1])
            phase_end("pe", pe)

        def ada_act(act):
            for c in range(4):
                ada_copy(act, c, bank[c % 2])
            phase_end("act", act)

        def ada_dve(dve):
            for c in range(4):
                ada_add(dve, c, bank[c % 2])
            phase_end("dve", dve)

        h_rows = arena[:, 0:TILES * D].rearrange("p (t d) -> p t d", d=D)
        junk = arena[:, 14336:15360]
        NORM = sems("norm", "square", "rstd", "scaled", "shifted", "tr", "ev_a", "ev_v", "self", "gain")
        NORM_NO = {"norm_mix0": 0, "norm_ffn0": 1, "norm_mix1": 2, "norm_ffn1": 3}

        def scale_shift(name, t):
            r, grp = rows(t), group(t)
            if name.startswith("norm_mix"):
                return mod1[0:r, 1, grp, :], mod1[0:r, 0, grp, :]
            return bc[0:r, A2, grp, :], bc[0:r, B2, grp, :]

        def part_of(dst, u):
            return dst[:, 4 * (u % 2):4 * (u % 2) + 4, cols(u // 2)]

        def bank_of(u):
            return bank[u % 8][:, :].rearrange("p (k c) -> p k c", k=4)[:, :, 0:rows(u // 2)]

        EV_A, EV_V = (0, 10, 15, 25), (0, 10, 15, 25)

        def norm_act(act, name):
            s, o = NORM, NORM_NO[name]
            if name == "norm_mix0":
                act.wait_ge(g["load_x"], 32)
            for t in range(TILES):
                if t >= 1:
                    act.wait_ge(s["square"], TILES * o + t)
                act.activation(junk[0:rows(t), :], x[0:rows(t), t, :], ACT.Square,
                               accum_out=ss[0:rows(t), t:t + 1]).then_inc(s["square"], 1)
            act.wait_ge(s["square"], TILES * (o + 1))
            act.activation(rstd[:, 0:TILES], ss[:, 0:TILES], ACT.Ln, scale=1.0 / D, bias=eps[:, :]).then_inc(s["self"], 1)
            act.wait_ge(s["self"], o + 1)
            act.activation(rstd[:, 0:TILES], rstd[:, 0:TILES], ACT.Exp, scale=-0.5).then_inc(s["rstd"], 1)
            if name.startswith("norm_mix"):
                for u in range(2 * TILES):
                    act.wait_ge(s["tr"], 10 * o + u + 1)
                    act.activation(r32(part_of(hT, u)), bank_of(u), ACT.Copy).then_inc(s["ev_a"], 1)
            else:
                for t in range(TILES):
                    act.wait_ge(s["tr"], 10 * o + 2 * t + 1)
                    act.activation(part_of(hT, 2 * t), bank_of(2 * t), ACT.Copy).then_inc(s["ev_a"], 1)
            phase_end("act", act)

        def norm_dve(dve, name):
            s, o = NORM, NORM_NO[name]
            l = int(name[-1])
            if name.startswith("norm_mix"):
                dve.wait_ge(AD["mix"], 80 * (l + 1))
            else:
                dve.wait_ge(AD["ffn"], 112 * (l + 1))
            for grp in range(2):
                scale = scale_shift(name, NT * grp)[0]
                dve.scalar_tensor_tensor(out=scale, in0=scale, scalar=1.0, in1=normg[0:(P, DEC)[grp], :],
                                         op0=ALU.add, op1=ALU.mult).then_inc(s["gain"], 1)
            dve.wait_ge(s["gain"], 2 * o + 2)
            dve.wait_ge(s["rstd"], o + 1)
            for t in range(TILES):
                r = rows(t)
                dve.scalar_tensor_tensor(out=h_rows[0:r, t, :], in0=x[0:r, t, :], scalar=rstd[0:r, t:t + 1],
                                         in1=scale_shift(name, t)[0], op0=ALU.mult, op1=ALU.mult).then_inc(s["scaled"], 1)
                if t >= 1:
                    evac(dve, name, t - 1)
            evac(dve, name, TILES - 1)
            phase_end("dve", dve)

        def evac(dve, name, t):
            s, o = NORM, NORM_NO[name]
            if name.startswith("norm_mix"):
                for u in (2 * t, 2 * t + 1):
                    dve.wait_ge(s["ev_a"], EV_A[o] + u + 1)
                    dve.tensor_tensor(r32(part_of(hT2, u)), bank_of(u), f32(part_of(hT, u)), ALU.subtract).then_inc(s["ev_v"], 1)
            else:
                dve.wait_ge(s["tr"], 10 * o + 2 * t + 2)
                dve.tensor_copy(part_of(hT, 2 * t + 1), bank_of(2 * t + 1)).then_inc(s["ev_v"], 1)

        def norm_pool(pool, name):
            s, o = NORM, NORM_NO[name]
            if name.startswith("norm_mix"):
                for flat in (hT_flat, hT2_flat):
                    pool.tensor_copy(r32(flat[:, KD * TOK:HT_LEN]), ones[:, 0:P - DEC])
            for t in range(TILES):
                r = rows(t)
                pool.wait_ge(s["scaled"], 5 * o + t + 1)
                pool.tensor_tensor(h_rows[0:r, t, :], h_rows[0:r, t, :], scale_shift(name, t)[1],
                                   ALU.add).then_inc(s["shifted"], 1)
            phase_end("pool", pool)

        def norm_pe(pe, name):
            s, o = NORM, NORM_NO[name]
            for t in range(TILES):
                r = rows(t)
                pe.wait_ge(s["shifted"], 5 * o + t + 1)
                if t == 4:
                    both = 2 if name.startswith("norm_mix") else 1
                    pe.wait_ge(s["ev_a"], EV_A[o] + both)
                    pe.wait_ge(s["ev_v"], EV_V[o] + both)
                for half in range(2):
                    for k in range(4):
                        d0 = P * (4 * half + k)
                        last = nc.tensor.transpose(bank[(2 * t + half) % 8][:, P * k:P * k + r],
                                                   h_rows[0:r, t, d0:d0 + P], ident[0:r, 0:r])
                    last.then_inc(s["tr"], 1)
            phase_end("pe", pe)

        PROJ = sems("proj", "w0", "w1", "hi", "lo", "mm", "used", "ev_a", "ev_v")
        CH = KD // 2
        stage = [ring[:, 0, CH * CB * h:CH * CB * (h + 1)] for h in range(2)]
        high = [ring[:, 1, CH * CB * h:CH * CB * (h + 1)] for h in range(2)]
        chunk = lambda v: v.rearrange("p (k c) -> p k c", k=CH)

        def split_product(acc, rows_hi, rows_lo, w_hi, w_lo, first, last):
            nc.tensor.matmul(acc, rows_hi, w_hi, start=first, stop=False)
            nc.tensor.matmul(acc, rows_hi, w_lo, start=False, stop=False)
            return nc.tensor.matmul(acc, rows_lo, w_hi, start=False, stop=last)

        def tile_cols(flat, k, t):
            c = TOK * k + P * t
            return r32(flat[:, c:c + P])

        def proj_sync(sp, l):
            s, w = PROJ, a["w_in_even" if l == 0 else "w_in_odd"][0].rearrange("(h k p) c -> p h k c", p=P, h=2)

            def load(b, h):
                sp.dma_start(chunk(stage[h]), w[:, h, :, bass.ds(b * CB, CB)]).then_inc(s[f"w{h}"], 16)
            if l == 0:
                sp.wait_ge(AD["mv"], 8)
            else:
                sp.wait_ge(g["phase"], PH["moe0"])
            load(0, 0)
            load(0, 1)
            if l == 0:
                sp.wait_ge(g["zero_rows"], 1)
                sp.dma_start(slot_rows.rearrange("(n p) d -> p n d", p=P),
                             ring[:, 2, 0:D].unsqueeze(1).to_broadcast([P, MAX_ITEMS, D])).then_inc(g["zeroed"], 16)
            with sp.Fori(1, 6) as j:
                for h in range(2):
                    sp.wait_ge(s["used"], 2 * j + h - 1 + 12 * l)
                    load(j, h)

        def proj_pe(pe, l):
            s = PROJ
            with pe.Fori(0, 6) as j:
                for h in range(2):
                    pe.wait_ge(s["lo"], 2 * j + h + 1 + 12 * l)
                    hi, lo = r32(chunk(high[h])), r32(chunk(stage[h]))
                    for k in range(CH):
                        kk = CH * h + k
                        for t in range(TILES):
                            if kk == 0:
                                if t % 2 == 0:
                                    pe.wait_ge(s["ev_a"], 3 * j + t // 2 + 1 + 21 * l)
                                else:
                                    pe.wait_ge(s["ev_v"], 2 * j + t // 2 + 1 + 14 * l)
                            last = split_product(bank[t][:, :], tile_cols(hT_flat, kk, t), tile_cols(hT2_flat, kk, t),
                                                 hi[:, k, :], lo[:, k, :], kk == 0, kk == KD - 1)
                            if kk == KD - 1:
                                last.then_inc(s["mm"], 1)
                    nc.tensor.drain().then_inc(s["used"], 1)
            if l == 1:
                for k in range(KD):
                    w_hi, w_lo = (r32(wf[:, i, N_FOX * k:N_FOX * k + P]) for i in range(2))
                    for acc, c0, c1 in ((bank[5], 0, SEQ), (bank[6], SEQ, TOK)):
                        r_hi, r_lo = r32(hT[:, k, c0:c1]), r32(hT2[:, k, c0:c1])
                        n = c1 - c0
                        split_product(acc[:, 0:n], w_hi, w_lo, r_hi, r_lo, k == 0, k == KD - 1)
            phase_end("pe", pe)

        def proj_act(act, l):
            s = PROJ
            act.sem_inc(s["ev_a"], 3)

            def split(j, h):
                act.wait_ge(s[f"w{h}"], 16 * j + 16 + 96 * l)
                if not isinstance(j, int):
                    act.wait_ge(s["used"], 2 * j + h - 1 + 12 * l)
                act.activation(r32(high[h]), stage[h], ACT.Copy).then_inc(s["hi"], 1)

            def results(j):
                for t in (0, 2, 4):
                    act.wait_ge(s["mm"], 5 * j + t + 1 + 30 * l)
                    act.activation(qkv[0:rows(t), t, bass.ds(j * CB, CB)], bank[t][0:rows(t), :], ACT.Copy).then_inc(s["ev_a"], 1)

            split(0, 0)
            split(0, 1)
            with act.Fori(0, 5) as j:
                split(j + 1, 0)
                results(j)
                split(j + 1, 1)
            results(5)
            phase_end("act", act)

        def proj_dve(dve, l):
            s = PROJ
            dve.sem_inc(s["ev_v"], 2)

            def split(j, h):
                dve.wait_ge(s["hi"], 2 * j + h + 1 + 12 * l)
                dve.tensor_tensor(r32(stage[h]), stage[h], f32(high[h]), ALU.subtract).then_inc(s["lo"], 1)

            def results(j):
                for t in (1, 3):
                    dve.wait_ge(s["mm"], 5 * j + t + 1 + 30 * l)
                    dve.tensor_copy(qkv[0:rows(t), t, bass.ds(j * CB, CB)], bank[t][0:rows(t), :]).then_inc(s["ev_v"], 1)

            split(0, 0)
            split(0, 1)
            with dve.Fori(0, 5) as j:
                split(j + 1, 0)
                results(j)
                split(j + 1, 1)
            results(5)
            phase_end("dve", dve)

        ROPE = sems("rope", "self", "lam")

        def rope_dve(dve):
            dve.wait_ge(g["load_rope"], 48)
            lk = Link(dve, ROPE["self"])
            t1, t2, t3, t4 = (work[:, 512 * i:512 * i + 512] for i in range(4))
            for t0, nt, r in ((0, NT, P), (NT, 1, DEC)):
                n = nt * 64
                for blk in range(2):
                    v = qkv[0:r, t0:t0 + nt, CB * blk:CB * blk + CB].rearrange("p t (h d) -> p t h d", d=HD)
                    x1, x2 = v[:, :, :, 0:8], v[:, :, :, 8:16]
                    cos = rope[0:r, t0:t0 + nt, 0, :].unsqueeze(2).to_broadcast([r, nt, 8, 8])
                    sin = rope[0:r, t0:t0 + nt, 1, :].unsqueeze(2).to_broadcast([r, nt, 8, 8])

                    def tmp(b):
                        return b[0:r, 0:n].rearrange("p (t h d) -> p t h d", t=nt, d=8)
                    lk.step(dve.tensor_tensor(tmp(t1), x1, cos, ALU.mult))
                    lk.step(dve.tensor_tensor(tmp(t2), x2, sin, ALU.mult))
                    lk.step(dve.tensor_tensor(tmp(t3), x2, cos, ALU.mult))
                    lk.do(dve.tensor_tensor(tmp(t4), x1, sin, ALU.mult))
                    lk.step(dve.tensor_tensor(x1, tmp(t1), tmp(t2), ALU.subtract))
                    lk.do(dve.tensor_tensor(x2, tmp(t3), tmp(t4), ALU.add))
            dve.wait_ge(ROPE["lam"], 1)
            dve.tensor_scalar(lam[:, 2:3], lam[:, 1:2], lam[:, 0:1], -LAM_INIT, ALU.subtract, ALU.add)
            phase_end("dve", dve)

        def store_kv(sp, l):
            sp.wait_ge(g["phase"], PH["rope" if l == 0 else "forget"])
            s = out_sems[f"kv{l}"]
            if l == 0:
                parts = [("diff_k", 1 * CB, CB), ("diff_v", 2 * CB, CB), ("sb_k", 4 * CB, CB), ("sb_v", 5 * CB, CB)]
            else:
                parts = [("fox_k", D, D), ("fox_v", 2 * D, D)]
            for n, c0, w in parts:
                sp.dma_start(out[n + "_p"].rearrange("a b (t p) h d -> p (a b t) (h d)", p=P),
                             qkv[:, 0:NT, c0:c0 + w]).then_inc(s, 16)
                sp.dma_start(out[n + "_s"].rearrange("a b p h d -> (a b p) (h d)"),
                             qkv[0:DEC, NT, c0:c0 + w]).then_inc(s, 16)
            if l == 1:
                sp.dma_start(out["fox_logf_p"].rearrange("a b (t p) h -> p (a b t) h", p=P), logf[:, 0:NT, :]).then_inc(s, 16)
                sp.dma_start(out["fox_logf_s"].rearrange("a b p h -> (a b p) h"), logf[0:DEC, 6, :]).then_inc(s, 16)

        KP, KS, QS, QKT = 512, 1024, 1312, 1344
        DF = sems("df", "past_k", "past_v", "staged", "staged_v", "tr", "tr_ev", "s", "mx", "e", "sc", "w", "pt", "pt_ev",
                  "o", "sq", "on", "ot", "ot_ev", "self_v", "self_a", "v_free")
        df_q = work[:, 0:640].rearrange("p (t d) -> p t d", d=P)
        df_k = work[:, 640:1536].rearrange("p (t d) -> p t d", d=P)
        df_pv = work[:, 4096:4480].rearrange("p (t d) -> p t d", d=P)
        df_p = work[:, 1792:3840].rearrange("p (u c k) -> p u c k", u=2, c=2)
        df_on = work[:, 3840:4096].rearrange("p (u d) -> p u d", u=2)
        df_qk = w1[:, 0:QKT]
        df_pt = w1[:, QKT:QKT + 1024].rearrange("p (u k) -> p u k", u=2)

        def transpose_rows(out_bank, tiles, np_):
            c = 0
            for src, r in tiles:
                last = nc.tensor.transpose(out_bank[0:np_, c:c + r], src, ident[0:r, 0:r])
                c += r
            return last

        def nkeys(i):
            return P * (i + 1) if i < NT else PAST + DEC

        def key_tiles(i):
            return [(j, P, P * j) for j in range(i + 1)] if i < NT else [(4, P, 0), (5, P, P), (6, DEC, 2 * P)]

        def diff_sync(sp):
            sp.wait_ge(g["phase"], PH["rope"])
            ck = a["cache_diff_k"][0, 0].rearrange("(t p) h d -> p t (h d)", p=P)
            cv = a["cache_diff_v"][0, 0].rearrange("(t p) h d -> p t (h d)", p=P)
            def head(h, more):
                sp.wait_ge(DF["tr"], 3 * h + 1)
                sp.dma_start(df_k[:, 4:6, :], ck[:, :, bass.ds(h * P, P)]).then_inc(DF["past_k"], 16)
                sp.wait_ge(DF["v_free"], h + 1)
                sp.dma_start(df_pv[:, 0:2, :], cv[:, :, bass.ds(h * P, P)]).then_inc(DF["past_v"], 16)
                c = 2 * h + 4
                ada_load(sp, 0, c, c)
                if more:
                    ada_store_before(sp, 0, c, c)
                ada_bias(sp, 0, c, c)
                ada_load(sp, 0, c + 1, c + 1)
                ada_store_before(sp, 0, c + 1, c + 1)
                ada_bias(sp, 0, c + 1, c + 1)

            head(0, False)
            with sp.Fori(1, N_DIFF) as h:
                head(h, True)
            ada_store_before(sp, 0, 12, 12)

        def diff_pool(pool):
            with pool.Fori(0, N_DIFF) as h:
                pool.wait_ge(DF["tr"], 3 * h + 1)
                for dst, c0, t_new in ((df_q, 0, 4), (df_k, CB, 6)):
                    pool.tensor_copy(dst[:, 0:NT, :], qkv[:, 0:NT, bass.ds(h * P + c0, P)]).then_inc(DF["staged"], 1)
                    pool.tensor_copy(dst[0:DEC, t_new, :], qkv[0:DEC, NT, bass.ds(h * P + c0, P)]).then_inc(DF["staged"], 1)
                pool.wait_ge(DF["v_free"], h + 1)
                pool.tensor_copy(df_pv[0:DEC, 2, :], qkv[0:DEC, NT, bass.ds(h * P + 2 * CB, P)]).then_inc(DF["staged_v"], 1)
            phase_end("pool", pool)

        def diff_pe(pe):
            pe.sem_inc(DF["tr"], 1)
            pe.sem_inc(DF["v_free"], 1)
            with pe.Fori(0, N_DIFF) as h:
                pe.wait_ge(DF["staged"], 4 * h + 4)
                transpose_rows(bank[7], [(df_q[:, t, :], P) for t in range(NT)], P).then_inc(DF["tr"], 1)
                transpose_rows(bank[4], [(df_k[:, t, :], P) for t in range(NT)], P).then_inc(DF["tr"], 1)
                pe.wait_ge(DF["past_k"], 16 * h + 16)
                pe.wait_ge(DF["tr_ev"], 3 * h + 1)
                transpose_rows(bank[7], [(df_k[:, 4, :], P), (df_k[:, 5, :], P), (df_k[0:DEC, 6, :], DEC),
                                         (df_q[0:DEC, 4, :], DEC)], P).then_inc(DF["tr"], 1)
                pe.wait_ge(DF["tr_ev"], 3 * h + 3)

                def scores(i):
                    if i >= 2:
                        pe.wait_ge(DF["e"], 10 * h + 2 * (i - 2) + 2)
                    if i == NT:
                        settle(pe)
                    r = rows(i)
                    q0, k0 = (P * i, KP) if i < NT else (QS, KS)
                    for c in range(2):
                        b = bank[2 * (i % 2) + c]
                        half = slice(HD * c, HD * c + HD)
                        last = nc.tensor.matmul(b[0:r, 0:nkeys(i)], df_qk[half, q0:q0 + r],
                                                df_qk[half, k0:k0 + nkeys(i)], start=True, stop=i == NT)
                        if i < NT:
                            last = nc.tensor.matmul(b[:, P * i:P * i + P], ident_b[:, :], chunk_b[:, :],
                                                    start=False, stop=True)
                        last.then_inc(DF["s"], 1)

                def turn(i):
                    pe.wait_ge(DF["w"], 5 * h + i + 1)
                    if i >= 1:
                        pe.wait_ge(DF["pt_ev"], 5 * h + i)
                    if i == NT:
                        settle(pe)
                    r = rows(i)
                    for n, (j, kr, c) in enumerate(key_tiles(i)):
                        last = nc.tensor.transpose(bank[4][0:kr, r * n:r * n + r], df_p[0:r, i % 2, 0, c:c + kr],
                                                   ident[0:r, 0:r])
                    last.then_inc(DF["pt"], 1)

                def values(i):
                    pe.wait_ge(DF["pt_ev"], 5 * h + i + 1)
                    if i >= 1:
                        pe.wait_ge(DF["on"], 5 * h + i)
                    if i == NT:
                        pe.wait_ge(DF["past_v"], 16 * h + 16)
                        pe.wait_ge(DF["staged_v"], h + 1)
                        settle(pe)
                    r = rows(i)
                    tiles = key_tiles(i)
                    for n, (j, kr, c) in enumerate(tiles):
                        if j < NT:
                            v = qkv[:, j, bass.ds(h * P + 2 * CB, P)]
                        else:
                            v = df_pv[0:kr, j - 4, :]
                        last = nc.tensor.matmul(bank[5][0:r, 0:P], df_pt[0:kr, i % 2, r * n:r * n + r], v,
                                                start=n == 0, stop=n == len(tiles) - 1)
                    last.then_inc(DF["o"], 1)

                def back(i):
                    pe.wait_ge(DF["on"], 5 * h + i + 1)
                    if i >= 1:
                        pe.wait_ge(DF["ot_ev"], 5 * h + i)
                    if i == NT:
                        settle(pe)
                    r = rows(i)
                    nc.tensor.transpose(bank[6][:, 0:r], df_on[0:r, i % 2, :], ident[0:r, 0:r]).then_inc(DF["ot"], 1)

                scores(0)
                for i in range(TILES):
                    if i + 1 < TILES:
                        scores(i + 1)
                    turn(i)
                    if i >= 1:
                        back(i - 1)
                    values(i)
                    if i == 0:
                        ada_matvec(pe, 2 * h + 4, bank[7])
                    elif i == 1:
                        ada_sum(pe, 2 * h + 4, bank[7])
                    elif i == 2:
                        pe.wait_ge(AD["row"], 2 * h + 5)
                        ada_matvec(pe, 2 * h + 5, bank[7])
                    elif i == 3:
                        ada_sum(pe, 2 * h + 5, bank[7])
                pe.wait_ge(AD["row"], 2 * h + 6)
                back(TILES - 1)
                nc.tensor.drain().then_inc(DF["v_free"], 1)
            phase_end("pe", pe)

        def diff_act(act):
            act.preload_act_table_set("natural_log_exp_and_others")
            act.wait_ge(g["zeroed"], 16)
            with act.Fori(0, N_DIFF) as h:
                for n, (b, c0, w) in enumerate(((7, 0, 512), (4, KP, 512), (7, KS, 320))):
                    act.wait_ge(DF["tr"], 3 * h + n + 2)
                    act.activation(df_qk[:, c0:c0 + w], bank[b][:, 0:w], ACT.Copy).then_inc(DF["tr_ev"], 1)

                def probs(i):
                    r = rows(i)
                    if i >= 2:
                        act.wait_ge(DF["pt"], 5 * h + i - 1)
                    act.wait_ge(DF["mx"], 5 * h + i + 1)
                    for c in range(2):
                        act.activation(df_p[0:r, i % 2, c, 0:nkeys(i)], bank[2 * (i % 2) + c][0:r, 0:nkeys(i)], ACT.Exp,
                                       scale=HD ** -0.5, bias=small[0:r, 8 * (i % 2) + c:8 * (i % 2) + c + 1],
                                       accum_out=small[0:r, 8 * (i % 2) + 2 + c:8 * (i % 2) + 3 + c]).then_inc(DF["e"], 1)

                def turned(i):
                    r, n = rows(i), len(key_tiles(i))
                    act.wait_ge(DF["pt"], 5 * h + i + 1)
                    if i < NT:
                        act.activation(df_pt[:, i % 2, 0:r * n], bank[4][:, 0:r * n], ACT.Copy).then_inc(DF["pt_ev"], 1)
                    else:
                        act.activation(df_pt[:, i % 2, 0:2 * r], bank[4][:, 0:2 * r], ACT.Copy)
                        act.activation(df_pt[0:DEC, i % 2, 2 * r:3 * r], bank[4][0:DEC, 2 * r:3 * r],
                                       ACT.Copy).then_inc(DF["pt_ev"], 1)

                def norm(i):
                    r = rows(i)
                    act.wait_ge(DF["o"], 5 * h + i + 1)
                    z = small[0:r, 32:33]
                    lk = Link(act, DF["self_a"], base=15 * h + 3 * i)
                    lk.do(act.activation(df_on[0:r, i % 2, :], bank[5][0:r, 0:P], ACT.Square, accum_out=z))
                    lk.do(act.activation(z, z, ACT.Ln, scale=1.0 / P, bias=eps[0:r, :]))
                    lk.do(act.activation(z, z, ACT.Exp, scale=-0.5))
                    act.activation(df_on[0:r, i % 2, :], bank[5][0:r, 0:P], ACT.Copy, scale=z).then_inc(DF["on"], 1)

                def placed(i):
                    r = rows(i)
                    act.wait_ge(DF["ot"], 5 * h + i + 1)
                    act.activation(hT[:, bass.ds(h, 1), cols(i)].rearrange("p a c -> p (a c)"), bank[6][:, 0:r],
                                   ACT.Copy, scale=subg[:, :]).then_inc(DF["ot_ev"], 1)

                probs(0)
                for i in range(TILES):
                    if i + 1 < TILES:
                        probs(i + 1)
                    turned(i)
                    if i >= 1:
                        placed(i - 1)
                    norm(i)
                    if i in (0, 2):
                        ada_copy(act, 2 * h + 4 + i // 2, bank[7])
                placed(TILES - 1)
            phase_end("act", act)

        def diff_dve(dve):
            with dve.Fori(0, N_DIFF) as h:
                lk = Link(dve, DF["self_v"], base=15 * h)

                def maxima(i):
                    r, o = rows(i), 8 * (i % 2)
                    for c in range(2):
                        dve.wait_ge(DF["s"], 10 * h + 2 * i + c + 1)
                        ins = dve.reduce_max(small[0:r, o + 4 + c:o + 5 + c], bank[2 * (i % 2) + c][0:r, 0:nkeys(i)], X)
                    lk.do(ins)
                    dve.tensor_scalar(small[0:r, o:o + 2], small[0:r, o + 4:o + 6], -HD ** -0.5, None,
                                      ALU.mult).then_inc(DF["mx"], 1)

                def weights(i):
                    r, o, n = rows(i), 8 * (i % 2), nkeys(i)
                    dve.wait_ge(DF["e"], 10 * h + 2 * i + 2)
                    lk.do(dve.reciprocal(small[0:r, o + 6:o + 8], small[0:r, o + 2:o + 4]))
                    dve.tensor_scalar(small[0:r, o + 7:o + 8], small[0:r, o + 7:o + 8], lam[0:r, 2:3], None, ALU.mult)
                    lk.do(dve.tensor_scalar(df_p[0:r, i % 2, 0, 0:n], df_p[0:r, i % 2, 0, 0:n],
                                            small[0:r, o + 6:o + 7], None, ALU.mult))
                    dve.scalar_tensor_tensor(out=df_p[0:r, i % 2, 0, 0:n], in0=df_p[0:r, i % 2, 1, 0:n],
                                             scalar=small[0:r, o + 7:o + 8], in1=df_p[0:r, i % 2, 0, 0:n],
                                             op0=ALU.mult, op1=ALU.add).then_inc(DF["w"], 1)

                maxima(0)
                for i in range(TILES):
                    if i + 1 < TILES:
                        maxima(i + 1)
                    weights(i)
                    if i in (2, 4):
                        ada_add(dve, 2 * h + 4 + (i - 2) // 2, bank[7])
            phase_end("dve", dve)

        SB = sems("sb", "past_k", "past_v", "staged", "tr", "ev_a", "ev_v", "z", "abs", "self_a", "e", "sp", "tri", "r", "w",
                  "pv", "o", "v_free", "self_p")
        sb_q = work[:, 0:640].rearrange("p (t d) -> p t d", d=P)
        sb_k = work[:, 640:1536].rearrange("p (t d) -> p t d", d=P)
        sb_v = work[:, 1536:2432].rearrange("p (t d) -> p t d", d=P)
        sb_r = work[:, 2432:3520].rearrange("p (h c) -> p h c", h=2)
        sb_w = work[:, 3520:4608].rearrange("p (u c) -> p u c", u=2)
        sb_qT = w1[:, 0:TOK]
        sb_kT = w1[:, TOK:TOK + 7 * P]
        sb_e = w1[:, 1440:2464].rearrange("p (u c) -> p u c", u=2)
        sb_s = w1[:, 2464:3488].rearrange("p (u c) -> p u c", u=2)
        SB_UNITS = [(j, hd) for j in (3, 2, 1, 0) for hd in (0, 1)]
        SB_SAMPLE = {3: 6, 2: 5, 1: 4}

        def sb_cols(j):
            return (SEQ - P * j) + (DEC if j >= 1 else 0)

        def sb_sync(sp):
            sp.wait_ge(g["phase"], PH["diff"])
            ck = a["cache_sb_k"][0, 0].rearrange("(t p) h d -> p t (h d)", p=P)
            cv = a["cache_sb_v"][0, 0].rearrange("(t p) h d -> p t (h d)", p=P)
            def pair(i, more):
                sp.wait_ge(SB["tr"], 3 * i + 1)
                sp.dma_start(sb_k[:, 4:6, :], ck[:, :, bass.ds(i * P, P)]).then_inc(SB["past_k"], 16)
                sp.wait_ge(SB["v_free"], i + 1)
                sp.dma_start(sb_v[:, 4:6, :], cv[:, :, bass.ds(i * P, P)]).then_inc(SB["past_v"], 16)
                ada_load(sp, 1, i + 12, i)
                if more:
                    ada_store_before(sp, 1, i + 12, i)
                ada_bias(sp, 1, i + 12, i)

            pair(0, False)
            sp.wait_ge(AD["stored"], 16 * 12)
            with sp.Fori(1, N_SB // 2) as i:
                pair(i, True)
            ada_store_before(sp, 1, 16, 4)

        def sb_pool(pool):
            pool.memset(sb_k[:, 6, :], 0.0)
            pool.memset(sb_v[:, 6, :], 0.0)
            pool.drain()
            with pool.Fori(0, N_SB // 2) as i:
                pool.wait_ge(SB["tr"], 3 * i + 1)
                for dst, c0, t_new in ((sb_q, 3 * CB, 4), (sb_k, 4 * CB, 6)):
                    pool.tensor_copy(dst[:, 0:NT, :], qkv[:, 0:NT, bass.ds(i * P + c0, P)]).then_inc(SB["staged"], 1)
                    pool.tensor_copy(dst[0:DEC, t_new, :], qkv[0:DEC, NT, bass.ds(i * P + c0, P)]).then_inc(SB["staged"], 1)
                pool.wait_ge(SB["v_free"], i + 1)
                pool.tensor_copy(sb_v[:, 0:NT, :], qkv[:, 0:NT, bass.ds(i * P + 5 * CB, P)]).then_inc(SB["staged"], 1)
                pool.tensor_copy(sb_v[0:DEC, 6, :], qkv[0:DEC, NT, bass.ds(i * P + 5 * CB, P)]).then_inc(SB["staged"], 1)
                for u, (j, hd) in enumerate(SB_UNITS):
                    if j == 0:
                        continue
                    n = sb_cols(j)
                    pool.wait_ge(SB["sp"], 8 * i + u + 1)
                    settle(pool)
                    pool.tensor_copy(sb_r[:, hd, P * j:P * j + (P if j < 3 else n)],
                                     sb_s[:, u % 2, 0:(P if j < 3 else n)]).then_inc(SB["r"], 1)
                    if j < 3:
                        pool.wait_ge(SB["tri"], 8 * i + u + 1)
                        pool.tensor_tensor(sb_r[:, hd, P * j + P:TOK], sb_r[:, hd, P * j + P:TOK],
                                           sb_s[:, u % 2, P:n], ALU.add).then_inc(SB["r"], 1)
            phase_end("pool", pool)

        SB_R = [1, 2, 4, 6, 8, 10, 10, 10]

        def sb_pe(pe):
            pe.sem_inc(SB["tr"], 1)
            pe.sem_inc(SB["v_free"], 1)
            with pe.Fori(0, N_SB // 2) as i:
                pe.wait_ge(SB["staged"], 6 * i + 4)
                transpose_rows(bank[0], [(sb_q[:, t, :], P) for t in range(NT)], P).then_inc(SB["tr"], 1)
                transpose_rows(bank[1], [(sb_k[:, t, :], P) for t in range(NT)], P).then_inc(SB["tr"], 1)
                pe.wait_ge(SB["past_k"], 16 * i + 16)
                pe.wait_ge(SB["ev_a"], 3 * i + 1)
                transpose_rows(bank[0], [(sb_k[:, 4, :], P), (sb_k[:, 5, :], P), (sb_k[:, 6, :], P),
                                         (sb_q[0:DEC, 4, :], DEC)], P).then_inc(SB["tr"], 1)
                pe.wait_ge(SB["ev_a"], 3 * i + 3)
                pe.wait_ge(SB["ev_v"], i + 1)
                pe.wait_ge(SB["staged"], 6 * i + 6)
                pe.wait_ge(SB["past_v"], 16 * i + 16)

                def logits(u):
                    j, hd = SB_UNITS[u]
                    b, half, n = bank[2 + u % 4], slice(HD * hd, HD * hd + HD), SEQ - P * j
                    if u >= 4:
                        pe.wait_ge(SB["w"], 8 * i + u - 3)
                    nc.tensor.matmul(b[:, 0:n], sb_kT[half, P * j:P * j + P], sb_qT[half, P * j:SEQ],
                                     start=True, stop=False, skip_group_check=True)
                    if j >= 1:
                        kt = SB_SAMPLE[j]
                        nc.tensor.matmul(b[:, n:n + DEC], sb_kT[half, P * kt:P * kt + P], sb_qT[half, SEQ:TOK],
                                         start=False, stop=False, skip_group_check=True)
                    if j == 3:
                        nc.tensor.matmul(b[:, n:n + DEC], ident_b[:, :], strict_b[:, 0:DEC],
                                         start=False, stop=False, skip_group_check=True)
                    nc.tensor.matmul(b[:, 0:P], ident_b[:, :], strict_b[:, :],
                                     start=False, stop=True, skip_group_check=True).then_inc(SB["z"], 1)

                def later(u):
                    j, hd = SB_UNITS[u]
                    b, n = bank[2 + u % 4], sb_cols(j)
                    pe.wait_ge(SB["sp"], 8 * i + u + 1)
                    last = nc.tensor.matmul(b[:, 0:n], neg_from[:, :], sb_s[:, u % 2, 0:n], start=False, stop=True,
                                            skip_group_check=True)
                    if j < 3:
                        pe.wait_ge(SB["r"], 10 * i + SB_R[u - 2])
                        last = nc.tensor.matmul(b[:, P:n], neg_ones[:, :], sb_r[:, hd, P * j + P:P * j + n],
                                                start=False, stop=True, skip_group_check=True)
                    last.then_inc(SB["tri"], 1)

                def values(u):
                    j, hd = SB_UNITS[u]
                    half, n = slice(HD * hd, HD * hd + HD), SEQ - P * j
                    pe.wait_ge(SB["w"], 8 * i + u + 1)
                    last = nc.tensor.matmul(bank[7][half, P * j:SEQ], sb_v[:, j, half], sb_w[:, u % 2, 0:n],
                                            start=j == 3, stop=j == 0, skip_group_check=True)
                    if j >= 1:
                        last = nc.tensor.matmul(bank[6][half, 0:DEC], sb_v[:, SB_SAMPLE[j], half],
                                                sb_w[:, u % 2, n:n + DEC], start=j == 3, stop=j == 1)
                    last.then_inc(SB["pv"], 1)

                logits(0)
                logits(1)
                for u in range(8):
                    if u + 2 < 8:
                        logits(u + 2)
                    later(u)
                    if u >= 1:
                        values(u - 1)
                    if u == 2:
                        ada_matvec(pe, i + 12, bank[0])
                    elif u == 4:
                        ada_sum(pe, i + 12, bank[0])
                pe.wait_ge(AD["row"], i + 13)
                values(7)
                nc.tensor.drain().then_inc(SB["v_free"], 1)
            phase_end("pe", pe)

        def sb_act(act):
            act.preload_act_table_set("natural_log_exp_and_others")
            with act.Fori(0, N_SB // 2) as i:
                act.wait_ge(SB["tr"], 3 * i + 2)
                act.activation(sb_qT[:, 0:SEQ], bank[0][:, :], ACT.Copy, scale=HD ** -0.5).then_inc(SB["ev_a"], 1)
                act.wait_ge(SB["tr"], 3 * i + 4)
                act.activation(sb_kT[:, 4 * P:7 * P], bank[0][:, 0:3 * P], ACT.Copy).then_inc(SB["ev_a"], 1)
                act.activation(sb_qT[:, SEQ:TOK], bank[0][:, 3 * P:3 * P + DEC], ACT.Copy, scale=HD ** -0.5).then_inc(SB["ev_a"], 1)

                def log_part(u):
                    j, _ = SB_UNITS[u]
                    n, e = sb_cols(j), sb_e[:, u % 2, 0:sb_cols(j)]
                    act.wait_ge(SB["z"], 8 * i + u + 1)
                    if u >= 2:
                        act.wait_ge(SB["sp"], 8 * i + u - 1)
                    lk = Link(act, SB["self_a"], base=16 * i + 2 * u)
                    lk.do(act.activation(e, bank[2 + u % 4][:, 0:n], ACT.Abs))
                    lk.do(act.activation(e, e, ACT.Exp, scale=-1.0))
                    act.activation(e, e, ACT.Ln, bias=1.0).then_inc(SB["e"], 1)

                def weight(u):
                    n = sb_cols(SB_UNITS[u][0])
                    act.wait_ge(SB["tri"], 8 * i + u + 1)
                    if u >= 2:
                        act.wait_ge(SB["pv"], 8 * i + u - 1)
                    act.activation(sb_w[:, u % 2, 0:n], bank[2 + u % 4][:, 0:n], ACT.Exp).then_inc(SB["w"], 1)

                log_part(0)
                log_part(1)
                for u in range(8):
                    if u + 2 < 8:
                        log_part(u + 2)
                    weight(u)
                    if u == 2:
                        ada_copy(act, i + 12, bank[0])
            phase_end("act", act)

        def sb_dve(dve):
            with dve.Fori(0, N_SB // 2) as i:
                dve.wait_ge(SB["tr"], 3 * i + 3)
                dve.tensor_copy(sb_kT[:, 0:SEQ], bank[1][:, :]).then_inc(SB["ev_v"], 1)
                for u, (j, hd) in enumerate(SB_UNITS):
                    n = sb_cols(j)
                    dve.wait_ge(SB["e"], 8 * i + u + 1)
                    if u >= 2:
                        dve.wait_ge(SB["tri"], 8 * i + u - 1)
                        dve.wait_ge(SB["r"], 10 * i + SB_R[u - 2])
                    dve.scalar_tensor_tensor(out=sb_s[:, u % 2, 0:n], in0=bank[2 + u % 4][:, 0:n], scalar=0.0,
                                             in1=sb_e[:, u % 2, 0:n], op0=ALU.max, op1=ALU.add).then_inc(SB["sp"], 1)
                    if u == 5:
                        ada_add(dve, i + 12, bank[0])
                for hd in range(2):
                    half = slice(HD * hd, HD * hd + HD)
                    dve.wait_ge(SB["pv"], 8 * i + 7 + hd)
                    dve.tensor_copy(hT[half, bass.ds(i + 4, 1), 0:SEQ].rearrange("p a c -> p (a c)"), bank[7][half, :])
                    dve.tensor_copy(hT[half, bass.ds(i + 4, 1), SEQ:TOK].rearrange("p a c -> p (a c)"),
                                    bank[6][half, 0:DEC]).then_inc(SB["o"], 1)
            phase_end("dve", dve)

        FG = sems("fg", "rows", "fl", "self", "biased", "l1", "logf", "cum")

        fl_rows = ring[0:N_FOX, 2, 0:TOK]

        def forget_dve(dve):
            lk = Link(dve, FG["self"])
            y = work[:, 0:TILES * N_FOX].rearrange("p (t h) -> p t h", h=N_FOX)
            dve.wait_ge(FG["fl"], 1)
            for t in range(TILES):
                r = rows(t)
                dve.tensor_tensor(y[0:r, t, :], bank[7][0:r, N_FOX * t:N_FOX * t + N_FOX], bfb[0:r, :],
                                  ALU.add).then_inc(FG["biased"], 1)
            dve.wait_ge(FG["l1"], 2)
            e = work[:, 128:128 + TILES * N_FOX].rearrange("p (t h) -> p t h", h=N_FOX)
            dve.scalar_tensor_tensor(out=logf[:, 0:NT, :], in0=y[:, 0:NT, :], scalar=0.0, in1=e[:, 0:NT, :],
                                     op0=ALU.min, op1=ALU.subtract).then_inc(FG["logf"], 1)
            dve.scalar_tensor_tensor(out=logf[0:DEC, 6, :], in0=y[0:DEC, NT, :], scalar=0.0, in1=e[0:DEC, NT, :],
                                     op0=ALU.min, op1=ALU.subtract).then_inc(FG["logf"], 1)
            dve.wait_ge(FG["cum"], 1)
            b6 = bank[6][:, 0:7 * N_FOX].rearrange("p (t h) -> p t h", h=N_FOX)
            for t0, t1, r in ((0, 6, P), (6, 7, DEC)):
                dve.tensor_copy(dcum[0:r, t0:t1, :], b6[0:r, t0:t1, :])
                dve.tensor_scalar(ndcum[0:r, t0:t1, :], b6[0:r, t0:t1, :], -1.0, None, ALU.mult)
            phase_end("dve", dve)

        def forget_act(act):
            act.preload_act_table_set("natural_log_exp_and_others")
            act.activation(fl_rows[:, 0:SEQ], bank[5][0:N_FOX, :], ACT.Copy)
            act.activation(fl_rows[:, SEQ:TOK], bank[6][0:N_FOX, 0:DEC], ACT.Copy).then_inc(FG["rows"], 1)
            act.wait_ge(FG["biased"], TILES)
            for n, (c0, c1, r) in enumerate(((0, NT * N_FOX, P), (NT * N_FOX, TILES * N_FOX, DEC))):
                e = work[0:r, 128 + c0:128 + c1]
                lk = Link(act, FG["self"], base=2 * n)
                lk.do(act.activation(e, work[0:r, c0:c1], ACT.Abs))
                lk.do(act.activation(e, e, ACT.Exp, scale=-1.0))
                act.activation(e, e, ACT.Ln, bias=1.0).then_inc(FG["l1"], 1)
            phase_end("act", act)

        def forget_pool(pool):
            pool.tensor_scalar(qkv[:, 0:NT, 0:D], qkv[:, 0:NT, 0:D], HD ** -0.5, None, ALU.mult)
            pool.tensor_scalar(qkv[0:DEC, NT, 0:D], qkv[0:DEC, NT, 0:D], HD ** -0.5, None, ALU.mult)
            phase_end("pool", pool)

        def forget_pe(pe):
            pe.wait_ge(FG["rows"], 1)
            for t in range(TILES):
                last = nc.tensor.transpose(bank[7][0:rows(t), N_FOX * t:N_FOX * t + N_FOX], fl_rows[:, cols(t)],
                                           ident[0:N_FOX, 0:N_FOX])
            last.then_inc(FG["fl"], 1)
            pe.wait_ge(FG["logf"], 2)
            pe.wait_ge(g["load_rope"], 48)
            for tiles in ([(0, P), (1, P), (2, P), (3, P)], [(4, P), (5, P), (6, DEC)]):
                for n, (t, r) in enumerate(tiles):
                    dst = bank[6][0:r, N_FOX * t:N_FOX * t + N_FOX]
                    last = nc.tensor.matmul(dst, upto[0:r, 0:r], logf[0:r, t, :], start=True, stop=n == 0)
                    for m, (e, _) in enumerate(tiles[:n]):
                        last = nc.tensor.matmul(dst, ones[:, 0:r], logf[:, e, :], start=False, stop=m == n - 1)
            last.then_inc(FG["cum"], 1)
            phase_end("pe", pe)

        FX = sems("fx", "past_k", "past_v", "staged", "staged_v", "tr", "ev_a", "ev_v", "s", "m", "e", "p", "pt", "pt_ev", "pv",
                  "o", "v_free", "self_v")
        KQ = HD + 2
        fx_q = work[:, 0:660].rearrange("p (t h d) -> p t h d", h=2, d=KQ)
        fx_k = work[:, 660:1584].rearrange("p (t h d) -> p t h d", h=2, d=KQ)
        fx_v = work[:, 1584:2480].rearrange("p (t h d) -> p t h d", h=2, d=HD)
        fx_p = work[:, 2480:4016].rearrange("p (u k) -> p u k", u=3)
        fx_qk = w1[:, 0:2 * QKT].rearrange("p (h c) -> p h c", h=2)
        fx_pt = w1[:, 2 * QKT:2 * QKT + 1024].rearrange("p (u k) -> p u k", u=2)
        FX_UNITS = [(i, hd) for i in range(TILES) for hd in (0, 1)]

        def fox_sync(sp):
            sp.wait_ge(g["phase"], PH["forget"])
            ck = a["cache_fox_k"][0, 0].rearrange("(t p) h d -> p t h d", p=P)
            cv = a["cache_fox_v"][0, 0].rearrange("(t p) h d -> p t h d", p=P)
            def pair(i, more):
                sp.wait_ge(FX["tr"], 6 * i + 1)
                for hd in range(2):
                    sp.dma_start(fx_k[:, 4:6, hd, 0:HD], ck[:, :, bass.ds(2 * i + hd, 1), :].rearrange("p t a d -> p t (a d)")
                                 ).then_inc(FX["past_k"], 16)
                sp.wait_ge(FX["v_free"], i + 1)
                sp.dma_start(fx_v[:, 4:6, :, :].rearrange("p t h d -> p t (h d)"),
                             cv[:, :, bass.ds(2 * i, 2), :].rearrange("p t h d -> p t (h d)")).then_inc(FX["past_v"], 16)
                ada_load(sp, 1, i + 16, i + 4)
                if more:
                    ada_store_before(sp, 1, i + 16, i + 4)
                ada_bias(sp, 1, i + 16, i + 4)

            pair(0, False)
            with sp.Fori(1, N_FOX // 2) as i:
                pair(i, True)
            ada_store_before(sp, 1, 24, 12)

        def fox_pool(pool):
            pool.memset(fx_q[:, :, :, HD:HD + 1], 1.0)
            pool.memset(fx_k[:, :, :, HD + 1:HD + 2], 1.0)
            pool.drain()
            with pool.Fori(0, N_FOX // 2) as i:
                pool.wait_ge(FX["tr"], 6 * i + 1)
                for t0, nt, r, tk in ((0, NT, P, 0), (NT, 1, DEC, 6)):
                    def heads(c0):
                        return qkv[0:r, t0:t0 + nt, bass.ds(i * P + c0, P)].rearrange("p t (h d) -> p t h d", d=HD)
                    pool.tensor_copy(fx_q[0:r, t0:t0 + nt, :, 0:HD], heads(0)).then_inc(FX["staged"], 1)
                    pool.tensor_copy(fx_q[0:r, t0:t0 + nt, :, HD + 1], dcum[0:r, tk:tk + nt, bass.ds(2 * i, 2)]
                                     ).then_inc(FX["staged"], 1)
                    pool.tensor_copy(fx_k[0:r, tk:tk + nt, :, 0:HD], heads(D)).then_inc(FX["staged"], 1)
                pool.tensor_copy(fx_k[:, 0:6, :, HD], ndcum[:, 0:6, bass.ds(2 * i, 2)]).then_inc(FX["staged"], 1)
                pool.tensor_copy(fx_k[0:DEC, 6, :, HD], ndcum[0:DEC, 6, bass.ds(2 * i, 2)]).then_inc(FX["staged"], 1)
                pool.wait_ge(FX["v_free"], i + 1)
                pool.tensor_copy(fx_v[:, 0:NT, :, :].rearrange("p t h d -> p t (h d)"),
                                 qkv[:, 0:NT, bass.ds(i * P + 2 * D, P)]).then_inc(FX["staged_v"], 1)
                pool.tensor_copy(fx_v[0:DEC, 6, :, :].rearrange("p h d -> p (h d)"),
                                 qkv[0:DEC, NT, bass.ds(i * P + 2 * D, P)]).then_inc(FX["staged_v"], 1)
            phase_end("pool", pool)

        def fox_pe(pe):
            pe.sem_inc(FX["tr"], 1)
            pe.sem_inc(FX["v_free"], 1)
            with pe.Fori(0, N_FOX // 2) as i:
                pe.wait_ge(FX["staged"], 8 * i + 8)
                for hd in range(2):
                    b0, b1 = (0, 1) if hd == 0 else (1, 0)
                    if hd == 1:
                        pe.wait_ge(FX["ev_a"], 3 * i + 2)
                    transpose_rows(bank[b0], [(fx_q[:, t, hd, :], P) for t in range(NT)], KQ).then_inc(FX["tr"], 1)
                    if hd == 1:
                        pe.wait_ge(FX["ev_a"], 3 * i + 3)
                    transpose_rows(bank[b1], [(fx_k[:, t, hd, :], P) for t in range(NT)], KQ).then_inc(FX["tr"], 1)
                    if hd == 0:
                        pe.wait_ge(FX["past_k"], 32 * i + 32)
                        pe.wait_ge(FX["ev_a"], 3 * i + 1)
                    else:
                        pe.wait_ge(FX["ev_v"], 3 * i + 1)
                    transpose_rows(bank[b0], [(fx_k[:, 4, hd, :], P), (fx_k[:, 5, hd, :], P), (fx_k[0:DEC, 6, hd, :], DEC),
                                              (fx_q[0:DEC, 4, hd, :], DEC)], KQ).then_inc(FX["tr"], 1)
                pe.wait_ge(FX["ev_a"], 3 * i + 3)

                def scores(u):
                    t, hd = FX_UNITS[u]
                    b, r, n = bank[2 + u % 3], rows(t), nkeys(t)
                    if hd == 1:
                        pe.wait_ge(FX["ev_v"], 3 * i + 3)
                    if u >= 3:
                        pe.wait_ge(FX["e"], 10 * i + u - 2)
                    q0, k0 = (P * t, KP) if t < NT else (QS, KS)
                    nc.tensor.matmul(b[0:r, 0:n], fx_qk[0:KQ, hd, q0:q0 + r], fx_qk[0:KQ, hd, k0:k0 + n],
                                     start=True, stop=False)
                    nc.tensor.matmul(b[0:r, n - r:n], ident_b[0:r, 0:r], causal_b[0:r, 0:r],
                                     start=False, stop=True).then_inc(FX["s"], 1)

                def turn(u):
                    t, hd = FX_UNITS[u]
                    r = rows(t)
                    pe.wait_ge(FX["p"], 10 * i + u + 1)
                    if u >= 2:
                        pe.wait_ge(FX["pt_ev"], 10 * i + u - 1)
                    if t == NT:
                        settle(pe)
                    for n, (j, kr, c) in enumerate(key_tiles(t)):
                        last = nc.tensor.transpose(bank[5 + u % 2][0:kr, r * n:r * n + r], fx_p[0:r, u % 3, c:c + kr],
                                                   ident[0:r, 0:r])
                    last.then_inc(FX["pt"], 1)

                def values(u):
                    t, hd = FX_UNITS[u]
                    r, half = rows(t), slice(HD * hd, HD * hd + HD)
                    pe.wait_ge(FX["pt_ev"], 10 * i + u + 1)
                    if u == 0:
                        pe.wait_ge(FX["staged_v"], 2 * i + 2)
                    if t == NT and hd == 0:
                        pe.wait_ge(FX["past_v"], 16 * i + 16)
                    dst = bank[7][half, P * t:P * t + P] if t < NT else bank[5 + u % 2][half, P:P + DEC]
                    tiles = key_tiles(t)
                    for n, (j, kr, c) in enumerate(tiles):
                        last = nc.tensor.matmul(dst, fx_v[0:kr, j, hd, :], fx_pt[0:kr, u % 2, r * n:r * n + r],
                                                start=n == 0, stop=n == len(tiles) - 1)
                    last.then_inc(FX["pv"], 1)

                scores(0)
                scores(1)
                for u in range(10):
                    if u + 2 < 10:
                        scores(u + 2)
                    turn(u)
                    if u >= 1:
                        values(u - 1)
                    if u == 3:
                        ada_matvec(pe, i + 16, bank[0])
                    elif u == 5:
                        ada_sum(pe, i + 16, bank[0], 1)
                pe.wait_ge(AD["row"], i + 17)
                values(9)
                nc.tensor.drain().then_inc(FX["v_free"], 1)
            phase_end("pe", pe)

        def fox_act(act):
            act.preload_act_table_set("natural_log_exp_and_others")
            with act.Fori(0, N_FOX // 2) as i:
                for n, (b, c0, w) in enumerate(((0, 0, 512), (1, KP, 512), (0, KS, 320))):
                    act.wait_ge(FX["tr"], 6 * i + n + 2)
                    act.activation(fx_qk[0:KQ, 0, c0:c0 + w], bank[b][0:KQ, 0:w], ACT.Copy).then_inc(FX["ev_a"], 1)

                def probs(u):
                    t, hd = FX_UNITS[u]
                    r, n = rows(t), nkeys(t)
                    act.wait_ge(FX["m"], 10 * i + u + 1)
                    if u >= 3:
                        act.wait_ge(FX["pt"], 10 * i + u - 2)
                    act.activation(fx_p[0:r, u % 3, 0:n], bank[2 + u % 3][0:r, 0:n], ACT.Exp, scale=1.0,
                                   bias=small[0:r, u:u + 1], accum_out=small[0:r, 16 + u:17 + u]).then_inc(FX["e"], 1)

                def turned(u):
                    t, hd = FX_UNITS[u]
                    r, n = rows(t), len(key_tiles(t))
                    act.wait_ge(FX["pt"], 10 * i + u + 1)
                    if u >= 2:
                        act.wait_ge(FX["pv"], 10 * i + u - 1)
                    b = bank[5 + u % 2]
                    if t < NT:
                        act.activation(fx_pt[:, u % 2, 0:r * n], b[:, 0:r * n], ACT.Copy).then_inc(FX["pt_ev"], 1)
                    else:
                        act.activation(fx_pt[:, u % 2, 0:2 * r], b[:, 0:2 * r], ACT.Copy)
                        act.activation(fx_pt[0:DEC, u % 2, 2 * r:3 * r], b[0:DEC, 2 * r:3 * r],
                                       ACT.Copy).then_inc(FX["pt_ev"], 1)

                probs(0)
                probs(1)
                for u in range(10):
                    if u + 2 < 10:
                        probs(u + 2)
                    turned(u)
                    if u == 3:
                        ada_copy(act, i + 16, bank[0], 1)
            phase_end("act", act)

        def fox_dve(dve):
            with dve.Fori(0, N_FOX // 2) as i:
                for n, (b, c0, w) in enumerate(((1, 0, 512), (0, KP, 512), (1, KS, 320))):
                    dve.wait_ge(FX["tr"], 6 * i + n + 5)
                    dve.tensor_copy(fx_qk[0:KQ, 1, c0:c0 + w], bank[b][0:KQ, 0:w]).then_inc(FX["ev_v"], 1)

                def maxima(u):
                    t, hd = FX_UNITS[u]
                    r, n = rows(t), nkeys(t)
                    dve.wait_ge(FX["s"], 10 * i + u + 1)
                    dve.reduce_max(small[0:r, u:u + 1], bank[2 + u % 3][0:r, 0:n], X, negate=True).then_inc(FX["m"], 1)

                def normed(u):
                    t, hd = FX_UNITS[u]
                    r, n = rows(t), nkeys(t)
                    dve.wait_ge(FX["e"], 10 * i + u + 1)
                    lk = Link(dve, FX["self_v"], base=10 * i + u)
                    lk.do(dve.reciprocal(small[0:r, 16 + u:17 + u], small[0:r, 16 + u:17 + u]))
                    dve.tensor_scalar(fx_p[0:r, u % 3, 0:n], fx_p[0:r, u % 3, 0:n], small[0:r, 16 + u:17 + u], None,
                                      ALU.mult).then_inc(FX["p"], 1)

                maxima(0)
                for u in range(10):
                    if u + 1 < 10:
                        maxima(u + 1)
                    normed(u)
                    if u == 6:
                        ada_add(dve, i + 16, bank[0])
                for hd in range(2):
                    half = slice(HD * hd, HD * hd + HD)
                    dve.wait_ge(FX["pv"], 10 * i + 9 + hd)
                    dve.tensor_copy(hT[half, bass.ds(i, 1), 0:SEQ].rearrange("p a c -> p (a c)"), bank[7][half, :])
                    dve.tensor_copy(hT[half, bass.ds(i, 1), SEQ:TOK].rearrange("p a c -> p (a c)"),
                                    bank[5 + hd][half, P:P + DEC]).then_inc(FX["o"], 1)
            phase_end("dve", dve)

        OUT = sems("outp", "w0", "w1", "hi", "lo", "mm", "ev", "add")
        o_tmp = arena[:, 0:1024].rearrange("p (u c) -> p u c", u=2)
        out_hi = [ring[:, 2, :], arena[:, 1024:1024 + KD * CB]]
        OUT_PIECES = []
        for n in range(2):
            for q in range(4):
                c0, c1 = 2 * TOK * q + (P - DEC if q else 0), min(2 * TOK * (q + 1) + P - DEC, KD * TOK)
                if n == 0:
                    OUT_PIECES.append((0, hT2_flat[:, c0:c1], hT_flat[:, c0:c1]))
                OUT_PIECES.append((n, out_hi[n][:, 2 * CB * q:2 * CB * (q + 1)], ring[:, 1 - n, 2 * CB * q:2 * CB * (q + 1)]))

        def out_sync(sp, l):
            s, w = OUT, a["w_out_even" if l == 0 else "w_out_odd"][0]
            for n in range(2):
                sp.wait_ge(*((PROJ["used"], 12 * l + 12) if n == 0 else (AD["mv"], (32, 48)[l])))
                sp.dma_start(ring[:, 1 - n, :].rearrange("p (k c) -> p k c", k=KD),
                             w[:, CB * n:CB * n + CB].rearrange("(k p) c -> p k c", p=P)).then_inc(s[f"w{n}"], 16)

        def out_pe(pe, l):
            s = OUT
            for n in range(2):
                hi, lo = (r32(v.rearrange("p (k c) -> p k c", k=KD)) for v in (out_hi[n], ring[:, 1 - n, :]))
                for k in range(KD):
                    if k % 2 == 0:
                        pe.wait_ge(s["lo"], len(OUT_PIECES) * l + (k + 2 if n == 0 else 8 + k // 2 + 1))
                    for t in range(TILES):
                        u = TILES * n + t
                        if k == 0 and u >= 8:
                            pe.wait_ge(s["ev"], 10 * l + u - 7)
                        last = split_product(bank[u % 8][:, :], tile_cols(hT2_flat, k, t), tile_cols(hT_flat, k, t),
                                             hi[:, k, :], lo[:, k, :], k == 0, k == KD - 1)
                        if k == KD - 1:
                            last.then_inc(s["mm"], 1)
            phase_end("pe", pe)

        def out_act(act, l):
            act.activation(r32(hT2_flat[:, KD * TOK:HT_LEN]), ones[:, 0:P - DEC], ACT.Copy)
            for n, hi, whole in OUT_PIECES:
                act.wait_ge(OUT[f"w{n}"], 16 * l + 16)
                if n == 1:
                    act.wait_ge(out_sems[f"kv{l}"], 16 * (8 if l == 0 else 6))
                act.activation(r32(hi), whole, ACT.Copy).then_inc(OUT["hi"], 1)
            phase_end("act", act)

        def out_dve(dve, l):
            s = OUT
            for i, (n, hi, whole) in enumerate(OUT_PIECES):
                dve.wait_ge(s["hi"], len(OUT_PIECES) * l + i + 1)
                dve.tensor_tensor(r32(whole), whole, f32(hi), ALU.subtract).then_inc(s["lo"], 1)
            dve.wait_ge(out_sems[f"kv{l}"], 16 * (8 if l == 0 else 6))
            dve.wait_ge(AD["out"], 32 * (l + 1))
            for u in range(2 * TILES):
                n, t = u // TILES, u % TILES
                r = rows(t)
                dve.wait_ge(s["mm"], 10 * l + u + 1)
                if u >= 2:
                    dve.wait_ge(s["add"], 10 * l + u - 1)
                dve.tensor_tensor(o_tmp[0:r, u % 2, :], bank[u % 8][0:r, :], bc[0:r, G1, group(t), CB * n:CB * n + CB],
                                  ALU.mult).then_inc(s["ev"], 1)
            phase_end("dve", dve)

        def out_pool(pool, l):
            s = OUT
            for u in range(2 * TILES):
                n, t = u // TILES, u % TILES
                r = rows(t)
                pool.wait_ge(s["ev"], 10 * l + u + 1)
                pool.tensor_tensor(x[0:r, t, CB * n:CB * n + CB], x[0:r, t, CB * n:CB * n + CB],
                                   o_tmp[0:r, u % 2, :], ALU.add).then_inc(s["add"], 1)
            phase_end("pool", pool)

        RT = sems("rt", "logits", "e", "self", "mask", "pos", "cnt", "done", "scat")
        rt_self = [0]
        rt = arena[:, 5120:9216]

        def rv(i, n=TILES * NE):
            return rt[:, 96 * i:96 * i + n]

        def route_pe(pe, l):
            s = RT
            for t in range(TILES):
                for k in range(KD):
                    last = nc.tensor.matmul(bank[0][0:rows(t), NE * t:NE * t + NE], hT[:, k, cols(t)], wr[:, k, :],
                                            start=k == 0, stop=k == KD - 1)
            last.then_inc(s["logits"], 1)
            pe.wait_ge(s["mask"], l + 1)
            mask = rv(12).rearrange("p (t e) -> p t e", e=NE)
            for t in range(TILES):
                r = rows(t)
                dst = bank[1][0:r, NE * t:NE * t + NE]
                last = nc.tensor.matmul(dst, before[0:r, 0:r], mask[0:r, t, :], start=True, stop=t == 0)
                for e in range(t):
                    last = nc.tensor.matmul(dst, ones[:, 0:r], mask[:, e, :], start=False, stop=e == t - 1)
            for t in range(TILES):
                last = nc.tensor.matmul(bank[2][:, 0:NE], ones[0:rows(t), :], mask[0:rows(t), t, :],
                                        start=t == 0, stop=t == TILES - 1)
            last.then_inc(s["pos"], 1)
            phase_end("pe", pe)

        def route_act(act, l):
            s = RT
            act.preload_act_table_set("natural_log_exp_and_others")
            act.wait_ge(s["cnt"], l + 1)
            act.wait_ge(s["logits"], l + 1)
            act.activation(rv(0)[:, 0:NT * NE], bank[0][:, 0:NT * NE], ACT.Exp, scale=-1.0)
            act.activation(rv(0)[0:DEC, NT * NE:TILES * NE], bank[0][0:DEC, NT * NE:TILES * NE], ACT.Exp,
                           scale=-1.0).then_inc(s["e"], 1)
            phase_end("act", act)

        def route_pool(pool, l):
            s = RT
            pool.iota(rt[:, 2400:2416], pattern=[[-1, NE]], base=NE, channel_multiplier=0, allow_small_or_imprecise_dtypes=True)
            pool.iota(rt[:, 2416:2420], pattern=[[-1, NG]], base=NG, channel_multiplier=0, allow_small_or_imprecise_dtypes=True)
            pool.iota(rt[:, 2432:2432 + MAX_ITEMS], pattern=[[1, MAX_ITEMS]], base=0, channel_multiplier=0,
                      allow_small_or_imprecise_dtypes=True)
            pool.memset(rv(0), 1.0).then_inc(s["cnt"], 1)
            pool.wait_ge(s["done"], l + 1)
            for t in range(TILES):
                r = rows(t)
                for c in range(2):
                    pool.indirect_dma_start(slot_rows, bass.IndirectOffsetOnAxis(ids[0:r, c, t:t + 1], 0),
                                            h_rows[0:r, t, :], None).then_inc(s["scat"], 16)
            pool.wait_ge(s["scat"], 16 * 2 * TILES * (l + 1))
            phase_end("pool", pool)

        def route_dve(dve, l):
            s = RT
            lk = Link(dve, s["self"], base=rt_self[0])
            T3 = lambda v, e: v.rearrange("p (t e) -> p t e", e=e)
            sig, sel, pair, selm, tmp, oh1, oh2, key, mask, dst = rv(1), rv(2), rv(3, 120), rv(5), rv(6), rv(7), rv(8), rv(9), rv(12), rv(13)
            gs, gk, gsel = rt[:, 2080:2100], rt[:, 2100:2120], rt[:, 2120:2140]
            m1 = rt[:, 2140:2145]
            rank, grank, item = rt[:, 2400:2416], rt[:, 2416:2420], rt[:, 2432:2432 + MAX_ITEMS]

            def bt(v, n):
                return v.unsqueeze(1).to_broadcast([P, TILES, n])

            def be(v, n):
                return v.unsqueeze(2).to_broadcast([P, TILES, n])

            dve.wait_ge(s["cnt"], l + 1)
            dve.wait_ge(s["e"], l + 1)
            lk.do(dve.tensor_scalar(sig, rv(0), 1.0, None, ALU.add))
            lk.do(dve.reciprocal(sig, sig))
            lk.do(dve.tensor_tensor(T3(sel, NE), T3(sig, NE), bt(br[:, :], NE), ALU.add))
            s4 = sel.rearrange("p (n e) -> p n e", e=EPG)
            p6 = pair.rearrange("p (n e) -> p n e", e=6)
            lk.step(dve.tensor_tensor(p6[:, :, 0:3], s4[:, :, 0:3], s4[:, :, 1:4], ALU.add))
            lk.step(dve.tensor_tensor(p6[:, :, 3:5], s4[:, :, 0:2], s4[:, :, 2:4], ALU.add))
            lk.do(dve.tensor_tensor(p6[:, :, 5:6], s4[:, :, 0:1], s4[:, :, 3:4], ALU.add))
            lk.do(dve.tensor_reduce(gs, p6, X, ALU.max))

            def first_max(v, n, rank_row, best, onehot):
                v3, o3 = T3(v, n), T3(onehot, n)
                lk.do(dve.tensor_reduce(best, v3, X, ALU.max))
                lk.do(dve.tensor_tensor(o3, v3, be(best, n), ALU.is_ge))
                lk.do(dve.tensor_tensor(o3, o3, bt(rank_row, n), ALU.mult))
                lk.do(dve.tensor_reduce(best, o3, X, ALU.max))
                lk.do(dve.tensor_tensor(o3, o3, be(best, n), ALU.is_equal))

            first_max(gs, NG, grank, m1, gsel)
            lk.do(dve.tensor_scalar(gk, gsel, 1.0, -NEG, ALU.subtract, ALU.mult))
            lk.do(dve.tensor_tensor(selm.rearrange("p (n e) -> p n e", e=EPG), s4,
                                    gk.unsqueeze(2).to_broadcast([P, TILES * NG, EPG]), ALU.add))
            first_max(selm, NE, rank, m1, oh1)
            lk.do(dve.scalar_tensor_tensor(out=selm, in0=oh1, scalar=2.0 * NEG, in1=selm, op0=ALU.mult, op1=ALU.add))
            first_max(selm, NE, rank, m1, oh2)
            lk.do(dve.tensor_tensor(mask, oh1, oh2, ALU.add))
            dve.drain().then_inc(s["mask"], 1)
            for c, oh in enumerate((oh1, oh2)):
                lk.do(dve.tensor_tensor(tmp, sig, oh, ALU.mult))
                lk.do(dve.tensor_reduce(gates[:, c, :], T3(tmp, NE), X, ALU.add))
            lk.do(dve.tensor_tensor(m1, gates[:, 0, :], gates[:, 1, :], ALU.add))
            lk.do(dve.reciprocal(m1, m1))
            lk.do(dve.tensor_tensor(gates[:, :, :], gates[:, :, :], m1.unsqueeze(1).to_broadcast([P, 2, TILES]), ALU.mult))
            dve.wait_ge(s["pos"], l + 1)
            cnt, nt_, end, st = rt[:, 2144:2160], rt[:, 2160:2176], rt[:, 2176:2192], rt[:, 2192:2208]
            lk.do(dve.tensor_copy(cnt, bank[2][:, 0:NE]))
            lk.do(dve.tensor_scalar(nt_, cnt, 0.0, None, ALU.is_gt))
            lk.do(dve.memset(nt_[:, 0:1], 1.0))
            for j in range(1, TILES):
                lk.do(dve.scalar_tensor_tensor(out=nt_, in0=cnt, scalar=float(P * j), in1=nt_, op0=ALU.is_gt, op1=ALU.add))
            lk.do(dve.tensor_tensor_scan(end, ones[:, 0:NE], nt_, 0.0, ALU.mult, ALU.add))
            lk.do(dve.tensor_tensor(st, end, nt_, ALU.subtract))
            lk.do(dve.tensor_scalar(st, st, float(P), None, ALU.mult))
            lk.do(dve.tensor_copy(dst[:, 0:NT * NE], bank[1][:, 0:NT * NE]))
            lk.do(dve.memset(dst[:, NT * NE:TILES * NE], 0.0))
            lk.do(dve.tensor_copy(dst[0:DEC, NT * NE:TILES * NE], bank[1][0:DEC, NT * NE:TILES * NE]))
            lk.do(dve.tensor_tensor(T3(dst, NE), T3(dst, NE), bt(st, NE), ALU.add))
            for c, oh in enumerate((oh1, oh2)):
                lk.do(dve.tensor_tensor(tmp, dst, oh, ALU.mult))
                lk.do(dve.tensor_reduce(m1, T3(tmp, NE), X, ALU.add))
                lk.do(dve.tensor_copy(ids[:, c, :], m1))
            grid = rt[0:1, 2560:2560 + MAX_ITEMS * NE].rearrange("p (n e) -> p n e", e=NE)
            lk.do(dve.tensor_tensor(grid, item[0:1, :].unsqueeze(2).to_broadcast([1, MAX_ITEMS, NE]),
                                    end[0:1, :].unsqueeze(1).to_broadcast([1, MAX_ITEMS, NE]), ALU.is_ge))
            ie = rt[0:1, 2304:2304 + MAX_ITEMS]
            lk.do(dve.tensor_reduce(ie, grid, X, ALU.add))
            lk.do(dve.tensor_scalar(ie, ie, float(NE - 1), None, ALU.min))
            lk.do(dve.tensor_copy(item_expert[:, :], ie))
            lk.step(dve.tensor_copy(n_items[:, 0:1], total[:, :]))
            lk.step(dve.tensor_scalar(n_items[:, 1:2], end[0:1, NE - 1:NE], total[:, :], 1.0, ALU.add, ALU.subtract))
            lk.step(dve.tensor_tensor(n_items[:, 2:3], end[0:1, NE - 1:NE], total[:, :], ALU.add))
            lk.do(dve.tensor_scalar(n_items[:, 3:4], end[0:1, NE - 1:NE], total[:, :], 2.0, ALU.add, ALU.subtract))
            lk.do(dve.tensor_tensor(total[:, :], total[:, :], end[0:1, NE - 1:NE], ALU.add))
            rt_self[0] += lk.n
            dve.drain().then_inc(s["done"], 1)
            phase_end("dve", dve)

        MO = sems("mo", "wg0", "wg1", "wu0", "wu1", "wd0", "wd1", "hi_g", "hi_u", "hi_d", "lo_g", "lo_u", "lo_d",
                  "lop_g", "lop_u", "lop_d", "x", "tx", "xh", "xl", "g", "sg", "u", "a", "at", "ah", "al", "d", "ev", "y",
                  "stored")
        m_x = arena[:, 0:1024]
        m_xh = arena[:, 1024:2048].rearrange("p (k c) -> p k c", k=KD)
        m_xl = arena[:, 2048:3072].rearrange("p (k c) -> p k c", k=KD)
        m_sg = arena[:, 3072:3584]
        m_a = arena[:, 3584:4096]
        m_ah = arena[:, 4096:4608].rearrange("p (k c) -> p k c", k=KE)
        m_al = arena[:, 4608:5120].rearrange("p (k c) -> p k c", k=KE)
        m_y = arena[:, 8192:9216]
        SLAB = KD * CB
        m_low = {"g": ring[:, 0, :], "u": ring[:, 1, :], "d": ring[:, 2, :]}
        m_high = {"g": hT_flat[:, 0:SLAB], "u": work[:, 0:SLAB], "d": arena[:, 10240:10240 + SLAB]}

        def piece(v, q):
            return v[:, SLAB // 4 * q:SLAB // 4 * (q + 1)]

        def item_no(eng, which):
            i = {"first": 0, "last": 1, "end": 2, "last-1": 3}[which]
            return eng.value_load(n_items[0:1, i:i + 1], min_val=(0, 8, 9, 7)[i], max_val=2 * MAX_ITEMS)

        def first_item(eng, l):
            return 0 if l == 0 else item_no(eng, "first")

        def moe_sync(sp, l):
            s = MO
            slabs = {"g": (a["w_gate"][l], KD), "u": (a["w_up"][l], KD), "d": (a["w_down"][l], KE)}

            def load(c, e):
                w, k = slabs[c]
                w = w[bass.ds(e, 1), :, :].rearrange("a (p k) c -> p (a k) c", k=k)
                for h in range(2):
                    sp.dma_start(m_low[c][:, SLAB // 2 * h:SLAB // 2 * (h + 1)].rearrange("p (k c) -> p k c", k=k // 2),
                                 w[:, k // 2 * h:k // 2 * (h + 1), :]).then_inc(s[f"w{c}{h}"], 16)

            sp.wait_ge(g["phase"], PH[f"out{l}"])
            for c in "gud":
                load(c, 0)
            sp.wait_ge(g["phase"], PH[f"route{l}"])
            if l == 0:
                sp.sem_inc(s["y"], 16)
            first, last, last_1, end = first_item(sp, l), item_no(sp, "last"), item_no(sp, "last-1"), item_no(sp, "end")

            def slot(n):
                i = nc.s_assert_within(n - first, 0, MAX_ITEMS - 1, skip_runtime_bounds_check_because="n is an item of this layer")
                return slot_rows[bass.ds(i * P, P), :]

            def expert(n):
                i = nc.s_assert_within(n - first, 0, MAX_ITEMS - 1, skip_runtime_bounds_check_because="n is an item of this layer")
                return sp.value_load(item_expert[0:1, bass.ds(i, 1)], min_val=0, max_val=NE - 1)

            def rows_in(n):
                sp.wait_ge(s["tx"], 2 * n)
                sp.dma_start(m_x, slot(n)).then_inc(s["x"], 16)

            def store_before(n):
                sp.wait_ge(s["ev"], 2 * n)
                sp.dma_start(slot(n - 1), m_y).then_inc(s["y"], 16)

            def turn(n, down, more_rows):
                e = expert(n + 1)
                sp.wait_ge(s["g"], n + 1)
                load("g", e)
                if more_rows:
                    rows_in(n + 2)
                sp.wait_ge(s["u"], n + 1)
                load("u", e)
                if down:
                    e = expert(n)
                    sp.wait_ge(s["d"], n)
                    load("d", e)
                    store_before(n)

            sp.dma_start(m_x, slot_rows[0:P, :]).then_inc(s["x"], 16)
            rows_in(first + 1)
            turn(first, False, True)
            with sp.Fori(first + 1, last_1) as n:
                turn(n, True, True)
            turn(last_1, True, False)
            e = expert(last)
            sp.wait_ge(s["d"], last)
            load("d", e)
            store_before(last)
            store_before(end)
            sp.wait_ge(s["y"], 16 * end + 16)
            sp.sem_inc(s["stored"], 1)

        def moe_pe(pe, l):
            s = MO
            first, last = first_item(pe, l), item_no(pe, "last")

            def turn_rows(n):
                pe.wait_ge(s["x"], 16 * n + 16)
                settle(pe)
                xk = m_x.rearrange("p (j k) -> p k j", k=KD)
                for half in range(2):
                    for k in range(4):
                        last_ = nc.tensor.transpose(bank[half][:, P * k:P * k + P], xk[:, 4 * half + k, :], ident[:, :])
                    last_.then_inc(s["tx"], 1)

            def wait_piece(c, n, q):
                if q == 1:
                    pe.wait_ge(s[f"lop_{c}"], n if c == "d" else n + 1)
                else:
                    pe.wait_ge(s[f"lo_{c}"], 3 * n + (1, 0, 2, 3)[q])

            def gate_or_up(c, n):
                if c == "g":
                    pe.wait_ge(s["xh"], 2 * n + 2)
                    pe.wait_ge(s["xl"], 2 * n + 2)
                    pe.wait_ge(s["sg"], n)
                else:
                    pe.wait_ge(s["a"], n)
                acc = bank[2 if c == "g" else 3][:, :]
                hi, lo = (r32(v[c].rearrange("p (k c) -> p k c", k=KD)) for v in (m_high, m_low))
                for k in range(KD):
                    if k % 2 == 0:
                        wait_piece(c, n, k // 2)
                    last_ = split_product(acc, r32(m_xh[:, k, :]), r32(m_xl[:, k, :]), hi[:, k, :], lo[:, k, :],
                                          k == 0, k == KD - 1)
                last_.then_inc(s[c], 1)

            def turn_act(n):
                pe.wait_ge(s["a"], n + 1)
                settle(pe)
                ak = m_a.rearrange("p (j k) -> p k j", k=KE)
                for k in range(KE):
                    last_ = nc.tensor.transpose(bank[6][:, P * k:P * k + P], ak[:, k, :], ident[:, :])
                last_.then_inc(s["at"], 1)

            def down_before(n):
                pe.wait_ge(s["al"], n)
                hi, lo = (r32(v["d"].rearrange("p (k c) -> p k c", k=KE)) for v in (m_high, m_low))
                for k in range(KE):
                    wait_piece("d", n, k)
                    for h in range(2):
                        c = slice(CB * h, CB * h + CB)
                        last_ = split_product(bank[4 + h][:, :], r32(m_ah[:, k, :]), r32(m_al[:, k, :]), hi[:, k, c],
                                              lo[:, k, c], k == 0, k == KE - 1)
                last_.then_inc(s["d"], 1)

            turn_rows(first)
            gate_or_up("g", first)
            turn_rows(first + 1)
            gate_or_up("u", first)
            turn_act(first)
            with pe.Fori(first + 1, last) as n:
                gate_or_up("g", n)
                turn_rows(n + 1)
                gate_or_up("u", n)
                down_before(n)
                turn_act(n)
            gate_or_up("g", last)
            gate_or_up("u", last)
            down_before(last)
            turn_act(last)
            down_before(last + 1)
            phase_end("pe", pe)

        def moe_act(act, l):
            s = MO
            act.preload_act_table(ACT.Silu)
            first, last = first_item(act, l), item_no(act, "last")
            if l == 0:
                act.sem_inc(s["hi_d"], 4)

            def split(c, n, *pieces):
                for q in pieces:
                    if q in (0, 2):
                        act.wait_ge(s[f"w{c}{q // 2}"], 16 * n if c == "d" else 16 * n + 16)
                    act.activation(r32(piece(m_high[c], q)), piece(m_low[c], q), ACT.Copy).then_inc(s[f"hi_{c}"], 1)

            def rows_high(n):
                for half in range(2):
                    act.wait_ge(s["tx"], 2 * n + half + 1)
                    act.activation(r32(m_xh[:, 4 * half:4 * half + 4, :]),
                                   bank[half][:, :].rearrange("p (k c) -> p k c", k=4), ACT.Copy).then_inc(s["xh"], 1)

            def silu(n):
                act.wait_ge(s["g"], n + 1)
                act.wait_ge(s["a"], n)
                act.activation(m_sg, bank[2][:, :], ACT.Silu).then_inc(s["sg"], 1)

            def act_high_before(n):
                act.wait_ge(s["at"], n)
                act.activation(r32(m_ah), bank[6][:, :].rearrange("p (k c) -> p k c", k=KE), ACT.Copy).then_inc(s["ah"], 1)

            def results_before(n):
                act.wait_ge(s["d"], n)
                act.wait_ge(s["y"], 16 * n)
                for h in range(2):
                    act.activation(m_y[:, CB * h:CB * h + CB], bank[4 + h][:, :], ACT.Copy).then_inc(s["ev"], 1)

            rows_high(first)
            split("g", first, 0, 1, 2, 3)
            split("u", first, 0, 1)

            def turn(n, before):
                if before:
                    act_high_before(n)
                split("u", n, 2, 3)
                silu(n)
                if before:
                    split("d", n, 0, 1, 2, 3)
                split("g", n + 1, 0, 1)
                act.wait_ge(s["u"], n + 1)
                rows_high(n + 1)
                split("g", n + 1, 2, 3)
                if before:
                    results_before(n)
                split("u", n + 1, 0, 1)

            turn(first, False)
            with act.Fori(first + 1, last) as n:
                turn(n, True)
            act_high_before(last)
            split("u", last, 2, 3)
            silu(last)
            split("d", last, 0, 1, 2, 3)
            results_before(last)
            act_high_before(last + 1)
            split("d", last + 1, 0, 1, 2, 3)
            results_before(last + 1)
            phase_end("act", act)

        def moe_dve(dve, l):
            s = MO
            first, last = first_item(dve, l), item_no(dve, "last")
            if l == 0:
                dve.sem_inc(s["lo_d"], 3)

            def split(c, n, *pieces):
                for q in pieces:
                    dve.wait_ge(s[f"hi_{c}"], 4 * n + q + 1)
                    dve.tensor_tensor(r32(piece(m_low[c], q)), piece(m_low[c], q), f32(piece(m_high[c], q)),
                                      ALU.subtract).then_inc(s[f"lo_{c}"], 1)

            def rows_low(n):
                for half in range(2):
                    dve.wait_ge(s["xh"], 2 * n + half + 1)
                    k = slice(4 * half, 4 * half + 4)
                    dve.tensor_tensor(r32(m_xl[:, k, :]), bank[half][:, :].rearrange("p (k c) -> p k c", k=4),
                                      f32(m_xh[:, k, :]), ALU.subtract).then_inc(s["xl"], 1)

            def product(n):
                dve.wait_ge(s["u"], n + 1)
                dve.wait_ge(s["sg"], n + 1)
                dve.wait_ge(s["at"], n)
                dve.tensor_tensor(m_a, bank[3][:, :], m_sg, ALU.mult).then_inc(s["a"], 1)

            def act_low_before(n):
                dve.wait_ge(s["ah"], n)
                dve.tensor_tensor(r32(m_al), bank[6][:, :].rearrange("p (k c) -> p k c", k=KE), f32(m_ah),
                                  ALU.subtract).then_inc(s["al"], 1)

            rows_low(first)
            split("g", first, 0, 2, 3)
            split("u", first, 0)

            def turn(n, before):
                if before:
                    act_low_before(n)
                split("u", n, 2, 3)
                if before:
                    split("d", n, 0, 2, 3)
                split("g", n + 1, 0)
                rows_low(n + 1)
                product(n)
                split("g", n + 1, 2, 3)
                split("u", n + 1, 0)

            turn(first, False)
            with dve.Fori(first + 1, last) as n:
                turn(n, True)
            act_low_before(last)
            split("u", last, 2, 3)
            split("d", last, 0, 2, 3)
            product(last)
            act_low_before(last + 1)
            split("d", last + 1, 0, 2, 3)
            phase_end("dve", dve)

        def moe_pool(pool, l):
            first, last = first_item(pool, l), item_no(pool, "last")

            def split(c, n):
                pool.wait_ge(MO[f"hi_{c}"], 4 * n + 2)
                settle(pool)
                pool.tensor_tensor(r32(piece(m_low[c], 1)), piece(m_low[c], 1), f32(piece(m_high[c], 1)),
                                   ALU.subtract).then_inc(MO[f"lop_{c}"], 1)

            split("g", first)
            split("u", first)
            split("g", first + 1)
            split("u", first + 1)
            with pool.Fori(first + 1, last) as n:
                split("d", n)
                split("g", n + 1)
                split("u", n + 1)
            split("d", last)
            split("d", last + 1)
            phase_end("pool", pool)

        CO = sems("co", "y0", "y1", "self", "acc")
        c_y = arena[:, 0:8192].rearrange("p (u c d) -> p u c d", u=4, c=2)

        def combine_pool(pool, l):
            s = CO
            pool.wait_ge(MO["stored"], l + 1)

            def gather(t):
                r = rows(t)
                for c in range(2):
                    pool.indirect_dma_start(c_y[0:r, t % 4, c, :], None, slot_rows,
                                            bass.IndirectOffsetOnAxis(ids[0:r, c, t:t + 1], 0)).then_inc(s[f"y{t % 2}"], 16)
            gather(0)
            gather(1)
            for t in range(TILES):
                r = rows(t)
                if t + 2 < TILES:
                    if t + 2 >= 4:
                        pool.wait_ge(s["acc"], 5 * l + t - 1)
                    pool.wait_ge(s[f"y{t % 2}"], (96, 64)[t % 2] * l + 32 * (t // 2 + 1))
                    gather(t + 2)
            phase_end("pool", pool)

        def combine_dve(dve, l):
            s = CO
            lk = Link(dve, s["self"], base=20 * l)
            for t in range(TILES):
                r = rows(t)
                y0, y1 = c_y[0:r, t % 4, 0, :], c_y[0:r, t % 4, 1, :]
                dve.wait_ge(s[f"y{t % 2}"], (96, 64)[t % 2] * l + 32 * (t // 2 + 1))
                lk.do(dve.tensor_scalar(y0, y0, gates[0:r, 0, t:t + 1], None, ALU.mult))
                lk.do(dve.scalar_tensor_tensor(out=y0, in0=y1, scalar=gates[0:r, 1, t:t + 1], in1=y0,
                                               op0=ALU.mult, op1=ALU.add))
                lk.do(dve.tensor_tensor(y0, y0, bc[0:r, G2, group(t), :], ALU.mult))
                lk.do(dve.tensor_tensor(x[0:r, t, :], x[0:r, t, :], y0, ALU.add))
                dve.drain().then_inc(s["acc"], 1)
            phase_end("dve", dve)

        FN = sems("fn", "norm")
        nf = arena[:, 10240:11264]

        def final_act(act):
            for t in range(TILES):
                if t >= 1:
                    act.wait_ge(NORM["square"], 4 * TILES + t)
                act.activation(junk[0:rows(t), :], x[0:rows(t), t, :], ACT.Square,
                               accum_out=ss[0:rows(t), t:t + 1]).then_inc(NORM["square"], 1)
            act.wait_ge(NORM["square"], 5 * TILES)
            act.activation(rstd[:, 0:TILES], ss[:, 0:TILES], ACT.Ln, scale=1.0 / D, bias=eps[:, :]).then_inc(NORM["self"], 1)
            act.wait_ge(NORM["self"], 5)
            act.activation(rstd[:, 0:TILES], rstd[:, 0:TILES], ACT.Exp, scale=-0.5).then_inc(NORM["rstd"], 1)
            phase_end("act", act)

        def final_dve(dve):
            dve.wait_ge(NORM["rstd"], 5)
            dve.wait_ge(FN["norm"], 16)
            for t in range(TILES):
                r = rows(t)
                dve.scalar_tensor_tensor(out=h_rows[0:r, t, :], in0=x[0:r, t, :], scalar=rstd[0:r, t:t + 1],
                                         in1=nf[0:r, :], op0=ALU.mult, op1=ALU.mult).then_inc(NORM["scaled"], 1)
            phase_end("dve", dve)

        def final_sync(sp):
            sp.wait_ge(g["phase"], PH["combine1"])
            sp.dma_start(nf, a["norm_final"].partition_broadcast(P)).then_inc(FN["norm"], 16)
            for t in range(TILES):
                sp.wait_ge(NORM["scaled"], 4 * TILES + t + 1)
                dst = out["y_prompt"][0, P * t:P * t + P, :] if t < NT else out["y_sample"][0]
                sp.dma_start(dst, h_rows[0:rows(t), t, :]).then_inc(out_sems["y"], 16)
            sp.wait_ge(out_sems["y"], 16 * TILES)
            sp.wait_ge(out_sems["kv0"], 16 * 8)
            sp.wait_ge(out_sems["kv1"], 16 * 6)

        @block.sync
        def _(sp):
            setup_sync(sp)
            ada_sync(sp)
            for l in range(2):
                if l == 1:
                    sp.wait_ge(g["phase"], PH["moe0"])
                    mix_load(sp, l)
                proj_sync(sp, l)
                store_kv(sp, l)
                if l == 0:
                    diff_sync(sp)
                    sb_sync(sp)
                else:
                    fox_sync(sp)
                out_sync(sp, l)
                sp.wait_ge(g["phase"], PH["sb" if l == 0 else "fox"])
                sp.wait_ge(AD["stored"], 16 * (16 if l == 0 else 24))
                out_load(sp, l)
                moe_sync(sp, l)
            final_sync(sp)

        @block.tensor
        def _(pe):
            phase_end("pe", pe)
            ada_pe(pe)
            for l in range(2):
                norm_pe(pe, f"norm_mix{l}")
                proj_pe(pe, l)
                if l == 0:
                    phase_end("pe", pe)
                    diff_pe(pe)
                    sb_pe(pe)
                else:
                    forget_pe(pe)
                    fox_pe(pe)
                out_pe(pe, l)
                norm_pe(pe, f"norm_ffn{l}")
                route_pe(pe, l)
                moe_pe(pe, l)
                phase_end("pe", pe)
            phase_end("pe", pe)

        @block.scalar
        def _(act):
            setup_act(act)
            ada_act(act)
            for l in range(2):
                norm_act(act, f"norm_mix{l}")
                proj_act(act, l)
                if l == 0:
                    act.activation(lam[:, 0:2], lam[:, 0:2], ACT.Exp).then_inc(ROPE["lam"], 1)
                    phase_end("act", act)
                    diff_act(act)
                    sb_act(act)
                else:
                    forget_act(act)
                    fox_act(act)
                out_act(act, l)
                norm_act(act, f"norm_ffn{l}")
                route_act(act, l)
                moe_act(act, l)
                phase_end("act", act)
            final_act(act)

        @block.vector
        def _(dve):
            setup_dve(dve)
            ada_dve(dve)
            for l in range(2):
                norm_dve(dve, f"norm_mix{l}")
                proj_dve(dve, l)
                if l == 0:
                    rope_dve(dve)
                    diff_dve(dve)
                    sb_dve(dve)
                else:
                    forget_dve(dve)
                    fox_dve(dve)
                out_dve(dve, l)
                norm_dve(dve, f"norm_ffn{l}")
                route_dve(dve, l)
                moe_dve(dve, l)
                combine_dve(dve, l)
            final_dve(dve)

        @block.gpsimd
        def _(pool):
            setup_pool(pool)
            phase_end("pool", pool)
            for l in range(2):
                norm_pool(pool, f"norm_mix{l}")
                phase_end("pool", pool)
                if l == 0:
                    phase_end("pool", pool)
                    diff_pool(pool)
                    sb_pool(pool)
                else:
                    forget_pool(pool)
                    fox_pool(pool)
                out_pool(pool, l)
                norm_pool(pool, f"norm_ffn{l}")
                route_pool(pool, l)
                moe_pool(pool, l)
                combine_pool(pool, l)
            phase_end("pool", pool)


_INS = ["x_prompt", "x_sample", "c_prompt", "c_sample", "cache_diff_k", "cache_diff_v", "cache_sb_k", "cache_sb_v",
        "cache_fox_k", "cache_fox_v", "cache_fox_logf", "w_ada", "b_ada", "norm_mix", "norm_ffn", "w_in_even",
        "w_out_even", "diff_lq1", "diff_lk1", "diff_lq2", "diff_lk2", "diff_subln", "w_in_odd", "b_forget",
        "w_out_odd", "w_router", "b_router", "w_gate", "w_up", "w_down", "norm_final"]


def _outs():
    o = [("y_prompt", (1, SEQ, D)), ("y_sample", (1, DEC, D))]
    for tag, n in (("_p", SEQ), ("_s", DEC)):
        o += [("diff_k" + tag, (1, 1, n, N_DIFF, 2 * HD)), ("diff_v" + tag, (1, 1, n, N_DIFF, 2 * HD)),
              ("sb_k" + tag, (1, 1, n, N_SB, HD)), ("sb_v" + tag, (1, 1, n, N_SB, HD)),
              ("fox_k" + tag, (1, 1, n, N_FOX, HD)), ("fox_v" + tag, (1, 1, n, N_FOX, HD)),
              ("fox_logf" + tag, (1, 1, n, N_FOX))]
    return o


def _rope_table():
    pos = np.concatenate([np.arange(SEQ), PAST + np.arange(DEC)]).astype(np.float32)
    half = HD // 4 // 2
    inv = np.float32(500000.0) ** (-np.arange(half, dtype=np.float32) / np.float32(half))
    ang = pos[:, None] * inv[None, :].astype(np.float32)
    return np.concatenate([np.cos(ang), np.sin(ang)], axis=1).astype(np.float32)


def kernel(**inputs):
    import concourse.bacc as _bacc
    from concourse.bass_utils import run_bass_kernel_spmd as _run

    nc = _bacc.Bacc("TRN2", target_bir_lowering=False, num_devices=1)
    arrays, args = {}, {}
    for name in _INS:
        v = np.ascontiguousarray(inputs[name])
        arrays[f"in_{name}"] = v
        args[name] = nc.dram_tensor(f"in_{name}", v.shape, mybir.dt.from_np(v.dtype), kind="ExternalInput").ap()
    table = _rope_table()
    arrays["rope_table"] = table
    rope_dram = nc.dram_tensor("rope_table", table.shape, F32, kind="ExternalInput").ap()
    outs = {}
    for name, shape in _outs():
        outs[name] = nc.dram_tensor(f"out_{name}", shape, F32, kind="ExternalOutput").ap()
    encoder_step(nc, args, outs, rope_dram)
    r = _run(nc, [arrays], core_ids=[0])
    return tuple(r.results[0][f"out_{name}"] for name, _ in _outs())
```

```python
from contextlib import ExitStack

import numpy as np

import concourse.bass as bass
from concourse import mybir

F32 = mybir.dt.float32
F32R = mybir.dt.float32r
BF16 = mybir.dt.bfloat16
I32 = mybir.dt.int32
ALU = mybir.AluOpType
ACT = mybir.ActivationFunctionType
X = mybir.AxisListType.X

P = 128
D = 1024
KD = D // P
SEQ, DEC, PAST = 512, 32, 256
NT = SEQ // P
TILES = NT + 1
TOK = SEQ + DEC
HD = 64
N_DIFF, N_SB, N_FOX = D // 256, D // 128, D // HD
QKV = 3 * D
CB = 512
NE, NG, EPG = 16, 4, 4
DE = D // 2
KE = DE // P
EPS = 1e-6
NEG = -1e30
LAM_INIT = 0.8 - 0.6
MAX_ITEMS = (2 * TOK + NE * (P - 1)) // P + 1
SLOTS = MAX_ITEMS * P
HT_LEN = KD * TOK + P - DEC


def rows(t):
    return P if t < NT else DEC


def group(t):
    return 0 if t < NT else 1


def cols(t):
    return slice(P * t, P * t + rows(t))


class Link:

    def __init__(self, eng, sem, base=0):
        self.eng, self.sem, self.base, self.n = eng, sem, base, 0

    def step(self, ins):
        ins.then_inc(self.sem, 1)
        self.n += 1

    def wait(self):
        self.eng.wait_ge(self.sem, self.base + self.n)

    def do(self, ins):
        self.step(ins)
        self.wait()


def encoder_step(nc, a, out, rope_dram):
    ctx = ExitStack()
    with ctx:
        def sb(name, shape, dt=F32):
            return ctx.enter_context(nc.sbuf_tensor(name, shape, dt))

        def sems(prefix, *names):
            return {n: ctx.enter_context(nc.semaphore(f"{prefix}_{n}")) for n in names}

        rounded = {}

        def sb_both(name, shape):
            at = -(-nc.sbuf_base // 32) * 32
            t = sb(name, shape)
            rounded[t.name] = nc.alloc_sbuf_tensor_at(name + "_r", shape, F32R, offset=at)
            return t

        def r32(ap):
            return bass.AP(tensor=rounded[ap.tensor.name], offset=ap.offset, ap=ap.ap)

        def f32(ap):
            return r32(ap).bitcast(F32)

        slot_rows = nc.dram_tensor("slot_rows", (SLOTS, D), F32, kind="Internal").ap()

        mod_rows = nc.dram_tensor("mod_rows", (2, 2, 6 * D), F32, kind="Internal").ap()

        x = sb("x", [P, TILES, D])
        hT_flat = sb_both("hT", [P, HT_LEN])
        arena = sb_both("arena", [P, TILES * QKV])
        ring = sb_both("ring", [P, 3, KD * CB])
        bc = sb("bc", [P, 4, 2, D])
        work = sb_both("work", [P, 4608])
        G1, A2, B2, G2 = range(4)

        ident = sb("ident", [P, P])
        ident_b = sb("ident_b", [P, P], BF16)
        causal_b = sb("causal_b", [P, P], BF16)
        chunk_b = sb("chunk_b", [P, P], BF16)
        strict_b = sb("strict_b", [P, P], BF16)
        ones = sb("ones", [P, P])
        neg_ones = sb("neg_ones", [P, P])
        upto = sb("upto", [P, P])
        before_b = sb("before_b", [P, P], BF16)
        ones_b = sb("ones_b", [P, P], BF16)
        mask_b = sb("mask_b", [P, TILES * NE], BF16)
        neg_from = sb("neg_from", [P, P])
        pick = sb("pick", [P, 32])
        ada_row = sb("ada_row", [2, CB])
        eps = sb("eps", [P, 1])
        silu_c = sb("silu_c", [P, KD, 32])
        c_in = sb("c_in", [P, 2, KD])
        ss = sb("ss", [P, 8])
        rstd = sb("rstd", [P, 8])
        rope = sb("rope", [P, TILES, 2, 8])
        lamv = work[:, 0:4 * HD].rearrange("p (n d) -> p n d", d=HD)
        lam = sb("lam", [P, 8])
        subg = sb("subg", [P, 1])
        wr = sb("wr", [P, KD, NE])
        br = sb("br", [P, NE])
        wf = sb_both("wf", [P, 2, 256])
        bfb = sb("bfb", [P, N_FOX])
        logf = sb("logf", [P, 7, N_FOX])
        dcum = sb("dcum", [P, 7, N_FOX])
        ndcum = sb("ndcum", [P, 7, N_FOX])
        df_ss = sb("df_ss", [P, TILES, N_DIFF])
        small = sb("small", [P, 64])
        ids = sb("ids", [P, 2, TILES], I32)
        item_expert = sb("item_expert", [1, MAX_ITEMS], I32)
        n_items = sb("n_items", [1, 4], I32)
        total = sb("total", [1, 1])
        gates = sb("gates", [P, 2, TILES])
        bank = [ctx.enter_context(nc.psum_tensor(f"bank{i}", [P, 512], F32)) for i in range(8)]

        hT = hT_flat[:, 0:KD * TOK].rearrange("p (k c) -> p k c", k=KD)
        hT2_flat = work[:, 0:HT_LEN]
        hT2 = hT2_flat[:, 0:KD * TOK].rearrange("p (k c) -> p k c", k=KD)
        qkv = arena[:, :].rearrange("p (t c) -> p t c", c=QKV)
        w1 = ring[:, 2, :]

        g = sems("g", "settled", "phase", "const", "load_x", "load_small", "load_rest", "load_rope", "zero_rows", "zeroed", "pre_w", "setup")
        out_sems = sems("out", "kv0", "kv1", "y")

        phase_no = {"pe": 0, "act": 0, "dve": 0, "pool": 0}

        def phase_end(name, eng):
            phase_no[name] += 1
            eng.drain()
            eng.sem_inc(g["phase"], 1)
            eng.wait_ge(g["phase"], 4 * phase_no[name])

        def settle(eng):
            eng.sem_inc(g["settled"], 1)

        block = ctx.enter_context(nc.Block())

        PH = {}
        order = ["setup"]
        for l in range(2):
            order += ([f"ada{l}"] if l == 0 else []) + [f"norm_mix{l}", f"proj{l}"]
            order += ["rope", "diff", "sb"] if l == 0 else ["forget", "fox"]
            order += [f"out{l}", f"norm_ffn{l}", f"route{l}", f"moe{l}", f"combine{l}"]
        order += ["final"]
        for i, n in enumerate(order):
            PH[n] = 4 * (i + 1)

        def setup_pool(pool):
            pool.memset(ident[:, :], 0.0)
            pool.memset(ident_b[:, :], 0.0)
            pool.memset(causal_b[:, :], 0.0)
            pool.memset(chunk_b[:, :], 0.0)
            pool.memset(strict_b[:, :], 0.0)
            pool.memset(ones[:, :], 1.0)
            pool.memset(neg_ones[:, :], -1.0)
            pool.memset(upto[:, :], 1.0)
            pool.memset(before_b[:, :], 1.0)
            pool.memset(ones_b[:, :], 1.0)
            pool.memset(neg_from[:, :], -1.0)
            pool.memset(pick[:, :], 0.0)
            pool.memset(eps[:, :], EPS)
            pool.memset(wf[:, 1, P:256], 0.0)
            pool.memset(silu_c[:, :, :], 0.0).then_inc(g["const"], 1)
            pool.wait_ge(g["const"], 1)
            pool.memset(chunk_b[0:64, 64:128], NEG)
            for m in (ident, ident_b):
                pool.affine_select(out=m[:, :], in_=m[:, :], compare_op=ALU.not_equal, fill=1.0, base=0,
                                   pattern=[[-1, P]], channel_multiplier=1)
            pool.affine_select(out=causal_b[:, :], in_=causal_b[:, :], compare_op=ALU.is_ge, fill=NEG, base=0,
                               pattern=[[-1, P]], channel_multiplier=1)
            pool.affine_select(out=strict_b[:, :], in_=strict_b[:, :], compare_op=ALU.is_ge, fill=NEG, base=-1,
                               pattern=[[1, P]], channel_multiplier=-1)
            pool.affine_select(out=upto[:, :], in_=upto[:, :], compare_op=ALU.is_ge, fill=0.0, base=0,
                               pattern=[[1, P]], channel_multiplier=-1)
            pool.affine_select(out=before_b[:, :], in_=before_b[:, :], compare_op=ALU.is_ge, fill=0.0, base=-1,
                               pattern=[[1, P]], channel_multiplier=-1)
            pool.affine_select(out=neg_from[:, :], in_=neg_from[:, :], compare_op=ALU.is_ge, fill=0.0, base=0,
                               pattern=[[-1, P]], channel_multiplier=1)
            for q in range(4):
                pool.drain()
                pool.affine_select(out=pick[:, 0:2], in_=pick[:, 0:2], compare_op=ALU.not_equal,
                                   fill=1.0, base=-32 * q, pattern=[[-1, 2]], channel_multiplier=1)
            phase_end("pool", pool)

        def setup_act(act):
            act.wait_ge(g["load_small"], 16 * 7)
            act.wait_ge(g["const"], 1)
            act.activation(silu_c[:, :, 0:2], c_in[:, :, :].rearrange("p g k -> p k g"), ACT.Silu)
            phase_end("act", act)

        def setup_dve(dve):
            dve.memset(ss[:, :], 1.0)
            dve.memset(total[:, :], 0.0)
            dve.memset(df_ss[:, :, :], 1.0)
            dve.wait_ge(g["load_small"], 16 * 7)
            lk = Link(dve, g["setup"])
            for i in range(2):
                lk.do(dve.tensor_tensor(lamv[:, 2 * i, :], lamv[:, 2 * i, :], lamv[:, 2 * i + 1, :], ALU.mult))
                lk.do(dve.reduce_sum(lam[:, i:i + 1], lamv[:, 2 * i, :], X))
            dve.tensor_scalar(subg[:, :], subg[:, :], 1.0 - LAM_INIT, None, ALU.mult)
            phase_end("dve", dve)

        def setup_sync(sp):
            small_loads = [
                (c_in[:, 0, :], a["c_prompt"].rearrange("a (p k) -> (a p) k", p=P)),
                (c_in[:, 1, :], a["c_sample"].rearrange("a (p k) -> (a p) k", p=P)),
                (lamv[:, 0, :], a["diff_lq1"][0, :].partition_broadcast(P)),
                (lamv[:, 1, :], a["diff_lk1"][0, :].partition_broadcast(P)),
                (lamv[:, 2, :], a["diff_lq2"][0, :].partition_broadcast(P)),
                (lamv[:, 3, :], a["diff_lk2"][0, :].partition_broadcast(P)),
                (subg[:, :], a["diff_subln"].rearrange("a (p k) -> (a p) k", p=P)),
            ]
            for dst, src in small_loads:
                sp.dma_start(dst, src).then_inc(g["load_small"], 16)

        def rest_sync(sp):
            rest = [
                (wr[:, :, :], a["w_router"].rearrange("(k p) e -> p k e", p=P)),
                (br[:, :], a["b_router"].partition_broadcast(P)),
                (wf[:, 1, 0:P].rearrange("p (k e) -> p k e", e=N_FOX), a["w_in_odd"][0, :, QKV:QKV + N_FOX].rearrange("(k p) e -> p k e", p=P)),
                (bfb[:, :], a["b_forget"][0, :].partition_broadcast(P)),
            ]
            for dst, src in rest:
                sp.dma_start(dst, src).then_inc(g["load_rest"], 16)
            sp.dma_start(x[:, 0:NT, :], a["x_prompt"][0].rearrange("(t p) d -> p t d", p=P)).then_inc(g["load_x"], 16)
            sp.dma_start(x[0:DEC, NT, :], a["x_sample"][0]).then_inc(g["load_x"], 16)
            sp.dma_start(rope[:, 0:NT, :, :].rearrange("p t a b -> p t (a b)"),
                         rope_dram[0:SEQ, :].rearrange("(t p) c -> p t c", p=P)).then_inc(g["load_rope"], 16)
            sp.dma_start(rope[0:DEC, NT, :, :].rearrange("p a b -> p (a b)"),
                         rope_dram[SEQ:TOK, :]).then_inc(g["load_rope"], 16)
            sp.dma_start(logf[:, 4:6, :], a["cache_fox_logf"][0, 0].rearrange("(t p) h -> p t h", p=P)).then_inc(g["load_rope"], 16)

        AD = sems("ada", "w0", "w1", "bias", "mv", "part", "sum", "row", "stored", "mix", "ffn", "out")
        ada_w = [ring[:, 0, 4 * CB * h:4 * CB * (h + 1)].rearrange("p (k c) -> p k c", k=4) for h in range(2)]
        mod1 = arena[:, 10240:14336].rearrange("p (v g c) -> p v g c", v=2, g=2)
        normg = arena[:, 9216:10240]

        def ada_part(pre):
            return work[:, 4096:4608] if pre else ring[:, 0, 0:CB]

        def ada_load(sp, l, c, b):
            for h in range(2):
                if h == 0:
                    sp.wait_ge(AD["sum"], c)
                else:
                    sp.wait_ge(AD["mv"], 2 * c)
                sp.dma_start(ada_w[h], a["w_ada"][l, :, bass.ds(b * CB, CB)].rearrange("(p k) c -> p k c", k=KD)[:, 4 * h:4 * h + 4, :]
                             ).then_inc(AD[f"w{h}"], 16)

        def ada_bias(sp, l, c, b):
            sp.wait_ge(AD["stored"], 16 * c)
            sp.dma_start(ada_row[:, :], a["b_ada"][l, bass.ds(b * CB, CB)].partition_broadcast(2)).then_inc(AD["bias"], 16)

        def ada_store_before(sp, l, c, b):
            sp.wait_ge(AD["row"], c)
            sp.dma_start(mod_rows[l, :, bass.ds((b - 1) * CB, CB)], ada_row[:, :]).then_inc(AD["stored"], 16)

        def ada_matvec(pe, c, acc, halves=(0, 1)):
            for h in halves:
                pe.wait_ge(AD[f"w{h}"], 16 * c + 16)
                for q in range(4):
                    last = nc.tensor.matmul(acc[32 * q:32 * q + 32, :], silu_c[:, 4 * h + q, :], ada_w[h][:, q, :],
                                            start=h == 0, stop=h == 1)
                last.then_inc(AD["mv"], 1)

        def ada_sum(pe, c, acc, pre=False):
            pe.wait_ge(AD["part"], c + 1)
            nc.tensor.matmul(acc[0:32, :], pick[:, :], ada_part(pre), start=True, stop=True).then_inc(AD["sum"], 1)

        def ada_copy(act, c, acc, pre=False):
            act.wait_ge(AD["mv"], 2 * c + 2)
            act.wait_ge(AD["sum"], c)
            act.activation(ada_part(pre), acc[:, :], ACT.Copy).then_inc(AD["part"], 1)

        def ada_add(dve, c, acc):
            dve.wait_ge(AD["sum"], c + 1)
            dve.wait_ge(AD["bias"], 16 * c + 16)
            dve.tensor_tensor(ada_row[:, :], ada_row[:, :], acc[0:2, :], ALU.add).then_inc(AD["row"], 1)

        def mod_load(sp, l, v, dst, sem):
            for grp in range(2):
                n = (P, DEC)[grp]
                sp.dma_start(dst[0:n, grp, :], mod_rows[l, grp, D * v:D * v + D].partition_broadcast(n)).then_inc(AD[sem], 16)

        pre_w = [ring[:, c % 3, :].rearrange("p (k c) -> p k c", k=KD) for c in range(4)]
        pre_row = arena[0:2, 0:4 * CB]

        def ada_sync(sp):
            for c in range(4):
                if c == 3:
                    sp.wait_ge(AD["mv"], 2)
                sp.dma_start(pre_w[c], a["w_ada"][0, :, CB * c:CB * c + CB].rearrange("(p k) c -> p k c", k=KD)
                             ).then_inc(AD[f"w{c % 2}"] if c < 2 else g["pre_w"], 16)
                if c == 2:
                    sp.dma_start(pre_row, a["b_ada"][0, 0:4 * CB].partition_broadcast(2)).then_inc(AD["bias"], 64)
                    rest_sync(sp)
                    sp.wait_ge(g["pre_w"], 16)
            sp.wait_ge(AD["row"], 4)
            sp.dma_start(mod_rows[0, :, 0:4 * CB], pre_row).then_inc(AD["stored"], 64)
            sp.wait_ge(AD["stored"], 64)
            mix_load(sp, 0)

        def mix_load(sp, l):
            mod_load(sp, l, 0, mod1[:, 0], "mix")
            mod_load(sp, l, 1, mod1[:, 1], "mix")
            sp.dma_start(normg, a["norm_mix"][l, :].partition_broadcast(P)).then_inc(AD["mix"], 16)

        def out_load(sp, l):
            mod_load(sp, l, 2, bc[:, G1], "out")
            mod_load(sp, l, 3, bc[:, B2], "ffn")
            mod_load(sp, l, 4, bc[:, A2], "ffn")
            sp.dma_start(normg, a["norm_ffn"][l, :].partition_broadcast(P)).then_inc(AD["ffn"], 16)
            mod_load(sp, l, 5, bc[:, G2], "ffn")

        def ada_pe(pe):
            pe.sem_inc(AD["w0"], 48)
            pe.sem_inc(AD["w1"], 48)
            for c in range(4):
                if c < 2:
                    pe.wait_ge(AD[f"w{c}"], 64)
                else:
                    pe.wait_ge(g["pre_w"], 16 * (c - 1))
                for k in range(KD):
                    q = k % 4
                    last = nc.tensor.matmul(bank[c][32 * q:32 * q + 32, :], silu_c[:, k, :], pre_w[c][:, k, :],
                                            start=k < 4, stop=k >= 4)
                last.then_inc(AD["mv"], 2)
                if c >= 1:
                    ada_sum(pe, c - 1, bank[c - 1], True)
            ada_sum(pe, 3, bank[3], True)
            phase_end("pe", pe)

        def ada_act(act):
            for c in range(4):
                ada_copy(act, c, bank[c], True)
            act.wait_ge(g["load_rest"], 64)
            act.activation(r32(wf[:, 0, :]), wf[:, 1, :], ACT.Copy).then_inc(g["const"], 1)
            phase_end("act", act)

        def ada_dve(dve):
            for c in range(4):
                dve.wait_ge(AD["sum"], c + 1)
                dve.wait_ge(AD["bias"], 64)
                r = pre_row[:, CB * c:CB * c + CB]
                dve.tensor_tensor(r, r, bank[c][0:2, :], ALU.add).then_inc(AD["row"], 1)
            dve.wait_ge(g["const"], 2)
            dve.tensor_tensor(r32(wf[:, 1, :]), wf[:, 1, :], f32(wf[:, 0, :]), ALU.subtract)
            phase_end("dve", dve)

        h_rows = arena[:, 0:TILES * D].rearrange("p (t d) -> p t d", d=D)
        junk = arena[:, 14336:15360]
        NORM = sems("norm", "square", "rstd", "scaled", "shifted", "tr", "ev_a", "ev_v", "self", "gain", "shift_v")
        NORM_NO = {"norm_mix0": 0, "norm_ffn0": 1, "norm_mix1": 2, "norm_ffn1": 3}

        def scale_shift(name, t):
            r, grp = rows(t), group(t)
            if name.startswith("norm_mix"):
                return mod1[0:r, 1, grp, :], mod1[0:r, 0, grp, :]
            return bc[0:r, A2, grp, :], bc[0:r, B2, grp, :]

        def part_of(dst, u):
            return dst[:, 4 * (u % 2):4 * (u % 2) + 4, cols(u // 2)]

        def bank_of(u):
            return bank[u % 6][:, :].rearrange("p (k c) -> p k c", k=4)[:, :, 0:rows(u // 2)]

        EV_A, EV_V = (0, 10, 15, 25), (0, 10, 15, 25)

        def norm_act(act, name):
            s, o = NORM, NORM_NO[name]
            act.preload_act_table_set("natural_log_exp_and_others")
            if name == "norm_mix0":
                act.wait_ge(g["load_x"], 32)

            def evacuate(t):
                if name.startswith("norm_mix"):
                    for u in (2 * t, 2 * t + 1):
                        act.wait_ge(s["tr"], 10 * o + u + 1)
                        act.activation(r32(part_of(hT, u)), bank_of(u), ACT.Copy).then_inc(s["ev_a"], 1)
                else:
                    act.wait_ge(s["tr"], 10 * o + 2 * t + 1)
                    act.activation(part_of(hT, 2 * t), bank_of(2 * t), ACT.Copy).then_inc(s["ev_a"], 1)

            row_rstd(act, o, evacuate)
            phase_end("act", act)

        def row_rstd(act, o, evacuate=None):
            s = NORM

            def square(t):
                if t >= 1:
                    act.wait_ge(s["square"], TILES * o + t)
                act.activation(junk[0:rows(t), :], x[0:rows(t), t, :], ACT.Square,
                               accum_out=ss[0:rows(t), t:t + 1]).then_inc(s["square"], 1)

            def finish(t):
                z = rstd[0:rows(t), t:t + 1]
                act.wait_ge(s["square"], TILES * o + t + 1)
                act.activation(z, ss[0:rows(t), t:t + 1], ACT.Ln, scale=1.0 / D, bias=eps[0:rows(t), :]).then_inc(s["self"], 1)
                act.wait_ge(s["self"], TILES * o + t + 1)
                act.activation(z, z, ACT.Exp, scale=-0.5).then_inc(s["rstd"], 1)

            square(0)
            for t in range(1, TILES):
                square(t)
                finish(t - 1)
                if t >= 3 and evacuate:
                    evacuate(t - 3)
            finish(TILES - 1)
            if evacuate:
                for t in (2, 3, 4):
                    evacuate(t)

        def norm_dve(dve, name):
            s, o = NORM, NORM_NO[name]
            l = int(name[-1])
            if name.startswith("norm_mix"):
                dve.wait_ge(AD["mix"], 80 * (l + 1))
            else:
                dve.wait_ge(AD["ffn"], 112 * (l + 1))
            for grp in range(2):
                scale = scale_shift(name, NT * grp)[0]
                dve.scalar_tensor_tensor(out=scale, in0=scale, scalar=1.0, in1=normg[0:(P, DEC)[grp], :],
                                         op0=ALU.add, op1=ALU.mult).then_inc(s["gain"], 1)
            dve.wait_ge(s["gain"], 2 * o + 2)

            def scale(t):
                r = rows(t)
                dve.wait_ge(s["rstd"], TILES * o + t + 1)
                dve.scalar_tensor_tensor(out=h_rows[0:r, t, :], in0=x[0:r, t, :], scalar=rstd[0:r, t:t + 1],
                                         in1=scale_shift(name, t)[0], op0=ALU.mult, op1=ALU.mult).then_inc(s["scaled"], 1)

            def shift(t):
                dve.wait_ge(s["scaled"], TILES * o + t + 1)
                dve.tensor_tensor(h_rows[:, t, :], h_rows[:, t, :], scale_shift(name, t)[1], ALU.add).then_inc(s["shift_v"], 1)

            scale(0)
            scale(1)
            shift(1)
            scale(2)
            evac(dve, name, 0)
            scale(3)
            shift(3)
            evac(dve, name, 1)
            scale(4)
            for t in (2, 3, 4):
                evac(dve, name, t)
            phase_end("dve", dve)

        def evac(dve, name, t):
            s, o = NORM, NORM_NO[name]
            if name.startswith("norm_mix"):
                for u in (2 * t, 2 * t + 1):
                    dve.wait_ge(s["ev_a"], EV_A[o] + u + 1)
                    dve.tensor_tensor(r32(part_of(hT2, u)), bank_of(u), f32(part_of(hT, u)), ALU.subtract).then_inc(s["ev_v"], 1)
            else:
                dve.wait_ge(s["tr"], 10 * o + 2 * t + 2)
                dve.tensor_copy(part_of(hT, 2 * t + 1), bank_of(2 * t + 1)).then_inc(s["ev_v"], 1)

        def norm_pool(pool, name):
            s, o = NORM, NORM_NO[name]
            if name == "norm_mix0":
                pool.memset(ring[:, 2, 0:D], 0.0).then_inc(g["zero_rows"], 1)
            if name.startswith("norm_mix"):
                for flat in (hT_flat, hT2_flat):
                    pool.tensor_copy(r32(flat[:, KD * TOK:HT_LEN]), ones[:, 0:P - DEC])
            for t in (0, 2, 4):
                r = rows(t)
                pool.wait_ge(s["scaled"], 5 * o + t + 1)
                pool.tensor_tensor(h_rows[0:r, t, :], h_rows[0:r, t, :], scale_shift(name, t)[1],
                                   ALU.add).then_inc(s["shifted"], 1)
            phase_end("pool", pool)

        def norm_pe(pe, name):
            s, o = NORM, NORM_NO[name]
            both = 2 if name.startswith("norm_mix") else 1
            for t in range(TILES):
                r = rows(t)
                if t % 2 == 0:
                    pe.wait_ge(s["shifted"], 3 * o + t // 2 + 1)
                else:
                    pe.wait_ge(s["shift_v"], 2 * o + t // 2 + 1)
                if t >= 3:
                    pe.wait_ge(s["ev_a"], EV_A[o] + both * (t - 2))
                    pe.wait_ge(s["ev_v"], EV_V[o] + both * (t - 2))
                for half in range(2):
                    for k in range(4):
                        d0 = P * (4 * half + k)
                        last = nc.tensor.transpose(bank[(2 * t + half) % 6][:, P * k:P * k + r],
                                                   h_rows[0:r, t, d0:d0 + P], ident[0:r, 0:r])
                    last.then_inc(s["tr"], 1)
                if t >= 1 and name.startswith("norm_ffn"):
                    router_logits(pe, name, t - 1)
            if name.startswith("norm_ffn"):
                router_logits(pe, name, TILES - 1).then_inc(RT["logits"], 1)
            phase_end("pe", pe)

        RT = sems("rt", "logits", "e", "turned", "self", "mask", "pos", "cnt", "done", "scat")

        def router_logits(pe, name, t):
            s, o = NORM, NORM_NO[name]
            pe.wait_ge(s["ev_a"], EV_A[o] + t + 1)
            pe.wait_ge(s["ev_v"], EV_V[o] + t + 1)
            acc = bank[6][0:NE, cols(t)] if t < NT else bank[7][0:NE, 0:DEC]
            for k in range(KD):
                last = nc.tensor.matmul(acc, wr[:, k, :], hT[:, k, cols(t)], start=k == 0, stop=k == KD - 1)
            return last

        PROJ = sems("proj", "w0", "w1", "hi", "lo", "mm", "used", "ev_a", "ev_v")
        CH = KD // 2
        stage = [ring[:, 0, CH * CB * h:CH * CB * (h + 1)] for h in range(2)]
        high = [ring[:, 1, CH * CB * h:CH * CB * (h + 1)] for h in range(2)]
        chunk = lambda v: v.rearrange("p (k c) -> p k c", k=CH)

        def split_product(acc, rows_hi, rows_lo, w_hi, w_lo, first, last):
            nc.tensor.matmul(acc, rows_hi, w_hi, start=first, stop=False)
            nc.tensor.matmul(acc, rows_hi, w_lo, start=False, stop=False)
            return nc.tensor.matmul(acc, rows_lo, w_hi, start=False, stop=last)

        def tile_cols(flat, k, t):
            c = TOK * k + P * t
            return r32(flat[:, c:c + P])

        def proj_sync(sp, l):
            s, w = PROJ, a["w_in_even" if l == 0 else "w_in_odd"][0].rearrange("(h k p) c -> p h k c", p=P, h=2)

            def load(b, h):
                sp.dma_start(chunk(stage[h]), w[:, h, :, bass.ds(b * CB, CB)]).then_inc(s[f"w{h}"], 16)
            if l == 0:
                sp.wait_ge(AD["mv"], 8)
            else:
                sp.wait_ge(g["phase"], PH["combine0"])
            load(0, 0)
            load(0, 1)
            if l == 0:
                sp.wait_ge(g["zero_rows"], 1)
                sp.dma_start(slot_rows.rearrange("(n p) d -> p n d", p=P),
                             ring[:, 2, 0:D].unsqueeze(1).to_broadcast([P, MAX_ITEMS, D])).then_inc(g["zeroed"], 16)
            with sp.Fori(1, 6) as j:
                for h in range(2):
                    sp.wait_ge(s["used"], 2 * j + h - 1 + 12 * l)
                    load(j, h)

        def proj_pe(pe, l):
            s = PROJ
            with pe.Fori(0, 6) as j:
                for h in range(2):
                    pe.wait_ge(s["lo"], 2 * j + h + 1 + 12 * l)
                    hi, lo = r32(chunk(high[h])), r32(chunk(stage[h]))
                    for k in range(CH):
                        kk = CH * h + k
                        for t in range(TILES):
                            if kk == 0:
                                if t % 2 == 0:
                                    pe.wait_ge(s["ev_a"], 3 * j + t // 2 + 1 + 21 * l)
                                else:
                                    pe.wait_ge(s["ev_v"], 2 * j + t // 2 + 1 + 14 * l)
                            last = split_product(bank[t][:, :], tile_cols(hT_flat, kk, t), tile_cols(hT2_flat, kk, t),
                                                 hi[:, k, :], lo[:, k, :], kk == 0, kk == KD - 1)
                            if kk == KD - 1:
                                last.then_inc(s["mm"], 1)
                    nc.tensor.drain().then_inc(s["used"], 1)
            if l == 1:
                for k in range(KD):
                    w_hi, w_lo = (r32(wf[:, i, N_FOX * k:N_FOX * k + P]) for i in range(2))
                    for acc, c0, c1 in ((bank[5], 0, SEQ), (bank[6], SEQ, TOK)):
                        r_hi, r_lo = r32(hT[:, k, c0:c1]), r32(hT2[:, k, c0:c1])
                        n = c1 - c0
                        split_product(acc[:, 0:n], w_hi, w_lo, r_hi, r_lo, k == 0, k == KD - 1)
            phase_end("pe", pe)

        def proj_act(act, l):
            s = PROJ
            act.sem_inc(s["ev_a"], 3)

            def split(j, h):
                act.wait_ge(s[f"w{h}"], 16 * j + 16 + 96 * l)
                if not isinstance(j, int):
                    act.wait_ge(s["used"], 2 * j + h - 1 + 12 * l)
                act.activation(r32(high[h]), stage[h], ACT.Copy).then_inc(s["hi"], 1)

            def results(j, scale=1.0):
                for t in (0, 2, 4):
                    act.wait_ge(s["mm"], 5 * j + t + 1 + 30 * l)
                    act.activation(qkv[0:rows(t), t, bass.ds(j * CB, CB)], bank[t][0:rows(t), :], ACT.Copy,
                                   scale=scale).then_inc(s["ev_a"], 1)

            split(0, 0)
            split(0, 1)
            for j0, j1, scale in ((0, 5, 1.0),) if l == 0 else ((0, 2, HD ** -0.5), (2, 5, 1.0)):
                with act.Fori(j0, j1) as j:
                    split(j + 1, 0)
                    results(j, scale)
                    split(j + 1, 1)
            results(5)
            phase_end("act", act)

        def proj_dve(dve, l):
            s = PROJ
            dve.sem_inc(s["ev_v"], 2)

            def split(j, h):
                dve.wait_ge(s["hi"], 2 * j + h + 1 + 12 * l)
                dve.tensor_tensor(r32(stage[h]), stage[h], f32(high[h]), ALU.subtract).then_inc(s["lo"], 1)

            def results(j, scale=1.0):
                for t in (1, 3):
                    dve.wait_ge(s["mm"], 5 * j + t + 1 + 30 * l)
                    dst = qkv[0:rows(t), t, bass.ds(j * CB, CB)]
                    if scale == 1.0:
                        dve.tensor_copy(dst, bank[t][0:rows(t), :]).then_inc(s["ev_v"], 1)
                    else:
                        dve.tensor_scalar(dst, bank[t][0:rows(t), :], scale, None, ALU.mult).then_inc(s["ev_v"], 1)

            split(0, 0)
            split(0, 1)
            for j0, j1, scale in ((0, 5, 1.0),) if l == 0 else ((0, 2, HD ** -0.5), (2, 5, 1.0)):
                with dve.Fori(j0, j1) as j:
                    split(j + 1, 0)
                    results(j, scale)
                    split(j + 1, 1)
            results(5)
            phase_end("dve", dve)

        ROPE = sems("rope", "self", "lam")

        def rope_dve(dve):
            dve.wait_ge(g["load_rope"], 48)
            lk = Link(dve, ROPE["self"])
            t1, t2, t3, t4 = (work[:, 512 * i:512 * i + 512] for i in range(4))
            for t0, nt, r in ((0, NT, P), (NT, 1, DEC)):
                n = nt * 64
                for blk in range(2):
                    v = qkv[0:r, t0:t0 + nt, CB * blk:CB * blk + CB].rearrange("p t (h d) -> p t h d", d=HD)
                    x1, x2 = v[:, :, :, 0:8], v[:, :, :, 8:16]
                    cos = rope[0:r, t0:t0 + nt, 0, :].unsqueeze(2).to_broadcast([r, nt, 8, 8])
                    sin = rope[0:r, t0:t0 + nt, 1, :].unsqueeze(2).to_broadcast([r, nt, 8, 8])

                    def tmp(b):
                        return b[0:r, 0:n].rearrange("p (t h d) -> p t h d", t=nt, d=8)
                    lk.step(dve.tensor_tensor(tmp(t1), x1, cos, ALU.mult))
                    lk.step(dve.tensor_tensor(tmp(t2), x2, sin, ALU.mult))
                    lk.step(dve.tensor_tensor(tmp(t3), x2, cos, ALU.mult))
                    lk.do(dve.tensor_tensor(tmp(t4), x1, sin, ALU.mult))
                    lk.step(dve.tensor_tensor(x1, tmp(t1), tmp(t2), ALU.subtract))
                    lk.do(dve.tensor_tensor(x2, tmp(t3), tmp(t4), ALU.add))
            dve.wait_ge(ROPE["lam"], 1)
            dve.tensor_scalar(lam[:, 2:3], lam[:, 1:2], lam[:, 0:1], -LAM_INIT, ALU.subtract, ALU.add)
            phase_end("dve", dve)

        def store_kv(sp, l):
            sp.wait_ge(g["phase"], PH["rope" if l == 0 else "forget"])
            s = out_sems[f"kv{l}"]
            if l == 0:
                parts = [("diff_k", 1 * CB, CB), ("diff_v", 2 * CB, CB), ("sb_k", 4 * CB, CB), ("sb_v", 5 * CB, CB)]
            else:
                parts = [("fox_k", D, D), ("fox_v", 2 * D, D)]
            for n, c0, w in parts:
                sp.dma_start(out[n + "_p"].rearrange("a b (t p) h d -> p (a b t) (h d)", p=P),
                             qkv[:, 0:NT, c0:c0 + w]).then_inc(s, 16)
                sp.dma_start(out[n + "_s"].rearrange("a b p h d -> (a b p) (h d)"),
                             qkv[0:DEC, NT, c0:c0 + w]).then_inc(s, 16)
            if l == 1:
                sp.dma_start(out["fox_logf_p"].rearrange("a b (t p) h -> p (a b t) h", p=P), logf[:, 0:NT, :]).then_inc(s, 16)
                sp.dma_start(out["fox_logf_s"].rearrange("a b p h -> (a b p) h"), logf[0:DEC, 6, :]).then_inc(s, 16)

        KP, KS, QS, QKT = 512, 1024, 1312, 1344
        DF = sems("df", "past_k", "past_v", "staged", "staged_v", "tr", "tr_ev", "s", "mx", "e", "w", "pt", "pt_ev",
                  "o", "on", "ot", "normed", "self_v", "self_a", "v_free")
        df_q = work[:, 0:640].rearrange("p (t d) -> p t d", d=P)
        df_k = work[:, 640:1536].rearrange("p (t d) -> p t d", d=P)
        df_pv = work[:, 4096:4480].rearrange("p (t d) -> p t d", d=P)
        df_p = work[:, 1792:3840].rearrange("p (u c k) -> p u c k", u=2, c=2)
        df_o = qkv[:, :, 0:CB].rearrange("p t (h d) -> p t h d", d=P)
        df_qm = w1[:, 0:2 * TOK].rearrange("p (c n) -> p c n", c=2)
        df_kT = w1[:, 2 * TOK:2 * TOK + 800]
        df_pt = w1[:, 2 * TOK + 800:2 * TOK + 1824].rearrange("p (u k) -> p u k", u=2)

        df_sq = work[:, 3840:3968]

        def transpose_rows(out_bank, tiles, np_):
            c = 0
            for src, r in tiles:
                last = nc.tensor.transpose(out_bank[0:np_, c:c + r], src, ident[0:r, 0:r])
                c += r
            return last

        def nkeys(i):
            return P * (i + 1) if i < NT else PAST + DEC

        def key_tiles(i):
            return [(j, P, P * j) for j in range(i + 1)] if i < NT else [(4, P, 0), (5, P, P), (6, DEC, 2 * P)]

        def diff_sync(sp):
            sp.wait_ge(g["phase"], PH["rope"])
            ck = a["cache_diff_k"][0, 0].rearrange("(t p) h d -> p t (h d)", p=P)
            cv = a["cache_diff_v"][0, 0].rearrange("(t p) h d -> p t (h d)", p=P)
            def head(h, more):
                sp.wait_ge(DF["tr"], 3 * h + 1)
                sp.dma_start(df_k[:, 4:6, :], ck[:, :, bass.ds(h * P, P)]).then_inc(DF["past_k"], 16)
                sp.wait_ge(DF["v_free"], h + 1)
                sp.dma_start(df_pv[:, 0:2, :], cv[:, :, bass.ds(h * P, P)]).then_inc(DF["past_v"], 16)
                c = 2 * h + 4
                ada_load(sp, 0, c, c)
                if more:
                    ada_store_before(sp, 0, c, c)
                ada_bias(sp, 0, c, c)
                ada_load(sp, 0, c + 1, c + 1)
                ada_store_before(sp, 0, c + 1, c + 1)
                ada_bias(sp, 0, c + 1, c + 1)

            head(0, False)
            with sp.Fori(1, N_DIFF) as h:
                head(h, True)
            ada_store_before(sp, 0, 12, 12)

        def diff_pool(pool):
            pool.wait_ge(g["zeroed"], 16)
            pool.memset(df_qm, 0.0)
            pool.drain()
            with pool.Fori(0, N_DIFF) as h:
                pool.wait_ge(DF["tr"], 3 * h + 1)
                for dst, c0, t_new in ((df_q, 0, 4), (df_k, CB, 6)):
                    pool.tensor_copy(dst[:, 0:NT, :], qkv[:, 0:NT, bass.ds(h * P + c0, P)]).then_inc(DF["staged"], 1)
                    pool.tensor_copy(dst[0:DEC, t_new, :], qkv[0:DEC, NT, bass.ds(h * P + c0, P)]).then_inc(DF["staged"], 1)
                pool.wait_ge(DF["v_free"], h + 1)
                pool.tensor_copy(df_pv[0:DEC, 2, :], qkv[0:DEC, NT, bass.ds(h * P + 2 * CB, P)]).then_inc(DF["staged_v"], 1)
            phase_end("pool", pool)

        def diff_pe(pe):
            pe.sem_inc(DF["tr"], 1)
            pe.sem_inc(DF["v_free"], 1)
            with pe.Fori(0, N_DIFF) as h:
                pe.wait_ge(DF["staged"], 4 * h + 4)
                transpose_rows(bank[7], [(df_q[:, t, :], P) for t in range(NT)], P).then_inc(DF["tr"], 1)
                transpose_rows(bank[4], [(df_k[:, t, :], P) for t in range(NT)], P).then_inc(DF["tr"], 1)
                pe.wait_ge(DF["past_k"], 16 * h + 16)
                pe.wait_ge(DF["tr_ev"], 3 * h + 1)
                transpose_rows(bank[7], [(df_k[:, 4, :], P), (df_k[:, 5, :], P), (df_k[0:DEC, 6, :], DEC),
                                         (df_q[0:DEC, 4, :], DEC)], P).then_inc(DF["tr"], 1)
                pe.wait_ge(DF["tr_ev"], 3 * h + 3)

                def scores(i):
                    if i >= 2:
                        pe.wait_ge(DF["e"], 10 * h + 2 * (i - 2) + 2)
                    if i == NT:
                        settle(pe)
                    r = rows(i)
                    q0, k0 = P * i, 0 if i < NT else SEQ
                    for c in range(2):
                        b = bank[2 * (i % 2) + c]
                        last = nc.tensor.matmul(b[0:r, 0:nkeys(i)], df_qm[:, c, q0:q0 + r],
                                                df_kT[:, k0:k0 + nkeys(i)], start=True, stop=i == NT)
                        if i < NT:
                            last = nc.tensor.matmul(b[:, P * i:P * i + P], ident_b[:, :], chunk_b[:, :],
                                                    start=False, stop=True)
                        last.then_inc(DF["s"], 1)

                def turn(i):
                    pe.wait_ge(DF["w"], 5 * h + i + 1)
                    if i >= 2:
                        pe.wait_ge(DF["pt_ev"], 5 * h + i - 1)
                    if i == NT:
                        settle(pe)
                    r = rows(i)
                    for n, (j, kr, c) in enumerate(key_tiles(i)):
                        last = nc.tensor.transpose(bank[4 + 2 * (i % 2)][0:kr, r * n:r * n + r], df_p[0:r, i % 2, 0, c:c + kr],
                                                   ident[0:r, 0:r])
                    last.then_inc(DF["pt"], 1)

                def values(i):
                    pe.wait_ge(DF["pt_ev"], 5 * h + i + 1)
                    if i >= 1:
                        pe.wait_ge(DF["on"], 5 * h + i)
                    if i == NT:
                        pe.wait_ge(DF["past_v"], 16 * h + 16)
                        pe.wait_ge(DF["staged_v"], h + 1)
                        settle(pe)
                    r = rows(i)
                    tiles = key_tiles(i)
                    for n, (j, kr, c) in enumerate(tiles):
                        if j < NT:
                            v = qkv[:, j, bass.ds(h * P + 2 * CB, P)]
                        else:
                            v = df_pv[0:kr, j - 4, :]
                        last = nc.tensor.matmul(bank[5][0:r, 0:P], df_pt[0:kr, i % 2, r * n:r * n + r], v,
                                                start=n == 0, stop=n == len(tiles) - 1)
                    last.then_inc(DF["o"], 1)

                scores(0)
                scores(1)
                for i in range(TILES):
                    turn(i)
                    if i + 2 < TILES:
                        scores(i + 2)
                    if i >= 1:
                        values(i - 1)
                    if i == 0:
                        ada_matvec(pe, 2 * h + 4, bank[7])
                    elif i == 1:
                        ada_sum(pe, 2 * h + 4, bank[7])
                    elif i == 2:
                        pe.wait_ge(AD["row"], 2 * h + 5)
                        ada_matvec(pe, 2 * h + 5, bank[7])
                    elif i == 3:
                        ada_sum(pe, 2 * h + 5, bank[7])
                pe.wait_ge(AD["row"], 2 * h + 6)
                values(TILES - 1)
                nc.tensor.drain().then_inc(DF["v_free"], 1)
            for t in range(TILES):
                r = rows(t)
                pe.wait_ge(DF["normed"], t + 1)
                for hh in range(N_DIFF):
                    last = nc.tensor.transpose(bank[t][:, P * hh:P * hh + r], df_o[0:r, t, hh, :], ident[0:r, 0:r])
                last.then_inc(DF["ot"], 1)
            phase_end("pe", pe)

        def diff_act(act):
            act.preload_act_table_set("natural_log_exp_and_others")
            with act.Fori(0, N_DIFF) as h:
                act.wait_ge(DF["tr"], 3 * h + 2)
                act.activation(df_qm[0:HD, 0, 0:SEQ], bank[7][0:HD, :], ACT.Copy)
                act.activation(df_qm[HD:P, 1, 0:SEQ], bank[7][HD:P, :], ACT.Copy).then_inc(DF["tr_ev"], 1)
                act.wait_ge(DF["tr"], 3 * h + 3)
                act.activation(df_kT[:, 0:SEQ], bank[4][:, :], ACT.Copy).then_inc(DF["tr_ev"], 1)
                act.wait_ge(DF["tr"], 3 * h + 4)
                act.activation(df_kT[:, SEQ:800], bank[7][:, 0:288], ACT.Copy)
                act.activation(df_qm[0:HD, 0, SEQ:TOK], bank[7][0:HD, 288:320], ACT.Copy)
                act.activation(df_qm[HD:P, 1, SEQ:TOK], bank[7][HD:P, 288:320], ACT.Copy).then_inc(DF["tr_ev"], 1)

                def probs(i):
                    r = rows(i)
                    if i >= 2:
                        act.wait_ge(DF["pt"], 5 * h + i - 1)
                    act.wait_ge(DF["mx"], 5 * h + i + 1)
                    for c in range(2):
                        act.activation(df_p[0:r, i % 2, c, 0:nkeys(i)], bank[2 * (i % 2) + c][0:r, 0:nkeys(i)], ACT.Exp,
                                       scale=HD ** -0.5, bias=small[0:r, 8 * (i % 2) + c:8 * (i % 2) + c + 1],
                                       accum_out=small[0:r, 8 * (i % 2) + 2 + c:8 * (i % 2) + 3 + c]).then_inc(DF["e"], 1)

                def turned(i):
                    r, n, b = rows(i), len(key_tiles(i)), bank[4 + 2 * (i % 2)]
                    act.wait_ge(DF["pt"], 5 * h + i + 1)
                    if i >= 2:
                        act.wait_ge(DF["o"], 5 * h + i - 1)
                    if i < NT:
                        act.activation(df_pt[:, i % 2, 0:r * n], b[:, 0:r * n], ACT.Copy).then_inc(DF["pt_ev"], 1)
                    else:
                        act.activation(df_pt[:, i % 2, 0:2 * r], b[:, 0:2 * r], ACT.Copy)
                        act.activation(df_pt[0:DEC, i % 2, 2 * r:3 * r], b[0:DEC, 2 * r:3 * r],
                                       ACT.Copy).then_inc(DF["pt_ev"], 1)

                def result(i):
                    r = rows(i)
                    act.wait_ge(DF["o"], 5 * h + i + 1)
                    o = df_o[0:r, i, bass.ds(h, 1), :].rearrange("p a d -> p (a d)")
                    act.activation(o, bank[5][0:r, 0:P], ACT.Copy)
                    act.activation(df_sq[0:r, :], bank[5][0:r, 0:P], ACT.Square,
                                   accum_out=df_ss[0:r, i, bass.ds(h, 1)]).then_inc(DF["on"], 1)

                probs(0)
                probs(1)
                for i in range(TILES):
                    turned(i)
                    if i + 2 < TILES:
                        probs(i + 2)
                    if i >= 1:
                        result(i - 1)
                    if i in (0, 2):
                        ada_copy(act, 2 * h + 4 + i // 2, bank[7])
                result(TILES - 1)
            z = df_ss[:, :, :]
            act.drain()
            act.activation(z, z, ACT.Ln, scale=1.0 / P, bias=eps[:, :]).then_inc(DF["self_a"], 1)
            act.wait_ge(DF["self_a"], 1)
            act.activation(z, z, ACT.Exp, scale=-0.5).then_inc(DF["self_a"], 1)
            for t in range(TILES):
                act.wait_ge(DF["ot"], t + 1)
                act.activation(hT[:, 0:N_DIFF, cols(t)], bank[t][:, :].rearrange("p (h c) -> p h c", c=P)[:, :, 0:rows(t)],
                               ACT.Copy, scale=subg[:, :])
            phase_end("act", act)

        def diff_dve(dve):
            with dve.Fori(0, N_DIFF) as h:
                lk = Link(dve, DF["self_v"], base=15 * h)

                def maxima(i):
                    r, o = rows(i), 8 * (i % 2)
                    for c in range(2):
                        dve.wait_ge(DF["s"], 10 * h + 2 * i + c + 1)
                        ins = dve.reduce_max(small[0:r, o + 4 + c:o + 5 + c], bank[2 * (i % 2) + c][0:r, 0:nkeys(i)], X)
                    lk.do(ins)
                    dve.tensor_scalar(small[0:r, o:o + 2], small[0:r, o + 4:o + 6], -HD ** -0.5, None,
                                      ALU.mult).then_inc(DF["mx"], 1)

                def weights(i):
                    r, o, n = rows(i), 8 * (i % 2), nkeys(i)
                    dve.wait_ge(DF["e"], 10 * h + 2 * i + 2)
                    lk.do(dve.reciprocal(small[0:r, o + 6:o + 8], small[0:r, o + 2:o + 4]))
                    dve.tensor_scalar(small[0:r, o + 7:o + 8], small[0:r, o + 7:o + 8], lam[0:r, 2:3], None, ALU.mult)
                    lk.do(dve.tensor_scalar(df_p[0:r, i % 2, 0, 0:n], df_p[0:r, i % 2, 0, 0:n],
                                            small[0:r, o + 6:o + 7], None, ALU.mult))
                    dve.scalar_tensor_tensor(out=df_p[0:r, i % 2, 0, 0:n], in0=df_p[0:r, i % 2, 1, 0:n],
                                             scalar=small[0:r, o + 7:o + 8], in1=df_p[0:r, i % 2, 0, 0:n],
                                             op0=ALU.mult, op1=ALU.add).then_inc(DF["w"], 1)

                maxima(0)
                maxima(1)
                for i in range(TILES):
                    weights(i)
                    if i + 2 < TILES:
                        maxima(i + 2)
                    if i in (2, 4):
                        ada_add(dve, 2 * h + 4 + (i - 2) // 2, bank[7])
            dve.wait_ge(DF["self_a"], 2)
            for t in range(TILES):
                r = rows(t)
                dve.tensor_tensor(df_o[0:r, t, :, :], df_o[0:r, t, :, :], df_ss[0:r, t, :].unsqueeze(2).to_broadcast([r, N_DIFF, P]),
                                  ALU.mult).then_inc(DF["normed"], 1)
            phase_end("dve", dve)

        SB = sems("sb", "past_k", "past_v", "staged", "tr", "ev_a", "ev_v", "z", "self_a", "e", "sp", "tri", "r", "w",
                  "pv", "v_free")
        sb_q = work[:, 0:640].rearrange("p (t d) -> p t d", d=P)
        sb_k = work[:, 640:1536].rearrange("p (t d) -> p t d", d=P)
        sb_v = work[:, 1536:2432].rearrange("p (t d) -> p t d", d=P)
        sb_r = work[:, 2432:3520].rearrange("p (h c) -> p h c", h=2)
        sb_w = work[:, 3520:4608].rearrange("p (u c) -> p u c", u=2)
        sb_qm = w1[:, 0:2 * TOK].rearrange("p (h n) -> p h n", h=2)
        sb_kT = w1[:, 1088:1984]
        sb_e = w1[:, 1984:3008].rearrange("p (u c) -> p u c", u=2)
        sb_s = w1[:, 3008:4032].rearrange("p (u c) -> p u c", u=2)
        SB_UNITS = [(j, hd) for j in (3, 2, 1, 0) for hd in (0, 1)]
        SB_SAMPLE = {3: 6, 2: 5, 1: 4}

        def sb_cols(j):
            return (SEQ - P * j) + (DEC if j >= 1 else 0)

        def sb_sync(sp):
            sp.wait_ge(g["phase"], PH["diff"])
            ck = a["cache_sb_k"][0, 0].rearrange("(t p) h d -> p t (h d)", p=P)
            cv = a["cache_sb_v"][0, 0].rearrange("(t p) h d -> p t (h d)", p=P)
            def pair(i, more):
                sp.wait_ge(SB["tr"], 3 * i + 1)
                sp.dma_start(sb_k[:, 4:6, :], ck[:, :, bass.ds(i * P, P)]).then_inc(SB["past_k"], 16)
                sp.wait_ge(SB["v_free"], i + 1)
                sp.dma_start(sb_v[:, 4:6, :], cv[:, :, bass.ds(i * P, P)]).then_inc(SB["past_v"], 16)
                ada_load(sp, 1, i + 12, i)
                if more:
                    ada_store_before(sp, 1, i + 12, i)
                ada_bias(sp, 1, i + 12, i)

            pair(0, False)
            sp.wait_ge(AD["stored"], 16 * 12)
            with sp.Fori(1, N_SB // 2) as i:
                pair(i, True)
            ada_store_before(sp, 1, 16, 4)

        def sb_pool(pool):
            pool.memset(sb_k[:, 6, :], 0.0)
            pool.memset(sb_v[:, 6, :], 0.0)
            pool.memset(sb_qm, 0.0)
            pool.drain()
            with pool.Fori(0, N_SB // 2) as i:
                pool.wait_ge(SB["tr"], 3 * i + 1)
                for dst, c0, t_new in ((sb_q, 3 * CB, 4), (sb_k, 4 * CB, 6)):
                    pool.tensor_copy(dst[:, 0:NT, :], qkv[:, 0:NT, bass.ds(i * P + c0, P)]).then_inc(SB["staged"], 1)
                    pool.tensor_copy(dst[0:DEC, t_new, :], qkv[0:DEC, NT, bass.ds(i * P + c0, P)]).then_inc(SB["staged"], 1)
                pool.wait_ge(SB["v_free"], i + 1)
                pool.tensor_copy(sb_v[:, 0:NT, :], qkv[:, 0:NT, bass.ds(i * P + 5 * CB, P)]).then_inc(SB["staged"], 1)
                pool.tensor_copy(sb_v[0:DEC, 6, :], qkv[0:DEC, NT, bass.ds(i * P + 5 * CB, P)]).then_inc(SB["staged"], 1)
                for u, (j, hd) in enumerate(SB_UNITS):
                    if j == 0:
                        continue
                    n = sb_cols(j)
                    pool.wait_ge(SB["sp"], 8 * i + u + 1)
                    settle(pool)
                    pool.tensor_copy(sb_r[:, hd, P * j:P * j + (P if j < 3 else n)],
                                     sb_s[:, u % 2, 0:(P if j < 3 else n)]).then_inc(SB["r"], 1)
                    if j < 3:
                        pool.wait_ge(SB["tri"], 8 * i + u + 1)
                        pool.tensor_tensor(sb_r[:, hd, P * j + P:TOK], sb_r[:, hd, P * j + P:TOK],
                                           sb_s[:, u % 2, P:n], ALU.add).then_inc(SB["r"], 1)
            phase_end("pool", pool)

        SB_R = [1, 2, 4, 6, 8, 10, 10, 10]

        def sb_pe(pe):
            pe.sem_inc(SB["tr"], 1)
            pe.sem_inc(SB["v_free"], 1)
            with pe.Fori(0, N_SB // 2) as i:
                pe.wait_ge(SB["staged"], 6 * i + 4)
                transpose_rows(bank[0], [(sb_q[:, t, :], P) for t in range(NT)], P).then_inc(SB["tr"], 1)
                transpose_rows(bank[1], [(sb_k[:, t, :], P) for t in range(NT)], P).then_inc(SB["tr"], 1)
                pe.wait_ge(SB["past_k"], 16 * i + 16)
                pe.wait_ge(SB["ev_a"], 3 * i + 1)
                transpose_rows(bank[0], [(sb_k[:, 4, :], P), (sb_k[:, 5, :], P), (sb_k[:, 6, :], P),
                                         (sb_q[0:DEC, 4, :], DEC)], P).then_inc(SB["tr"], 1)
                pe.wait_ge(SB["ev_a"], 3 * i + 3)
                pe.wait_ge(SB["ev_v"], i + 1)
                pe.wait_ge(SB["staged"], 6 * i + 6)
                pe.wait_ge(SB["past_v"], 16 * i + 16)

                def logits(u):
                    j, hd = SB_UNITS[u]
                    b, n = bank[2 + u % 4], SEQ - P * j
                    if u >= 4:
                        pe.wait_ge(SB["w"], 8 * i + u - 3)
                    nc.tensor.matmul(b[:, 0:n], sb_kT[:, P * j:P * j + P], sb_qm[:, hd, P * j:SEQ],
                                     start=True, stop=False, skip_group_check=True)
                    if j >= 1:
                        kt = SB_SAMPLE[j]
                        nc.tensor.matmul(b[:, n:n + DEC], sb_kT[:, P * kt:P * kt + P], sb_qm[:, hd, SEQ:TOK],
                                         start=False, stop=False, skip_group_check=True)
                    if j == 3:
                        nc.tensor.matmul(b[:, n:n + DEC], ident_b[:, :], strict_b[:, 0:DEC],
                                         start=False, stop=False, skip_group_check=True)
                    nc.tensor.matmul(b[:, 0:P], ident_b[:, :], strict_b[:, :],
                                     start=False, stop=True, skip_group_check=True).then_inc(SB["z"], 1)

                def later(u):
                    j, hd = SB_UNITS[u]
                    b, n = bank[2 + u % 4], sb_cols(j)
                    pe.wait_ge(SB["sp"], 8 * i + u + 1)
                    last = nc.tensor.matmul(b[:, 0:n], neg_from[:, :], sb_s[:, u % 2, 0:n], start=False, stop=True,
                                            skip_group_check=True)
                    if j < 3:
                        pe.wait_ge(SB["r"], 10 * i + SB_R[u - 2])
                        last = nc.tensor.matmul(b[:, P:n], neg_ones[:, :], sb_r[:, hd, P * j + P:P * j + n],
                                                start=False, stop=True, skip_group_check=True)
                    last.then_inc(SB["tri"], 1)

                def values(u):
                    j, hd = SB_UNITS[u]
                    half, n = slice(HD * hd, HD * hd + HD), SEQ - P * j
                    pe.wait_ge(SB["w"], 8 * i + u + 1)
                    last = nc.tensor.matmul(bank[7][half, P * j:SEQ], sb_v[:, j, half], sb_w[:, u % 2, 0:n],
                                            start=j == 3, stop=j == 0, skip_group_check=True)
                    if j >= 1:
                        last = nc.tensor.matmul(bank[6][half, 0:DEC], sb_v[:, SB_SAMPLE[j], half],
                                                sb_w[:, u % 2, n:n + DEC], start=j == 3, stop=j == 1)
                    last.then_inc(SB["pv"], 1)

                logits(0)
                logits(1)
                for u in range(8):
                    if u + 2 < 8:
                        logits(u + 2)
                    later(u)
                    if u >= 1:
                        values(u - 1)
                    if u == 2:
                        ada_matvec(pe, i + 12, bank[0])
                    elif u == 4:
                        ada_sum(pe, i + 12, bank[0])
                pe.wait_ge(AD["row"], i + 13)
                values(7)
                nc.tensor.drain().then_inc(SB["v_free"], 1)
            phase_end("pe", pe)

        def sb_act(act):
            act.preload_act_table_set("natural_log_exp_and_others")
            with act.Fori(0, N_SB // 2) as i:
                act.wait_ge(SB["tr"], 3 * i + 2)
                act.activation(sb_qm[0:HD, 0, 0:SEQ], bank[0][0:HD, :], ACT.Copy, scale=HD ** -0.5)
                act.activation(sb_qm[HD:P, 1, 0:SEQ], bank[0][HD:P, :], ACT.Copy, scale=HD ** -0.5).then_inc(SB["ev_a"], 1)
                act.wait_ge(SB["tr"], 3 * i + 4)
                act.activation(sb_kT[:, 4 * P:7 * P], bank[0][:, 0:3 * P], ACT.Copy).then_inc(SB["ev_a"], 1)
                act.activation(sb_qm[0:HD, 0, SEQ:TOK], bank[0][0:HD, 3 * P:3 * P + DEC], ACT.Copy, scale=HD ** -0.5)
                act.activation(sb_qm[HD:P, 1, SEQ:TOK], bank[0][HD:P, 3 * P:3 * P + DEC], ACT.Copy,
                               scale=HD ** -0.5).then_inc(SB["ev_a"], 1)

                def log_part(u):
                    j, _ = SB_UNITS[u]
                    n, e = sb_cols(j), sb_e[:, u % 2, 0:sb_cols(j)]
                    act.wait_ge(SB["z"], 8 * i + u + 1)
                    if u >= 2:
                        act.wait_ge(SB["sp"], 8 * i + u - 1)
                    lk = Link(act, SB["self_a"], base=16 * i + 2 * u)
                    lk.do(act.activation(e, bank[2 + u % 4][:, 0:n], ACT.Abs))
                    lk.do(act.activation(e, e, ACT.Exp, scale=-1.0))
                    act.activation(e, e, ACT.Ln, bias=1.0).then_inc(SB["e"], 1)

                def weight(u):
                    n = sb_cols(SB_UNITS[u][0])
                    act.wait_ge(SB["tri"], 8 * i + u + 1)
                    if u >= 2:
                        act.wait_ge(SB["pv"], 8 * i + u - 1)
                    act.activation(sb_w[:, u % 2, 0:n], bank[2 + u % 4][:, 0:n], ACT.Exp).then_inc(SB["w"], 1)

                log_part(0)
                log_part(1)
                for u in range(8):
                    weight(u)
                    if u + 2 < 8:
                        log_part(u + 2)
                    if u == 2:
                        ada_copy(act, i + 12, bank[0])
            phase_end("act", act)

        def sb_dve(dve):
            with dve.Fori(0, N_SB // 2) as i:
                dve.wait_ge(SB["tr"], 3 * i + 3)
                dve.tensor_copy(sb_kT[:, 0:SEQ], bank[1][:, :]).then_inc(SB["ev_v"], 1)
                for u, (j, hd) in enumerate(SB_UNITS):
                    n = sb_cols(j)
                    dve.wait_ge(SB["e"], 8 * i + u + 1)
                    if u >= 2:
                        dve.wait_ge(SB["tri"], 8 * i + u - 1)
                        dve.wait_ge(SB["r"], 10 * i + SB_R[u - 2])
                    dve.scalar_tensor_tensor(out=sb_s[:, u % 2, 0:n], in0=bank[2 + u % 4][:, 0:n], scalar=0.0,
                                             in1=sb_e[:, u % 2, 0:n], op0=ALU.max, op1=ALU.add).then_inc(SB["sp"], 1)
                    if u == 5:
                        ada_add(dve, i + 12, bank[0])
                for hd in range(2):
                    half = slice(HD * hd, HD * hd + HD)
                    dve.wait_ge(SB["pv"], 8 * i + 7 + hd)
                    dve.tensor_copy(hT[half, bass.ds(i + 4, 1), 0:SEQ].rearrange("p a c -> p (a c)"), bank[7][half, :])
                    dve.tensor_copy(hT[half, bass.ds(i + 4, 1), SEQ:TOK].rearrange("p a c -> p (a c)"),
                                    bank[6][half, 0:DEC])
            phase_end("dve", dve)

        FG = sems("fg", "rows", "fl", "self", "biased", "l1", "logf", "cum")

        fl_rows = ring[0:N_FOX, 2, 0:TOK]

        def forget_dve(dve):
            lk = Link(dve, FG["self"])
            y = work[:, 0:TILES * N_FOX].rearrange("p (t h) -> p t h", h=N_FOX)
            dve.wait_ge(FG["fl"], 1)
            for t in range(TILES):
                r = rows(t)
                dve.tensor_tensor(y[0:r, t, :], bank[7][0:r, N_FOX * t:N_FOX * t + N_FOX], bfb[0:r, :],
                                  ALU.add).then_inc(FG["biased"], 1)
            dve.wait_ge(FG["l1"], 2)
            e = work[:, 128:128 + TILES * N_FOX].rearrange("p (t h) -> p t h", h=N_FOX)
            dve.scalar_tensor_tensor(out=logf[:, 0:NT, :], in0=y[:, 0:NT, :], scalar=0.0, in1=e[:, 0:NT, :],
                                     op0=ALU.min, op1=ALU.subtract).then_inc(FG["logf"], 1)
            dve.scalar_tensor_tensor(out=logf[0:DEC, 6, :], in0=y[0:DEC, NT, :], scalar=0.0, in1=e[0:DEC, NT, :],
                                     op0=ALU.min, op1=ALU.subtract).then_inc(FG["logf"], 1)
            dve.wait_ge(FG["cum"], 1)
            b6 = bank[6][:, 0:7 * N_FOX].rearrange("p (t h) -> p t h", h=N_FOX)
            for t0, t1, r in ((0, 6, P), (6, 7, DEC)):
                dve.tensor_copy(dcum[0:r, t0:t1, :], b6[0:r, t0:t1, :])
                dve.tensor_scalar(ndcum[0:r, t0:t1, :], b6[0:r, t0:t1, :], -1.0, None, ALU.mult)
            phase_end("dve", dve)

        def forget_act(act):
            act.preload_act_table_set("natural_log_exp_and_others")
            act.activation(fl_rows[:, 0:SEQ], bank[5][0:N_FOX, :], ACT.Copy)
            act.activation(fl_rows[:, SEQ:TOK], bank[6][0:N_FOX, 0:DEC], ACT.Copy).then_inc(FG["rows"], 1)
            act.wait_ge(FG["biased"], TILES)
            for n, (c0, c1, r) in enumerate(((0, NT * N_FOX, P), (NT * N_FOX, TILES * N_FOX, DEC))):
                e = work[0:r, 128 + c0:128 + c1]
                lk = Link(act, FG["self"], base=2 * n)
                lk.do(act.activation(e, work[0:r, c0:c1], ACT.Abs))
                lk.do(act.activation(e, e, ACT.Exp, scale=-1.0))
                act.activation(e, e, ACT.Ln, bias=1.0).then_inc(FG["l1"], 1)
            phase_end("act", act)

        def forget_pe(pe):
            pe.wait_ge(FG["rows"], 1)
            for t in range(TILES):
                last = nc.tensor.transpose(bank[7][0:rows(t), N_FOX * t:N_FOX * t + N_FOX], fl_rows[:, cols(t)],
                                           ident[0:N_FOX, 0:N_FOX])
            last.then_inc(FG["fl"], 1)
            pe.wait_ge(FG["logf"], 2)
            pe.wait_ge(g["load_rope"], 48)
            for tiles in ([(0, P), (1, P), (2, P), (3, P)], [(4, P), (5, P), (6, DEC)]):
                for n, (t, r) in enumerate(tiles):
                    dst = bank[6][0:r, N_FOX * t:N_FOX * t + N_FOX]
                    last = nc.tensor.matmul(dst, upto[0:r, 0:r], logf[0:r, t, :], start=True, stop=n == 0)
                    for m, (e, _) in enumerate(tiles[:n]):
                        last = nc.tensor.matmul(dst, ones[:, 0:r], logf[:, e, :], start=False, stop=m == n - 1)
            last.then_inc(FG["cum"], 1)
            phase_end("pe", pe)

        FX = sems("fx", "past_k0", "past_k1", "past_v0", "past_v1", "staged", "staged_v", "tr", "ev_a", "ev_v", "s", "m", "e", "p", "pt", "pt_ev", "pv",
                  "v_free", "self_v")
        KQ = HD + 2
        fx_q = work[:, 0:660].rearrange("p (t h d) -> p t h d", h=2, d=KQ)
        fx_k = work[:, 660:1584].rearrange("p (t h d) -> p t h d", h=2, d=KQ)
        fx_v = work[:, 1584:2480].rearrange("p (t h d) -> p t h d", h=2, d=HD)
        fx_p = work[:, 2480:4016].rearrange("p (u k) -> p u k", u=3)
        fx_qk = w1[:, 0:2 * QKT].rearrange("p (h c) -> p h c", h=2)
        fx_pt = w1[:, 2 * QKT:2 * QKT + 1024].rearrange("p (u k) -> p u k", u=2)
        FX_UNITS = [(i, hd) for hd in (0, 1) for i in range(TILES)]

        def fox_sync(sp):
            sp.wait_ge(g["phase"], PH["forget"])
            ck = a["cache_fox_k"][0, 0].rearrange("(t p) h d -> p t h d", p=P)
            cv = a["cache_fox_v"][0, 0].rearrange("(t p) h d -> p t h d", p=P)
            def pair(i, more):
                for hd in range(2):
                    sp.wait_ge(FX["tr"], 6 * i + 3 * hd + 1)
                    sp.dma_start(fx_k[:, 4:6, hd, 0:HD], ck[:, :, bass.ds(2 * i + hd, 1), :].rearrange("p t a d -> p t (a d)")
                                 ).then_inc(FX[f"past_k{hd}"], 16)
                    sp.wait_ge(FX["v_free"], 2 * i + hd + 1)
                    sp.dma_start(fx_v[:, 4:6, hd, :], cv[:, :, bass.ds(2 * i + hd, 1), :].rearrange("p t a d -> p t (a d)")
                                 ).then_inc(FX[f"past_v{hd}"], 16)
                ada_load(sp, 1, i + 16, i + 4)
                if more:
                    ada_store_before(sp, 1, i + 16, i + 4)
                ada_bias(sp, 1, i + 16, i + 4)

            pair(0, False)
            with sp.Fori(1, N_FOX // 2) as i:
                pair(i, True)
            ada_store_before(sp, 1, 24, 12)

        def fox_pool(pool):
            pool.memset(fx_qk[:, :, :], 0.0)
            pool.memset(fx_q[:, :, :, HD:HD + 1], 1.0)
            pool.memset(fx_k[:, :, :, HD + 1:HD + 2], 1.0)
            pool.drain()
            with pool.Fori(0, N_FOX // 2) as i:
                for hd in range(2):
                    pool.wait_ge(FX["tr"], 6 * i + 3 * hd + 1)
                    for t0, nt, r, tk in ((0, NT, P, 0), (NT, 1, DEC, 6)):
                        def head(c0):
                            return qkv[0:r, t0:t0 + nt, bass.ds(i * P + HD * hd + c0, HD)]
                        pool.tensor_copy(fx_q[0:r, t0:t0 + nt, hd, 0:HD], head(0)).then_inc(FX["staged"], 1)
                        pool.tensor_copy(fx_q[0:r, t0:t0 + nt, hd, HD + 1:HD + 2], dcum[0:r, tk:tk + nt, bass.ds(2 * i + hd, 1)]
                                         ).then_inc(FX["staged"], 1)
                        pool.tensor_copy(fx_k[0:r, tk:tk + nt, hd, 0:HD], head(D)).then_inc(FX["staged"], 1)
                    pool.tensor_copy(fx_k[:, 0:6, hd, HD:HD + 1], ndcum[:, 0:6, bass.ds(2 * i + hd, 1)]).then_inc(FX["staged"], 1)
                    pool.tensor_copy(fx_k[0:DEC, 6:7, hd, HD:HD + 1], ndcum[0:DEC, 6:7, bass.ds(2 * i + hd, 1)]).then_inc(FX["staged"], 1)
                    pool.wait_ge(FX["v_free"], 2 * i + hd + 1)
                    pool.tensor_copy(fx_v[:, 0:NT, hd, :], qkv[:, 0:NT, bass.ds(i * P + HD * hd + 2 * D, HD)]).then_inc(FX["staged_v"], 1)
                    pool.tensor_copy(fx_v[0:DEC, 6:7, hd, :], qkv[0:DEC, NT:NT + 1, bass.ds(i * P + HD * hd + 2 * D, HD)]
                                     ).then_inc(FX["staged_v"], 1)
            phase_end("pool", pool)

        def fox_pe(pe):
            pe.sem_inc(FX["tr"], 4)
            pe.sem_inc(FX["v_free"], 2)

            def rows_turned(i, hd, part):
                if part == 0:
                    pe.wait_ge(FX["staged"], 16 * i + 8 * hd + 8)
                    transpose_rows(bank[0], [(fx_q[:, t, hd, :], P) for t in range(NT)], KQ).then_inc(FX["tr"], 1)
                    transpose_rows(bank[1], [(fx_k[:, t, hd, :], P) for t in range(NT)], KQ).then_inc(FX["tr"], 1)
                else:
                    pe.wait_ge(FX[f"past_k{hd}"], 16 * i + 16)
                    pe.wait_ge(FX["ev_a" if hd == 0 else "ev_v"], 3 * i + 1)
                    transpose_rows(bank[0], [(fx_k[:, 4, hd, :], P), (fx_k[:, 5, hd, :], P), (fx_k[0:DEC, 6, hd, :], DEC),
                                             (fx_q[0:DEC, 4, hd, :], DEC)], KQ).then_inc(FX["tr"], 1)

            def pair(i, more):
                def scores(u):
                    t, hd = FX_UNITS[u]
                    b, r, n = bank[2 + u % 3], rows(t), nkeys(t)
                    if t == 0:
                        pe.wait_ge(FX["ev_a" if hd == 0 else "ev_v"], 3 * i + 3)
                    if u >= 3:
                        pe.wait_ge(FX["e"], 10 * i + u - 2)
                    q0, k0 = (P * t, KP) if t < NT else (QS, KS)
                    nc.tensor.matmul(b[0:r, 0:n], fx_qk[:, hd, q0:q0 + r], fx_qk[:, hd, k0:k0 + n],
                                     start=True, stop=False)
                    nc.tensor.matmul(b[0:r, n - r:n], ident_b[0:r, 0:r], causal_b[0:r, 0:r],
                                     start=False, stop=True).then_inc(FX["s"], 1)

                def turn(u):
                    t, hd = FX_UNITS[u]
                    r = rows(t)
                    pe.wait_ge(FX["p"], 10 * i + u + 1)
                    if u >= 2:
                        pe.wait_ge(FX["pt_ev"], 10 * i + u - 1)
                    if t == NT:
                        settle(pe)
                    for n, (j, kr, c) in enumerate(key_tiles(t)):
                        last = nc.tensor.transpose(bank[5 + u % 2][0:kr, r * n:r * n + r], fx_p[0:r, u % 3, c:c + kr],
                                                   ident[0:r, 0:r])
                    last.then_inc(FX["pt"], 1)

                def values(u):
                    t, hd = FX_UNITS[u]
                    r, half = rows(t), slice(HD * hd, HD * hd + HD)
                    pe.wait_ge(FX["pt_ev"], 10 * i + u + 1)
                    if t == 0:
                        pe.wait_ge(FX["staged_v"], 4 * i + 2 * hd + 2)
                    if t == NT:
                        pe.wait_ge(FX[f"past_v{hd}"], 16 * i + 16)
                    dst = bank[7][half, P * t:P * t + P] if t < NT else bank[5 + u % 2][half, P:P + DEC]
                    tiles = key_tiles(t)
                    for n, (j, kr, c) in enumerate(tiles):
                        last = nc.tensor.matmul(dst, fx_v[0:kr, j, hd, :], fx_pt[0:kr, u % 2, r * n:r * n + r],
                                                start=n == 0, stop=n == len(tiles) - 1)
                    last.then_inc(FX["pv"], 1)

                scores(0)
                scores(1)
                for u in range(10):
                    if u + 2 < 10:
                        scores(u + 2)
                    turn(u)
                    if u >= 1:
                        values(u - 1)
                    if u == 5:
                        nc.tensor.drain().then_inc(FX["v_free"], 1)
                    if u < 2:
                        rows_turned(i, 1, u)
                    if u in (2, 3):
                        if u == 2:
                            pe.wait_ge(FX["ev_v"], 3 * i + 3)
                        ada_matvec(pe, i + 16, bank[0], (u - 2,))
                    elif u == 4:
                        ada_sum(pe, i + 16, bank[0])
                    elif u == 6:
                        pe.wait_ge(AD["row"], i + 17)
                    if u in (6, 7) and more:
                        rows_turned(i + 1, 0, u - 6)
                values(9)
                nc.tensor.drain().then_inc(FX["v_free"], 1)

            rows_turned(0, 0, 0)
            rows_turned(0, 0, 1)
            with pe.Fori(0, N_FOX // 2 - 1) as i:
                pair(i, True)
            pair(N_FOX // 2 - 1, False)
            phase_end("pe", pe)

        def fox_act(act):
            act.preload_act_table_set("natural_log_exp_and_others")

            def rows_out(i, *parts):
                for n in parts:
                    b, c0, w = ((0, 0, 512), (1, KP, 512), (0, KS, 320))[n]
                    act.wait_ge(FX["tr"], 6 * i + n + 5)
                    act.activation(fx_qk[0:KQ, 0, c0:c0 + w], bank[b][0:KQ, 0:w], ACT.Copy).then_inc(FX["ev_a"], 1)

            def pair(i, more):

                def probs(u):
                    t, hd = FX_UNITS[u]
                    r, n = rows(t), nkeys(t)
                    act.wait_ge(FX["m"], 10 * i + u + 1)
                    if u >= 3:
                        act.wait_ge(FX["pt"], 10 * i + u - 2)
                    act.activation(fx_p[0:r, u % 3, 0:n], bank[2 + u % 3][0:r, 0:n], ACT.Exp, scale=1.0,
                                   bias=small[0:r, u:u + 1], accum_out=small[0:r, 16 + u:17 + u]).then_inc(FX["e"], 1)

                def turned(u):
                    t, hd = FX_UNITS[u]
                    r, n = rows(t), len(key_tiles(t))
                    act.wait_ge(FX["pt"], 10 * i + u + 1)
                    if u >= 2:
                        act.wait_ge(FX["pv"], 10 * i + u - 1)
                    b = bank[5 + u % 2]
                    if t < NT:
                        act.activation(fx_pt[:, u % 2, 0:r * n], b[:, 0:r * n], ACT.Copy).then_inc(FX["pt_ev"], 1)
                    else:
                        act.activation(fx_pt[:, u % 2, 0:2 * r], b[:, 0:2 * r], ACT.Copy)
                        act.activation(fx_pt[0:DEC, u % 2, 2 * r:3 * r], b[0:DEC, 2 * r:3 * r],
                                       ACT.Copy).then_inc(FX["pt_ev"], 1)

                probs(0)
                probs(1)
                for u in range(10):
                    turned(u)
                    if u + 2 < 10:
                        probs(u + 2)
                    if u == 3:
                        ada_copy(act, i + 16, bank[0])
                    if more and u == 6:
                        rows_out(i + 1, 0, 1)
                    if more and u == 7:
                        rows_out(i + 1, 2)

            rows_out(0, 0, 1, 2)
            with act.Fori(0, N_FOX // 2 - 1) as i:
                pair(i, True)
            pair(N_FOX // 2 - 1, False)
            phase_end("act", act)

        def fox_dve(dve):
            with dve.Fori(0, N_FOX // 2) as i:
                def rows_out(*parts):
                    for n in parts:
                        b, c0, w = ((0, 0, 512), (1, KP, 512), (0, KS, 320))[n]
                        dve.wait_ge(FX["tr"], 6 * i + n + 8)
                        dve.tensor_copy(fx_qk[0:KQ, 1, c0:c0 + w], bank[b][0:KQ, 0:w]).then_inc(FX["ev_v"], 1)

                def out_of(hd):
                    half = slice(HD * hd, HD * hd + HD)
                    dve.wait_ge(FX["pv"], 10 * i + 5 * hd + 5)
                    dve.tensor_copy(hT[half, bass.ds(i, 1), 0:SEQ].rearrange("p a c -> p (a c)"), bank[7][half, :])
                    dve.tensor_copy(hT[half, bass.ds(i, 1), SEQ:TOK].rearrange("p a c -> p (a c)"),
                                    bank[5 + hd][half, P:P + DEC])

                def maxima(u):
                    t, hd = FX_UNITS[u]
                    r, n = rows(t), nkeys(t)
                    dve.wait_ge(FX["s"], 10 * i + u + 1)
                    dve.reduce_max(small[0:r, u:u + 1], bank[2 + u % 3][0:r, 0:n], X, negate=True).then_inc(FX["m"], 1)

                def normed(u):
                    t, hd = FX_UNITS[u]
                    r, n = rows(t), nkeys(t)
                    dve.wait_ge(FX["e"], 10 * i + u + 1)
                    lk = Link(dve, FX["self_v"], base=10 * i + u)
                    lk.do(dve.reciprocal(small[0:r, 16 + u:17 + u], small[0:r, 16 + u:17 + u]))
                    dve.tensor_scalar(fx_p[0:r, u % 3, 0:n], fx_p[0:r, u % 3, 0:n], small[0:r, 16 + u:17 + u], None,
                                      ALU.mult).then_inc(FX["p"], 1)

                maxima(0)
                maxima(1)
                for u in range(10):
                    normed(u)
                    if u + 2 < 10:
                        maxima(u + 2)
                    if u == 0:
                        rows_out(0, 1)
                    elif u == 1:
                        rows_out(2)
                    elif u == 4:
                        ada_add(dve, i + 16, bank[0])
                    elif u == 5:
                        out_of(0)
                out_of(1)
            phase_end("dve", dve)

        OUT = sems("outp", "w0", "w1", "hi", "lo", "mm", "ev", "add")
        o_tmp = arena[:, 0:1024].rearrange("p (u c) -> p u c", u=2)
        out_hi = [ring[:, 2, :], arena[:, 1024:1024 + KD * CB]]
        OUT_PIECES = []
        for n in range(2):
            for q in range(4):
                c0, c1 = 2 * TOK * q + (P - DEC if q else 0), min(2 * TOK * (q + 1) + P - DEC, KD * TOK)
                if n == 0:
                    OUT_PIECES.append((0, hT2_flat[:, c0:c1], hT_flat[:, c0:c1]))
                OUT_PIECES.append((n, out_hi[n][:, 2 * CB * q:2 * CB * (q + 1)], ring[:, 1 - n, 2 * CB * q:2 * CB * (q + 1)]))

        def out_load_block(sp, l, n):
            sp.wait_ge(*((PROJ["used"], 12 * l + 12) if n == 0 else (AD["sum"], (16, 24)[l])))
            sp.dma_start(ring[:, 1 - n, :].rearrange("p (k c) -> p k c", k=KD),
                         a["w_out_even" if l == 0 else "w_out_odd"][0][:, CB * n:CB * n + CB].rearrange("(k p) c -> p k c", p=P)
                         ).then_inc(OUT[f"w{n}"], 16)

        def out_pe(pe, l):
            s = OUT
            for n in range(2):
                hi, lo = (r32(v.rearrange("p (k c) -> p k c", k=KD)) for v in (out_hi[n], ring[:, 1 - n, :]))
                for k in range(KD):
                    if k % 2 == 0:
                        pe.wait_ge(s["lo"], len(OUT_PIECES) * l + (k + 2 if n == 0 else 8 + k // 2 + 1))
                    for t in range(TILES):
                        u = TILES * n + t
                        if k == 0 and u >= 8:
                            pe.wait_ge(s["ev"], 10 * l + u - 7)
                        last = split_product(bank[u % 8][:, :], tile_cols(hT2_flat, k, t), tile_cols(hT_flat, k, t),
                                             hi[:, k, :], lo[:, k, :], k == 0, k == KD - 1)
                        if k == KD - 1:
                            last.then_inc(s["mm"], 1)
            phase_end("pe", pe)

        def out_act(act, l):
            act.activation(r32(hT2_flat[:, KD * TOK:HT_LEN]), ones[:, 0:P - DEC], ACT.Copy)
            for n, hi, whole in OUT_PIECES:
                act.wait_ge(OUT[f"w{n}"], 16 * l + 16)
                if n == 1:
                    act.wait_ge(out_sems[f"kv{l}"], 16 * (8 if l == 0 else 6))
                act.activation(r32(hi), whole, ACT.Copy).then_inc(OUT["hi"], 1)
            phase_end("act", act)

        def out_dve(dve, l):
            s = OUT
            for i, (n, hi, whole) in enumerate(OUT_PIECES):
                dve.wait_ge(s["hi"], len(OUT_PIECES) * l + i + 1)
                dve.tensor_tensor(r32(whole), whole, f32(hi), ALU.subtract).then_inc(s["lo"], 1)
            dve.wait_ge(out_sems[f"kv{l}"], 16 * (8 if l == 0 else 6))
            dve.wait_ge(AD["out"], 32 * (l + 1))
            for u in range(2 * TILES):
                n, t = u // TILES, u % TILES
                r = rows(t)
                dve.wait_ge(s["mm"], 10 * l + u + 1)
                if u >= 2:
                    dve.wait_ge(s["add"], 10 * l + u - 1)
                dve.tensor_tensor(o_tmp[0:r, u % 2, :], bank[u % 8][0:r, :], bc[0:r, G1, group(t), CB * n:CB * n + CB],
                                  ALU.mult).then_inc(s["ev"], 1)
            phase_end("dve", dve)

        def out_pool(pool, l):
            s = OUT
            for u in range(2 * TILES):
                n, t = u // TILES, u % TILES
                r = rows(t)
                pool.wait_ge(s["ev"], 10 * l + u + 1)
                pool.tensor_tensor(x[0:r, t, CB * n:CB * n + CB], x[0:r, t, CB * n:CB * n + CB],
                                   o_tmp[0:r, u % 2, :], ALU.add).then_inc(s["add"], 1)
            phase_end("pool", pool)

        rt_self = [0]
        rt = arena[:, 5120:9216]
        e_rows = rt[0:NE, 3200:3200 + TOK]

        def rv(i, n=TILES * NE):
            return rt[:, 96 * i:96 * i + n]

        def route_pe(pe, l):
            s = RT
            pe.wait_ge(s["e"], l + 1)
            for t in range(TILES):
                last = nc.tensor.transpose(bank[0][0:rows(t), NE * t:NE * t + NE], e_rows[:, cols(t)], ident[0:NE, 0:NE])
            last.then_inc(s["turned"], 1)
            pe.wait_ge(s["mask"], l + 1)
            nc.tensor.matmul(bank[1][:, 0:TILES * NE], before_b[:, :], mask_b[:, :], start=True, stop=False, skip_group_check=True)
            for e in range(TILES):
                m = mask_b[:, NE * e:NE * e + NE].unsqueeze(1).to_broadcast([P, TILES - e, NE])
                last = nc.tensor.matmul(bank[1][:, NE * (e + 1):NE * (TILES + 1)].rearrange("p (t e) -> p t e", e=NE),
                                        ones_b[:, :], m, start=False, stop=e == TILES - 1, skip_group_check=True)
            last.then_inc(s["pos"], 1)
            phase_end("pe", pe)

        def route_act(act, l):
            s = RT
            act.preload_act_table_set("natural_log_exp_and_others")
            act.wait_ge(s["logits"], l + 1)
            act.activation(e_rows[:, 0:SEQ], bank[6][0:NE, :], ACT.Exp, scale=-1.0)
            act.activation(e_rows[:, SEQ:TOK], bank[7][0:NE, 0:DEC], ACT.Exp, scale=-1.0).then_inc(s["e"], 1)
            phase_end("act", act)

        def route_pool(pool, l):
            s = RT
            pool.iota(rt[:, 2400:2416], pattern=[[-1, NE]], base=NE, channel_multiplier=0, allow_small_or_imprecise_dtypes=True)
            pool.iota(rt[:, 2416:2420], pattern=[[-1, NG]], base=NG, channel_multiplier=0, allow_small_or_imprecise_dtypes=True)
            pool.iota(rt[:, 2432:2432 + MAX_ITEMS], pattern=[[1, MAX_ITEMS]], base=0, channel_multiplier=0,
                      allow_small_or_imprecise_dtypes=True)
            pool.iota(rt[:, 2960:3040], pattern=[[0, NE], [P, TILES]], base=0, channel_multiplier=0,
                      allow_small_or_imprecise_dtypes=True)
            pool.memset(mask_b[:, :], 0.0)
            pool.drain()
            pool.memset(rt[:, 2960:2961], -1.0)
            pool.memset(rv(1), 1.0).then_inc(s["cnt"], 1)
            pool.wait_ge(s["done"], l + 1)
            for t in range(TILES):
                r = rows(t)
                for c in range(2):
                    pool.indirect_dma_start(slot_rows, bass.IndirectOffsetOnAxis(ids[0:r, c, t:t + 1], 0),
                                            h_rows[0:r, t, :], None).then_inc(s["scat"], 16)
            pool.wait_ge(s["scat"], 16 * 2 * TILES * (l + 1))
            phase_end("pool", pool)

        def route_dve(dve, l):
            s = RT
            lk = Link(dve, s["self"], base=rt_self[0])
            T3 = lambda v, e: v.rearrange("p (t e) -> p t e", e=e)
            sig, sel, pair, selm, tmp, oh1, oh2, dst = rv(1), rv(2), rv(3, 120), rv(5), rv(6), rv(7), rv(8), rv(13)
            gs, gk, gsel = rt[:, 2080:2100], rt[:, 2100:2120], rt[:, 2120:2140]
            m1 = rt[:, 2140:2145]
            rank, grank, item = rt[:, 2400:2416], rt[:, 2416:2420], rt[:, 2432:2432 + MAX_ITEMS]

            def bt(v, n):
                return v.unsqueeze(1).to_broadcast([P, TILES, n])

            def be(v, n):
                return v.unsqueeze(2).to_broadcast([P, TILES, n])

            dve.wait_ge(s["cnt"], l + 1)
            dve.wait_ge(s["turned"], l + 1)
            lk.step(dve.tensor_scalar(sig[:, 0:NT * NE], bank[0][:, 0:NT * NE], 1.0, None, ALU.add))
            lk.do(dve.tensor_scalar(sig[0:DEC, NT * NE:TILES * NE], bank[0][0:DEC, NT * NE:TILES * NE], 1.0, None, ALU.add))
            lk.do(dve.reciprocal(sig, sig))
            lk.do(dve.tensor_tensor(T3(sel, NE), T3(sig, NE), bt(br[:, :], NE), ALU.add))
            s4 = sel.rearrange("p (n e) -> p n e", e=EPG)
            p6 = pair.rearrange("p (n e) -> p n e", e=6)
            lk.step(dve.tensor_tensor(p6[:, :, 0:3], s4[:, :, 0:3], s4[:, :, 1:4], ALU.add))
            lk.step(dve.tensor_tensor(p6[:, :, 3:5], s4[:, :, 0:2], s4[:, :, 2:4], ALU.add))
            lk.do(dve.tensor_tensor(p6[:, :, 5:6], s4[:, :, 0:1], s4[:, :, 3:4], ALU.add))
            lk.do(dve.tensor_reduce(gs, p6, X, ALU.max))

            def first_max(v, n, rank_row, best, onehot):
                v3, o3 = T3(v, n), T3(onehot, n)
                lk.do(dve.tensor_reduce(best, v3, X, ALU.max))
                lk.do(dve.tensor_tensor(o3, v3, be(best, n), ALU.is_ge))
                lk.do(dve.tensor_tensor(o3, o3, bt(rank_row, n), ALU.mult))
                lk.do(dve.tensor_reduce(best, o3, X, ALU.max))
                lk.do(dve.tensor_tensor(o3, o3, be(best, n), ALU.is_equal))

            first_max(gs, NG, grank, m1, gsel)
            lk.do(dve.tensor_scalar(gk, gsel, 1.0, -NEG, ALU.subtract, ALU.mult))
            lk.do(dve.tensor_tensor(selm.rearrange("p (n e) -> p n e", e=EPG), s4,
                                    gk.unsqueeze(2).to_broadcast([P, TILES * NG, EPG]), ALU.add))
            first_max(selm, NE, rank, m1, oh1)
            lk.do(dve.scalar_tensor_tensor(out=selm, in0=oh1, scalar=2.0 * NEG, in1=selm, op0=ALU.mult, op1=ALU.add))
            first_max(selm, NE, rank, m1, oh2)
            lk.step(dve.tensor_tensor(mask_b[:, 0:NT * NE], oh1[:, 0:NT * NE], oh2[:, 0:NT * NE], ALU.add))
            lk.do(dve.tensor_tensor(mask_b[0:DEC, NT * NE:TILES * NE], oh1[0:DEC, NT * NE:TILES * NE],
                                    oh2[0:DEC, NT * NE:TILES * NE], ALU.add))
            dve.drain().then_inc(s["mask"], 1)
            for c, oh in enumerate((oh1, oh2)):
                lk.do(dve.tensor_tensor(tmp, sig, oh, ALU.mult))
                lk.do(dve.tensor_reduce(gates[:, c, :], T3(tmp, NE), X, ALU.add))
            lk.do(dve.tensor_tensor(m1, gates[:, 0, :], gates[:, 1, :], ALU.add))
            lk.do(dve.reciprocal(m1, m1))
            lk.do(dve.tensor_tensor(gates[:, :, :], gates[:, :, :], m1.unsqueeze(1).to_broadcast([P, 2, TILES]), ALU.mult))
            dve.wait_ge(s["pos"], l + 1)
            cnt, nt_, end, st = rt[:, 2144:2160], rt[:, 2160:2176], rt[:, 2176:2192], rt[:, 2192:2208]
            lk.do(dve.tensor_copy(cnt, bank[1][:, TILES * NE:(TILES + 1) * NE]))
            above = rt[:, 3040:3120].rearrange("p (e j) -> p e j", j=TILES)
            lk.do(dve.tensor_tensor(above, cnt.unsqueeze(2).to_broadcast([P, NE, TILES]),
                                    rt[:, 2960:3040].rearrange("p (e j) -> p e j", j=TILES), ALU.is_gt))
            lk.do(dve.tensor_reduce(nt_, above, X, ALU.add))
            lk.do(dve.tensor_tensor_scan(end, ones[:, 0:NE], nt_, 0.0, ALU.mult, ALU.add))
            lk.do(dve.tensor_tensor(st, end, nt_, ALU.subtract))
            lk.do(dve.tensor_scalar(st, st, float(P), None, ALU.mult))
            lk.do(dve.tensor_copy(dst[:, 0:NT * NE], bank[1][:, 0:NT * NE]))
            lk.do(dve.memset(dst[:, NT * NE:TILES * NE], 0.0))
            lk.do(dve.tensor_copy(dst[0:DEC, NT * NE:TILES * NE], bank[1][0:DEC, NT * NE:TILES * NE]))
            lk.do(dve.tensor_tensor(T3(dst, NE), T3(dst, NE), bt(st, NE), ALU.add))
            for c, oh in enumerate((oh1, oh2)):
                lk.do(dve.tensor_tensor(tmp, dst, oh, ALU.mult))
                lk.do(dve.tensor_reduce(m1, T3(tmp, NE), X, ALU.add))
                lk.do(dve.tensor_copy(ids[:, c, :], m1))
            dve.drain().then_inc(s["done"], 1)
            grid = rt[0:1, 2560:2560 + MAX_ITEMS * NE].rearrange("p (n e) -> p n e", e=NE)
            lk.do(dve.tensor_tensor(grid, item[0:1, :].unsqueeze(2).to_broadcast([1, MAX_ITEMS, NE]),
                                    end[0:1, :].unsqueeze(1).to_broadcast([1, MAX_ITEMS, NE]), ALU.is_ge))
            ie = rt[0:1, 2304:2304 + MAX_ITEMS]
            lk.do(dve.tensor_reduce(ie, grid, X, ALU.add))
            lk.do(dve.tensor_scalar(ie, ie, float(NE - 1), None, ALU.min))
            lk.do(dve.tensor_copy(item_expert[:, :], ie))
            lk.step(dve.tensor_copy(n_items[:, 0:1], total[:, :]))
            lk.step(dve.tensor_scalar(n_items[:, 1:2], end[0:1, NE - 1:NE], total[:, :], 1.0, ALU.add, ALU.subtract))
            lk.step(dve.tensor_tensor(n_items[:, 2:3], end[0:1, NE - 1:NE], total[:, :], ALU.add))
            lk.do(dve.tensor_scalar(n_items[:, 3:4], end[0:1, NE - 1:NE], total[:, :], 2.0, ALU.add, ALU.subtract))
            lk.do(dve.tensor_tensor(total[:, :], total[:, :], end[0:1, NE - 1:NE], ALU.add))
            rt_self[0] += lk.n
            phase_end("dve", dve)

        MO = sems("mo", "wg0", "wg1", "wu0", "wu1", "wd0", "wd1", "hi_g", "hi_u", "hi_d", "lo_g", "lo_u", "lo_d",
                  "lop_g", "lop_u", "lop_d", "x", "tx", "xh", "xl", "g", "sg", "u", "a", "at", "ah", "al", "d", "ev", "y",
                  "stored")
        m_x = arena[:, 0:1024]
        m_xh = arena[:, 1024:2048].rearrange("p (k c) -> p k c", k=KD)
        m_xl = arena[:, 2048:3072].rearrange("p (k c) -> p k c", k=KD)
        m_sg = arena[:, 3072:3584]
        m_a = arena[:, 3584:4096]
        m_ah = arena[:, 4096:4608].rearrange("p (k c) -> p k c", k=KE)
        m_al = arena[:, 4608:5120].rearrange("p (k c) -> p k c", k=KE)
        m_y = arena[:, 8192:9216]
        SLAB = KD * CB
        m_low = {"g": ring[:, 0, :], "u": ring[:, 1, :], "d": ring[:, 2, :]}
        m_high = {"g": hT_flat[:, 0:SLAB], "u": work[:, 0:SLAB], "d": arena[:, 10240:10240 + SLAB]}

        def piece(v, q):
            return v[:, SLAB // 4 * q:SLAB // 4 * (q + 1)]

        def item_no(eng, which):
            i = {"first": 0, "last": 1, "end": 2, "last-1": 3}[which]
            return eng.value_load(n_items[0:1, i:i + 1], min_val=(0, 8, 9, 7)[i], max_val=2 * MAX_ITEMS)

        def first_item(eng, l):
            return 0 if l == 0 else item_no(eng, "first")

        def moe_sync(sp, l):
            s = MO
            slabs = {"g": (a["w_gate"][l], KD), "u": (a["w_up"][l], KD), "d": (a["w_down"][l], KE)}

            def load(c, e):
                w, k = slabs[c]
                w = w[bass.ds(e, 1), :, :].rearrange("a (p k) c -> p (a k) c", k=k)
                for h in range(2):
                    sp.dma_start(m_low[c][:, SLAB // 2 * h:SLAB // 2 * (h + 1)].rearrange("p (k c) -> p k c", k=k // 2),
                                 w[:, k // 2 * h:k // 2 * (h + 1), :]).then_inc(s[f"w{c}{h}"], 16)

            sp.wait_ge(g["phase"], PH[f"out{l}"])
            for c in "gud":
                load(c, 0)
            sp.wait_ge(g["phase"], PH[f"route{l}"])
            if l == 0:
                sp.sem_inc(s["y"], 16)
            first, last, last_1, end = first_item(sp, l), item_no(sp, "last"), item_no(sp, "last-1"), item_no(sp, "end")

            def slot(n):
                i = nc.s_assert_within(n - first, 0, MAX_ITEMS - 1, skip_runtime_bounds_check_because="n is an item of this layer")
                return slot_rows[bass.ds(i * P, P), :]

            def expert(n):
                i = nc.s_assert_within(n - first, 0, MAX_ITEMS - 1, skip_runtime_bounds_check_because="n is an item of this layer")
                return sp.value_load(item_expert[0:1, bass.ds(i, 1)], min_val=0, max_val=NE - 1)

            def rows_in(n):
                sp.wait_ge(s["tx"], 2 * n)
                sp.dma_start(m_x, slot(n)).then_inc(s["x"], 16)

            def store_before(n):
                sp.wait_ge(s["ev"], 2 * n)
                sp.dma_start(slot(n - 1), m_y).then_inc(s["y"], 16)

            def turn(n, down, more_rows):
                e = expert(n + 1)
                sp.wait_ge(s["g"], n + 1)
                load("g", e)
                if more_rows:
                    rows_in(n + 2)
                sp.wait_ge(s["u"], n + 1)
                load("u", e)
                if down:
                    e = expert(n)
                    sp.wait_ge(s["d"], n)
                    load("d", e)
                    store_before(n)

            sp.dma_start(m_x, slot_rows[0:P, :]).then_inc(s["x"], 16)
            rows_in(first + 1)
            turn(first, False, True)
            with sp.Fori(first + 1, last_1) as n:
                turn(n, True, True)
            turn(last_1, True, False)
            e = expert(last)
            sp.wait_ge(s["d"], last)
            load("d", e)
            store_before(last)
            store_before(end)
            sp.wait_ge(s["y"], 16 * end + 16)
            sp.sem_inc(s["stored"], 1)

        def moe_pe(pe, l):
            s = MO
            first, last = first_item(pe, l), item_no(pe, "last")

            def turn_rows(n):
                pe.wait_ge(s["x"], 16 * n + 16)
                settle(pe)
                xk = m_x.rearrange("p (j k) -> p k j", k=KD)
                for half in range(2):
                    for k in range(4):
                        last_ = nc.tensor.transpose(bank[half][:, P * k:P * k + P], xk[:, 4 * half + k, :], ident[:, :])
                    last_.then_inc(s["tx"], 1)

            def wait_piece(c, n, q):
                if q == 1:
                    pe.wait_ge(s[f"lop_{c}"], n if c == "d" else n + 1)
                else:
                    pe.wait_ge(s[f"lo_{c}"], 3 * n + (1, 0, 2, 3)[q])

            def gate_or_up(c, n):
                if c == "g":
                    pe.wait_ge(s["xh"], 2 * n + 2)
                    pe.wait_ge(s["xl"], 2 * n + 2)
                    pe.wait_ge(s["sg"], n)
                else:
                    pe.wait_ge(s["a"], n)
                acc = bank[2 if c == "g" else 3][:, :]
                hi, lo = (r32(v[c].rearrange("p (k c) -> p k c", k=KD)) for v in (m_high, m_low))
                for k in range(KD):
                    if k % 2 == 0:
                        wait_piece(c, n, k // 2)
                    last_ = split_product(acc, r32(m_xh[:, k, :]), r32(m_xl[:, k, :]), hi[:, k, :], lo[:, k, :],
                                          k == 0, k == KD - 1)
                last_.then_inc(s[c], 1)

            def turn_act(n):
                pe.wait_ge(s["a"], n + 1)
                settle(pe)
                ak = m_a.rearrange("p (j k) -> p k j", k=KE)
                for k in range(KE):
                    last_ = nc.tensor.transpose(bank[6][:, P * k:P * k + P], ak[:, k, :], ident[:, :])
                last_.then_inc(s["at"], 1)

            def down_before(n):
                pe.wait_ge(s["al"], n)
                hi, lo = (r32(v["d"].rearrange("p (k c) -> p k c", k=KE)) for v in (m_high, m_low))
                for k in range(KE):
                    wait_piece("d", n, k)
                    for h in range(2):
                        c = slice(CB * h, CB * h + CB)
                        last_ = split_product(bank[4 + h][:, :], r32(m_ah[:, k, :]), r32(m_al[:, k, :]), hi[:, k, c],
                                              lo[:, k, c], k == 0, k == KE - 1)
                last_.then_inc(s["d"], 1)

            turn_rows(first)
            gate_or_up("g", first)
            turn_rows(first + 1)
            gate_or_up("u", first)
            turn_act(first)
            with pe.Fori(first + 1, last) as n:
                gate_or_up("g", n)
                turn_rows(n + 1)
                gate_or_up("u", n)
                down_before(n)
                turn_act(n)
            gate_or_up("g", last)
            gate_or_up("u", last)
            down_before(last)
            turn_act(last)
            down_before(last + 1)
            phase_end("pe", pe)

        def moe_act(act, l):
            s = MO
            act.preload_act_table(ACT.Silu)
            first, last = first_item(act, l), item_no(act, "last")
            if l == 0:
                act.sem_inc(s["hi_d"], 4)

            def split(c, n, *pieces):
                for q in pieces:
                    if q in (0, 2):
                        act.wait_ge(s[f"w{c}{q // 2}"], 16 * n if c == "d" else 16 * n + 16)
                    act.activation(r32(piece(m_high[c], q)), piece(m_low[c], q), ACT.Copy).then_inc(s[f"hi_{c}"], 1)

            def rows_high(n):
                for half in range(2):
                    act.wait_ge(s["tx"], 2 * n + half + 1)
                    act.activation(r32(m_xh[:, 4 * half:4 * half + 4, :]),
                                   bank[half][:, :].rearrange("p (k c) -> p k c", k=4), ACT.Copy).then_inc(s["xh"], 1)

            def silu(n):
                act.wait_ge(s["g"], n + 1)
                act.wait_ge(s["a"], n)
                act.activation(m_sg, bank[2][:, :], ACT.Silu).then_inc(s["sg"], 1)

            def act_high_before(n):
                act.wait_ge(s["at"], n)
                act.activation(r32(m_ah), bank[6][:, :].rearrange("p (k c) -> p k c", k=KE), ACT.Copy).then_inc(s["ah"], 1)

            def results_before(n):
                act.wait_ge(s["d"], n)
                act.wait_ge(s["y"], 16 * n)
                for h in range(2):
                    act.activation(m_y[:, CB * h:CB * h + CB], bank[4 + h][:, :], ACT.Copy).then_inc(s["ev"], 1)

            rows_high(first)
            split("g", first, 0, 1, 2, 3)
            split("u", first, 0, 1)

            def turn(n, before):
                if before:
                    act_high_before(n)
                split("u", n, 2, 3)
                silu(n)
                if before:
                    split("d", n, 0, 1, 2, 3)
                split("g", n + 1, 0, 1)
                act.wait_ge(s["u"], n + 1)
                rows_high(n + 1)
                split("g", n + 1, 2, 3)
                if before:
                    results_before(n)
                split("u", n + 1, 0, 1)

            turn(first, False)
            with act.Fori(first + 1, last) as n:
                turn(n, True)
            act_high_before(last)
            split("u", last, 2, 3)
            silu(last)
            split("d", last, 0, 1, 2, 3)
            results_before(last)
            act_high_before(last + 1)
            split("d", last + 1, 0, 1, 2, 3)
            results_before(last + 1)
            phase_end("act", act)

        def moe_dve(dve, l):
            s = MO
            first, last = first_item(dve, l), item_no(dve, "last")
            if l == 0:
                dve.sem_inc(s["lo_d"], 3)

            def split(c, n, *pieces):
                for q in pieces:
                    dve.wait_ge(s[f"hi_{c}"], 4 * n + q + 1)
                    dve.tensor_tensor(r32(piece(m_low[c], q)), piece(m_low[c], q), f32(piece(m_high[c], q)),
                                      ALU.subtract).then_inc(s[f"lo_{c}"], 1)

            def rows_low(n):
                for half in range(2):
                    dve.wait_ge(s["xh"], 2 * n + half + 1)
                    k = slice(4 * half, 4 * half + 4)
                    dve.tensor_tensor(r32(m_xl[:, k, :]), bank[half][:, :].rearrange("p (k c) -> p k c", k=4),
                                      f32(m_xh[:, k, :]), ALU.subtract).then_inc(s["xl"], 1)

            def product(n):
                dve.wait_ge(s["u"], n + 1)
                dve.wait_ge(s["sg"], n + 1)
                dve.wait_ge(s["at"], n)
                dve.tensor_tensor(m_a, bank[3][:, :], m_sg, ALU.mult).then_inc(s["a"], 1)

            def act_low_before(n):
                dve.wait_ge(s["ah"], n)
                dve.tensor_tensor(r32(m_al), bank[6][:, :].rearrange("p (k c) -> p k c", k=KE), f32(m_ah),
                                  ALU.subtract).then_inc(s["al"], 1)

            rows_low(first)
            split("g", first, 0, 2, 3)
            split("u", first, 0)

            def turn(n, before):
                if before:
                    act_low_before(n)
                split("u", n, 2, 3)
                if before:
                    split("d", n, 0, 2, 3)
                split("g", n + 1, 0)
                rows_low(n + 1)
                product(n)
                split("g", n + 1, 2, 3)
                split("u", n + 1, 0)

            turn(first, False)
            with dve.Fori(first + 1, last) as n:
                turn(n, True)
            act_low_before(last)
            split("u", last, 2, 3)
            split("d", last, 0, 2, 3)
            product(last)
            act_low_before(last + 1)
            split("d", last + 1, 0, 2, 3)
            phase_end("dve", dve)

        def moe_pool(pool, l):
            first, last = first_item(pool, l), item_no(pool, "last")

            def split(c, n):
                pool.wait_ge(MO[f"hi_{c}"], 4 * n + 2)
                settle(pool)
                pool.tensor_tensor(r32(piece(m_low[c], 1)), piece(m_low[c], 1), f32(piece(m_high[c], 1)),
                                   ALU.subtract).then_inc(MO[f"lop_{c}"], 1)

            split("g", first)
            split("u", first)
            split("g", first + 1)
            split("u", first + 1)
            with pool.Fori(first + 1, last) as n:
                split("d", n)
                split("g", n + 1)
                split("u", n + 1)
            split("d", last)
            split("d", last + 1)
            phase_end("pool", pool)

        CO = sems("co", "y0", "y1", "gated", "self", "acc", "sum")
        c_y = arena[:, 0:8192].rearrange("p (u c d) -> p u c d", u=4, c=2)
        CO_POOL = (2, 3)

        def combine_pool(pool, l):
            s = CO
            pool.wait_ge(MO["stored"], l + 1)

            def gather(t):
                r = rows(t)
                for c in range(2):
                    pool.indirect_dma_start(c_y[0:r, t % 4, c, :], None, slot_rows,
                                            bass.IndirectOffsetOnAxis(ids[0:r, c, t:t + 1], 0)).then_inc(s[f"y{t % 2}"], 16)
            gather(0)
            gather(1)
            for t in range(TILES):
                r = rows(t)
                if t + 2 < TILES:
                    if t + 2 >= 4:
                        pool.wait_ge(s["acc"], 3 * l + t - 1)
                    pool.wait_ge(s[f"y{t % 2}"], (96, 64)[t % 2] * l + 32 * (t // 2 + 1))
                    gather(t + 2)
            for i, t in enumerate(CO_POOL):
                pool.wait_ge(s["sum"], 2 * l + i + 1)
                pool.tensor_tensor(x[:, t, :], x[:, t, :], c_y[:, t % 4, 0, :], ALU.add)
            phase_end("pool", pool)

        def combine_act(act, l):
            for t in range(TILES):
                r = rows(t)
                act.wait_ge(CO[f"y{t % 2}"], (96, 64)[t % 2] * l + 32 * (t // 2 + 1))
                act.activation(c_y[0:r, t % 4, 0, :], c_y[0:r, t % 4, 0, :], ACT.Copy,
                               scale=gates[0:r, 0, t:t + 1]).then_inc(CO["gated"], 1)
            phase_end("act", act)

        def combine_dve(dve, l):
            s = CO
            lk = Link(dve, s["self"], base=8 * l)
            for t in range(TILES):
                r = rows(t)
                y0, y1 = c_y[0:r, t % 4, 0, :], c_y[0:r, t % 4, 1, :]
                dve.wait_ge(s["gated"], 5 * l + t + 1)
                lk.do(dve.scalar_tensor_tensor(out=y0, in0=y1, scalar=gates[0:r, 1, t:t + 1], in1=y0,
                                               op0=ALU.mult, op1=ALU.add))
                if t in CO_POOL:
                    dve.tensor_tensor(y0, y0, bc[0:r, G2, group(t), :], ALU.mult).then_inc(s["sum"], 1)
                else:
                    lk.do(dve.tensor_tensor(y0, y0, bc[0:r, G2, group(t), :], ALU.mult))
                    dve.tensor_tensor(x[0:r, t, :], x[0:r, t, :], y0, ALU.add).then_inc(s["acc"], 1)
            phase_end("dve", dve)

        FN = sems("fn", "norm")
        nf = arena[:, 10240:11264]

        def final_act(act):
            act.preload_act_table_set("natural_log_exp_and_others")
            row_rstd(act, 4)
            phase_end("act", act)

        def final_dve(dve):
            dve.wait_ge(FN["norm"], 16)
            for t in range(TILES):
                r = rows(t)
                dve.wait_ge(NORM["rstd"], 4 * TILES + t + 1)
                dve.scalar_tensor_tensor(out=h_rows[0:r, t, :], in0=x[0:r, t, :], scalar=rstd[0:r, t:t + 1],
                                         in1=nf[0:r, :], op0=ALU.mult, op1=ALU.mult).then_inc(NORM["scaled"], 1)
            phase_end("dve", dve)

        def final_sync(sp):
            sp.wait_ge(g["phase"], PH["combine1"])
            sp.dma_start(nf, a["norm_final"].partition_broadcast(P)).then_inc(FN["norm"], 16)
            for t in range(TILES):
                sp.wait_ge(NORM["scaled"], 4 * TILES + t + 1)
                dst = out["y_prompt"][0, P * t:P * t + P, :] if t < NT else out["y_sample"][0]
                sp.dma_start(dst, h_rows[0:rows(t), t, :]).then_inc(out_sems["y"], 16)
            sp.wait_ge(out_sems["y"], 16 * TILES)
            sp.wait_ge(out_sems["kv0"], 16 * 8)
            sp.wait_ge(out_sems["kv1"], 16 * 6)

        @block.sync
        def _(sp):
            setup_sync(sp)
            ada_sync(sp)
            for l in range(2):
                if l == 1:
                    sp.wait_ge(g["phase"], PH["moe0"])
                    mix_load(sp, l)
                proj_sync(sp, l)
                out_load_block(sp, l, 0)
                store_kv(sp, l)
                if l == 0:
                    diff_sync(sp)
                    sb_sync(sp)
                else:
                    fox_sync(sp)
                out_load_block(sp, l, 1)
                sp.wait_ge(g["phase"], PH["sb" if l == 0 else "fox"])
                sp.wait_ge(AD["stored"], 16 * (16 if l == 0 else 24))
                out_load(sp, l)
                moe_sync(sp, l)
            final_sync(sp)

        @block.tensor
        def _(pe):
            phase_end("pe", pe)
            ada_pe(pe)
            for l in range(2):
                norm_pe(pe, f"norm_mix{l}")
                proj_pe(pe, l)
                if l == 0:
                    phase_end("pe", pe)
                    diff_pe(pe)
                    sb_pe(pe)
                else:
                    forget_pe(pe)
                    fox_pe(pe)
                out_pe(pe, l)
                norm_pe(pe, f"norm_ffn{l}")
                route_pe(pe, l)
                moe_pe(pe, l)
                phase_end("pe", pe)
            phase_end("pe", pe)

        @block.scalar
        def _(act):
            setup_act(act)
            ada_act(act)
            for l in range(2):
                norm_act(act, f"norm_mix{l}")
                proj_act(act, l)
                if l == 0:
                    act.activation(lam[:, 0:2], lam[:, 0:2], ACT.Exp).then_inc(ROPE["lam"], 1)
                    phase_end("act", act)
                    diff_act(act)
                    sb_act(act)
                else:
                    forget_act(act)
                    fox_act(act)
                out_act(act, l)
                norm_act(act, f"norm_ffn{l}")
                route_act(act, l)
                moe_act(act, l)
                combine_act(act, l)
            final_act(act)

        @block.vector
        def _(dve):
            setup_dve(dve)
            ada_dve(dve)
            for l in range(2):
                norm_dve(dve, f"norm_mix{l}")
                proj_dve(dve, l)
                if l == 0:
                    rope_dve(dve)
                    diff_dve(dve)
                    sb_dve(dve)
                else:
                    forget_dve(dve)
                    fox_dve(dve)
                out_dve(dve, l)
                norm_dve(dve, f"norm_ffn{l}")
                route_dve(dve, l)
                moe_dve(dve, l)
                combine_dve(dve, l)
            final_dve(dve)

        @block.gpsimd
        def _(pool):
            setup_pool(pool)
            phase_end("pool", pool)
            for l in range(2):
                norm_pool(pool, f"norm_mix{l}")
                phase_end("pool", pool)
                if l == 0:
                    phase_end("pool", pool)
                    diff_pool(pool)
                    sb_pool(pool)
                else:
                    phase_end("pool", pool)
                    fox_pool(pool)
                out_pool(pool, l)
                norm_pool(pool, f"norm_ffn{l}")
                route_pool(pool, l)
                moe_pool(pool, l)
                combine_pool(pool, l)
            phase_end("pool", pool)


_INS = ["x_prompt", "x_sample", "c_prompt", "c_sample", "cache_diff_k", "cache_diff_v", "cache_sb_k", "cache_sb_v",
        "cache_fox_k", "cache_fox_v", "cache_fox_logf", "w_ada", "b_ada", "norm_mix", "norm_ffn", "w_in_even",
        "w_out_even", "diff_lq1", "diff_lk1", "diff_lq2", "diff_lk2", "diff_subln", "w_in_odd", "b_forget",
        "w_out_odd", "w_router", "b_router", "w_gate", "w_up", "w_down", "norm_final"]


def _outs():
    o = [("y_prompt", (1, SEQ, D)), ("y_sample", (1, DEC, D))]
    for tag, n in (("_p", SEQ), ("_s", DEC)):
        o += [("diff_k" + tag, (1, 1, n, N_DIFF, 2 * HD)), ("diff_v" + tag, (1, 1, n, N_DIFF, 2 * HD)),
              ("sb_k" + tag, (1, 1, n, N_SB, HD)), ("sb_v" + tag, (1, 1, n, N_SB, HD)),
              ("fox_k" + tag, (1, 1, n, N_FOX, HD)), ("fox_v" + tag, (1, 1, n, N_FOX, HD)),
              ("fox_logf" + tag, (1, 1, n, N_FOX))]
    return o


def _rope_table():
    pos = np.concatenate([np.arange(SEQ), PAST + np.arange(DEC)]).astype(np.float32)
    half = HD // 4 // 2
    inv = np.float32(500000.0) ** (-np.arange(half, dtype=np.float32) / np.float32(half))
    ang = pos[:, None] * inv[None, :].astype(np.float32)
    return np.concatenate([np.cos(ang), np.sin(ang)], axis=1).astype(np.float32)


def kernel(**inputs):
    import concourse.bacc as _bacc
    from concourse.bass_utils import run_bass_kernel_spmd as _run

    nc = _bacc.Bacc("TRN2", target_bir_lowering=False, num_devices=1)
    arrays, args = {}, {}
    for name in _INS:
        v = np.ascontiguousarray(inputs[name])
        arrays[f"in_{name}"] = v
        args[name] = nc.dram_tensor(f"in_{name}", v.shape, mybir.dt.from_np(v.dtype), kind="ExternalInput").ap()
    table = _rope_table()
    arrays["rope_table"] = table
    rope_dram = nc.dram_tensor("rope_table", table.shape, F32, kind="ExternalInput").ap()
    outs = {}
    for name, shape in _outs():
        outs[name] = nc.dram_tensor(f"out_{name}", shape, F32, kind="ExternalOutput").ap()
    encoder_step(nc, args, outs, rope_dram)
    r = _run(nc, [arrays], core_ids=[0])
    return tuple(r.results[0][f"out_{name}"] for name, _ in _outs())
```
